# Optimizing a Trainium2 kernel written in Bass

```python
import math
import jax, jax.numpy as jnp
from jax import lax
import numpy as np

D_MODEL = 1024
BATCH = 1
SEQ = 256
DEPTH = 2

CHUNK = 64
MEM_LEN = 256
POOL_GROUPS = 4
POOL_WINDOWS = (2, 4, 8, 16)
POOL_WIDTH = D_MODEL // 2
POOL_GC = POOL_WIDTH // POOL_GROUPS
N_HEADS = 8
HEAD_DIM = 64
ATTN_WIDTH = N_HEADS * HEAD_DIM
IDX_HEADS = 8
IDX_DIM = 64
TOPK_MAX = 256
Q_BLOCK = 128
ATTN_SCALE = HEAD_DIM ** -0.5
IDX_W_SCALE = (IDX_DIM ** -0.5) * (IDX_HEADS ** -0.5)
MEM_HEADS = 4
MEM_HEAD_DIM = 128
MEM_WIDTH = MEM_HEADS * MEM_HEAD_DIM
MEM_SCALE = MEM_HEAD_DIM ** -0.5
N_BRANCH = 3
REL_BUCKETS = 32
REL_MAX_DIST = 1024
EPS = 1e-6
NEG = -1e30
IN_SPLITS = (POOL_WIDTH, POOL_WIDTH,
             ATTN_WIDTH, ATTN_WIDTH, ATTN_WIDTH, ATTN_WIDTH,
             IDX_HEADS * IDX_DIM, IDX_DIM, IDX_HEADS,
             MEM_WIDTH, MEM_WIDTH,
             N_BRANCH * D_MODEL)
IN_COLS = sum(IN_SPLITS)


def rms_norm(x, g):
    x32 = x.astype(jnp.float32)
    y = x32 * lax.rsqrt(jnp.mean(x32 * x32, axis=-1, keepdims=True) + EPS)
    return (y * g.astype(jnp.float32)).astype(x.dtype)

def rel_bucket(rel):
    half = REL_BUCKETS // 2
    max_exact = half // 2
    ret = jnp.where(rel > 0, half, 0)
    n = jnp.abs(rel)
    nf = jnp.maximum(n, 1).astype(jnp.float32)
    large = max_exact + (jnp.log(nf / max_exact) / math.log(REL_MAX_DIST / max_exact)
                         * (half - max_exact)).astype(jnp.int32)
    large = jnp.minimum(large, half - 1)
    return ret + jnp.where(n < max_exact, n, large)

def multi_scale_pool(u, pool_w, pool_scale):
    b, s, _ = u.shape
    ug = u.reshape(b, s, POOL_GROUPS, POOL_GC).astype(jnp.float32)
    cs = jnp.cumsum(ug, axis=1)
    cs = jnp.concatenate([jnp.zeros_like(cs[:, :1]), cs], axis=1)
    t = jnp.arange(s, dtype=jnp.int32)[:, None]
    win = jnp.asarray(POOL_WINDOWS, jnp.int32)[None, :]
    start = jnp.maximum(t + 1 - win, 0)
    grp = jnp.arange(POOL_GROUPS, dtype=jnp.int32)[None, :]
    lo = cs[:, start, grp, :]
    count = (t + 1 - start).astype(jnp.float32)[None, :, :, None]
    pooled = (cs[:, 1:] - lo) / count - ug
    mixed = jnp.einsum('bsgc,gcd->bsgd', pooled.astype(u.dtype), pool_w)
    return mixed.reshape(b, s, POOL_WIDTH) * pool_scale

def dsa_attention(q, k, v, iq, ik, iw, rel_bias):
    b, s = q.shape[:2]
    topk = min(TOPK_MAX, s // 4)
    nb = s // Q_BLOCK
    key_pos = jnp.arange(s, dtype=jnp.int32)
    ik32 = ik.astype(jnp.float32)
    gather = jax.vmap(lambda arr, idx: arr[idx])

    def to_blocks(a):
        return jnp.moveaxis(a.reshape((b, nb, Q_BLOCK) + a.shape[2:]), 1, 0)

    def block(args):
        qb, iqb, iwb, qpos = args
        limit = (qpos // CHUNK + 1) * CHUNK
        sc = jnp.einsum('bqhd,bsd->bqhs', iqb.astype(jnp.float32), ik32)
        index_score = jnp.einsum('bqhs,bqh->bqs', jax.nn.relu(sc),
                                 iwb.astype(jnp.float32) * IDX_W_SCALE)
        admissible = key_pos[None, :] < limit[:, None]
        index_score = jnp.where(admissible[None], index_score, NEG)
        _, idx = lax.top_k(index_score, topk)
        k_sel = gather(k, idx)
        v_sel = gather(v, idx)
        logits = jnp.einsum('bqhd,bqkhd->bqhk', qb, k_sel).astype(jnp.float32) * ATTN_SCALE
        bias = rel_bias[rel_bucket(idx - qpos[None, :, None])]
        logits = logits + jnp.moveaxis(bias, -1, 2).astype(jnp.float32)
        valid = idx < limit[None, :, None]
        logits = jnp.where(valid[:, :, None, :], logits, NEG)
        p = jax.nn.softmax(logits, axis=-1).astype(v.dtype)
        return jnp.einsum('bqhk,bqkhd->bqhd', p, v_sel)

    out = lax.map(block, (to_blocks(q), to_blocks(iq), to_blocks(iw),
                          key_pos.reshape(nb, Q_BLOCK)))
    return jnp.moveaxis(out, 0, 1).reshape(b, s, N_HEADS * HEAD_DIM)

def memory_attention(q, mem_k, mem_v):
    b, s = q.shape[:2]
    logits = jnp.einsum('bshd,bmhd->bhsm', q, mem_k).astype(jnp.float32) * MEM_SCALE
    p = jax.nn.softmax(logits, axis=-1).astype(mem_v.dtype)
    return jnp.einsum('bhsm,bmhd->bshd', p, mem_v).reshape(b, s, MEM_WIDTH)

def first_inputs(seed: int = 0) -> dict:
    key = jax.random.key(seed)
    ks = jax.random.split(key, 14)
    f32 = jnp.float32
    nrm = lambda k, shape, scale: jax.random.normal(k, shape, f32) * scale
    return {
        "x": nrm(ks[0], (BATCH, SEQ, D_MODEL), 1.0),
        "mem": nrm(ks[1], (BATCH, MEM_LEN, D_MODEL), 1.0),
        "norm_g": 1.0 + nrm(ks[2], (DEPTH, D_MODEL), 0.02),
        "w_in": nrm(ks[3], (DEPTH, D_MODEL, IN_COLS), D_MODEL ** -0.5),
        "pool_w": nrm(ks[4], (DEPTH, POOL_GROUPS, POOL_GC, POOL_GC), POOL_GC ** -0.5),
        "pool_scale": 1.0 + nrm(ks[5], (DEPTH, POOL_WIDTH), 0.02),
        "mem_norm_g": 1.0 + nrm(ks[6], (DEPTH, D_MODEL), 0.02),
        "w_mem_kv": nrm(ks[7], (DEPTH, D_MODEL, 2 * MEM_WIDTH), D_MODEL ** -0.5),
        "w_branch": nrm(ks[8], (DEPTH, N_BRANCH, POOL_WIDTH, D_MODEL), POOL_WIDTH ** -0.5),
        "w_out": nrm(ks[9], (DEPTH, D_MODEL, D_MODEL), D_MODEL ** -0.5),
        "rel_bias": nrm(ks[10], (REL_BUCKETS, N_HEADS), 0.5),
        "final_g": 1.0 + nrm(ks[11], (D_MODEL,), 0.02),
    }

def first_block(x, mem, norm_g, w_in, pool_w, pool_scale, mem_norm_g, w_mem_kv,
              w_branch, w_out, rel_bias, final_g):
    b, s, _ = x.shape
    split_points = np.cumsum(np.asarray(IN_SPLITS))[:-1].tolist()
    for l in range(DEPTH):
        h = rms_norm(x, norm_g[l])
        proj = h @ w_in[l]
        (pool_u, pool_z, aq, ak, av, az, iq, ik, iw, mq, mz, gates) = jnp.split(
            proj, split_points, axis=-1)

        y_pool = multi_scale_pool(pool_u, pool_w[l], pool_scale[l]) * jax.nn.silu(pool_z)

        y_attn = dsa_attention(
            aq.reshape(b, s, N_HEADS, HEAD_DIM), ak.reshape(b, s, N_HEADS, HEAD_DIM),
            av.reshape(b, s, N_HEADS, HEAD_DIM), iq.reshape(b, s, IDX_HEADS, IDX_DIM),
            ik, iw, rel_bias) * jax.nn.silu(az)

        mkv = rms_norm(mem, mem_norm_g[l]) @ w_mem_kv[l]
        mk, mv = jnp.split(mkv, 2, axis=-1)
        mm = mem.shape[1]
        y_mem = memory_attention(
            mq.reshape(b, s, MEM_HEADS, MEM_HEAD_DIM),
            mk.reshape(b, mm, MEM_HEADS, MEM_HEAD_DIM),
            mv.reshape(b, mm, MEM_HEADS, MEM_HEAD_DIM)) * jax.nn.silu(mz)

        g = jax.nn.sigmoid(gates).reshape(b, s, N_BRANCH, D_MODEL)
        merged = (g[:, :, 0] * (y_pool @ w_branch[l, 0])
                  + g[:, :, 1] * (y_attn @ w_branch[l, 1])
                  + g[:, :, 2] * (y_mem @ w_branch[l, 2]))
        x = x + merged @ w_out[l]
    return rms_norm(x, final_g)


DEPTH_2 = 1

N_META = 16
META_PAD = (-N_META) % CHUNK
DN_HEADS = 8
DN_DK = 128
DN_DV = 128
DN_QK = DN_HEADS * DN_DK
DN_VW = DN_HEADS * DN_DV
DN_CONV = 5
SC_WIDTH = 1024
SC_CONV = 3
D_FF = -(-8 * D_MODEL // (3 * 256)) * 256
RMS_EPS = 1e-6
L2_EPS = 1e-6

SPLIT_SIZES = [DN_QK, DN_QK, DN_VW, DN_VW, 2 * DN_HEADS, 2 * DN_HEADS,
               SC_WIDTH, SC_WIDTH, SC_WIDTH, D_MODEL, D_MODEL]
W_IN_COLS = sum(SPLIT_SIZES)
SPLIT_POINTS = list(np.cumsum(SPLIT_SIZES)[:-1].tolist())


def rmsnorm(x, w):
    xf = x.astype(jnp.float32)
    y = xf * lax.rsqrt(jnp.mean(xf * xf, axis=-1, keepdims=True) + RMS_EPS)
    return (y * w.astype(jnp.float32)).astype(x.dtype)

def l2norm(t):
    return t * lax.rsqrt(jnp.sum(t * t, axis=-1, keepdims=True) + L2_EPS)

def depthwise_conv_centred(x, w):
    K, C = w.shape
    r = K // 2
    return lax.conv_general_dilated(
        x, w[:, None, :].astype(x.dtype), window_strides=(1,), padding=[(r, r)],
        dimension_numbers=("NWC", "WIO", "NWC"), feature_group_count=C)

def chunk_gated_delta_rule(q, k, v, g, beta):
    Bsz, T, H, dk = q.shape
    dv = v.shape[-1]
    N = T // CHUNK

    def chunks(t):
        return t.reshape(Bsz, N, CHUNK, H, t.shape[-1]).transpose(0, 1, 3, 2, 4)

    q, k, v = chunks(q), chunks(k), chunks(v)
    g = g.reshape(Bsz, N, CHUNK, H).transpose(0, 1, 3, 2)
    beta = beta.reshape(Bsz, N, CHUNK, H).transpose(0, 1, 3, 2)
    g = jnp.cumsum(g, axis=-1)

    tri = jnp.tril(jnp.ones((CHUNK, CHUNK), dtype=bool))
    strict = jnp.tril(jnp.ones((CHUNK, CHUNK), dtype=bool), -1)
    decay = jnp.exp(jnp.where(tri, g[..., :, None] - g[..., None, :], -jnp.inf))

    kk = jnp.einsum("bnhid,bnhjd->bnhij", k, k)
    lmat = jnp.where(strict, beta[..., :, None] * kk * decay, 0.0)
    a = lmat + jnp.eye(CHUNK, dtype=lmat.dtype)
    rhs = jnp.concatenate([v * beta[..., None], k * (beta * jnp.exp(g))[..., None]], axis=-1)
    sol = lax.linalg.triangular_solve(a, rhs, left_side=True, lower=True, unit_diagonal=True)
    u, w = sol[..., :dv], sol[..., dv:]

    qk = jnp.einsum("bnhid,bnhjd->bnhij", q, k) * decay
    q_dec = q * jnp.exp(g)[..., None]
    g_last = g[..., -1]
    k_dec = k * jnp.exp(g_last[..., None] - g)[..., None]

    xs = tuple(jnp.moveaxis(t, 1, 0) for t in (qk, q_dec, k_dec, u, w, jnp.exp(g_last)))

    def step(S, inp):
        qk_c, qd_c, kd_c, u_c, w_c, gl_c = inp
        v_new = u_c - jnp.einsum("bhcd,bhde->bhce", w_c, S)
        o_c = (jnp.einsum("bhcd,bhde->bhce", qd_c, S)
               + jnp.einsum("bhij,bhje->bhie", qk_c, v_new))
        S = S * gl_c[..., None, None] + jnp.einsum("bhcd,bhce->bhde", kd_c, v_new)
        return S, o_c

    S0 = jnp.zeros((Bsz, H, dk, dv), jnp.float32)
    _, o = lax.scan(step, S0, xs)
    return o.transpose(1, 0, 3, 2, 4).reshape(Bsz, T, H, dv)

def gated_deltanet_bidir(q, k, v, z, b_raw, a_raw, conv_w, A_log, dt_bias, norm_w):
    Bsz, L, _ = q.shape
    f32 = jnp.float32
    qkv = jax.nn.silu(depthwise_conv_centred(jnp.concatenate([q, k, v], axis=-1), conv_w)).astype(f32)
    qc, kc, vc = jnp.split(qkv, [DN_QK, 2 * DN_QK], axis=-1)
    qc = l2norm(qc.reshape(Bsz, L, DN_HEADS, DN_DK)) * (DN_DK ** -0.5)
    kc = l2norm(kc.reshape(Bsz, L, DN_HEADS, DN_DK))
    vc = vc.reshape(Bsz, L, DN_HEADS, DN_DV)
    beta = jax.nn.sigmoid(b_raw.astype(f32)).reshape(Bsz, L, 2, DN_HEADS)
    g = -jnp.exp(A_log.astype(f32)) * jax.nn.softplus(
        a_raw.astype(f32).reshape(Bsz, L, 2, DN_HEADS) + dt_bias.astype(f32))

    def pad(t):
        return jnp.pad(t, [(0, 0), (META_PAD, 0)] + [(0, 0)] * (t.ndim - 2))

    qp, kp, vp, bp, gp = pad(qc), pad(kc), pad(vc), pad(beta), pad(g)
    o_fwd = chunk_gated_delta_rule(qp, kp, vp, gp[:, :, 0], bp[:, :, 0])

    def flip(t):
        return jnp.flip(t, axis=1)

    o_bwd = flip(chunk_gated_delta_rule(flip(qp), flip(kp), flip(vp), flip(gp[:, :, 1]), flip(bp[:, :, 1])))
    o = (o_fwd + o_bwd)[:, META_PAD:]
    o = o * lax.rsqrt(jnp.mean(o * o, axis=-1, keepdims=True) + RMS_EPS) * norm_w.astype(f32)
    o = o * jax.nn.silu(z.reshape(Bsz, L, DN_HEADS, DN_DV).astype(f32))
    return o.reshape(Bsz, L, DN_VW).astype(z.dtype)

def second_inputs(seed: int = 0) -> dict:
    key = jax.random.key(seed)
    ks = jax.random.split(key, 20)
    f32 = jnp.float32

    def nrm(k, shape, scale):
        return jax.random.normal(k, shape, f32) * scale

    x = jax.random.normal(ks[0], (BATCH, SEQ, D_MODEL), f32)
    meta_tokens = nrm(ks[1], (N_META, D_MODEL), 1.0)
    norm1_w = 1.0 + nrm(ks[2], (DEPTH_2, D_MODEL), 0.02)
    w_in = nrm(ks[3], (DEPTH_2, D_MODEL, W_IN_COLS), D_MODEL ** -0.5)
    dn_conv_w = nrm(ks[4], (DEPTH_2, DN_CONV, DN_QK * 2 + DN_VW), DN_CONV ** -0.5)
    A_log = jnp.log(jax.random.uniform(ks[5], (DEPTH_2, 2, DN_HEADS), f32, 1.0, 16.0))
    dt = jnp.exp(jax.random.uniform(ks[6], (DEPTH_2, 2, DN_HEADS), f32, np.log(1e-3), np.log(1e-1)))
    dt_bias = dt + jnp.log(-jnp.expm1(-dt))
    dn_norm_w = 1.0 + nrm(ks[7], (DEPTH_2, DN_DV), 0.02)
    sc_conv_w = nrm(ks[8], (DEPTH_2, SC_CONV, SC_WIDTH), SC_CONV ** -0.5)
    w_branch_dn = nrm(ks[9], (DEPTH_2, DN_VW, D_MODEL), DN_VW ** -0.5)
    w_branch_sc = nrm(ks[10], (DEPTH_2, SC_WIDTH, D_MODEL), SC_WIDTH ** -0.5)
    w_out = nrm(ks[11], (DEPTH_2, D_MODEL, D_MODEL), D_MODEL ** -0.5)
    norm2_w = 1.0 + nrm(ks[12], (DEPTH_2, D_MODEL), 0.02)
    w_gate_up = nrm(ks[13], (DEPTH_2, D_MODEL, 2 * D_FF), D_MODEL ** -0.5)
    w_down = nrm(ks[14], (DEPTH_2, D_FF, D_MODEL), D_FF ** -0.5)
    final_norm_w = 1.0 + nrm(ks[15], (D_MODEL,), 0.02)
    return {"x": x, "meta_tokens": meta_tokens, "norm1_w": norm1_w, "w_in": w_in,
            "dn_conv_w": dn_conv_w, "A_log": A_log, "dt_bias": dt_bias, "dn_norm_w": dn_norm_w,
            "sc_conv_w": sc_conv_w, "w_branch_dn": w_branch_dn, "w_branch_sc": w_branch_sc,
            "w_out": w_out, "norm2_w": norm2_w, "w_gate_up": w_gate_up, "w_down": w_down,
            "final_norm_w": final_norm_w}

def second_block(x, meta_tokens, norm1_w, w_in, dn_conv_w, A_log, dt_bias, dn_norm_w,
              sc_conv_w, w_branch_dn, w_branch_sc, w_out, norm2_w, w_gate_up, w_down,
              final_norm_w):
    Bsz = x.shape[0]
    meta = jnp.broadcast_to(meta_tokens[None].astype(x.dtype), (Bsz, N_META, x.shape[-1]))
    h_res = jnp.concatenate([meta, x], axis=1)
    for l in range(DEPTH_2):
        h = rmsnorm(h_res, norm1_w[l])
        proj = h @ w_in[l]
        (q, k, v, z, b_raw, a_raw, sc_b, sc_c, sc_x, gate_a, gate_b) = jnp.split(proj, SPLIT_POINTS, axis=-1)
        o_dn = gated_deltanet_bidir(q, k, v, z, b_raw, a_raw, dn_conv_w[l], A_log[l], dt_bias[l], dn_norm_w[l])
        y_a = o_dn @ w_branch_dn[l]
        y_b = (sc_b * depthwise_conv_centred(sc_c * sc_x, sc_conv_w[l])) @ w_branch_sc[l]
        merged = jax.nn.sigmoid(gate_a) * y_a + jax.nn.sigmoid(gate_b) * y_b
        h_res = h_res + merged @ w_out[l]
        h2 = rmsnorm(h_res, norm2_w[l])
        gu = h2 @ w_gate_up[l]
        h_res = h_res + (jax.nn.silu(gu[..., :D_FF]) * gu[..., D_FF:]) @ w_down[l]
    out = rmsnorm(h_res, final_norm_w)
    return out[:, N_META:]


def setup_inputs(seed=0):
    out = dict(first_inputs(seed))
    for name, value in second_inputs(seed + 1).items():
        if name != "x":
            out[name + "_2"] = value
    return out


def reference(
    x, mem, norm_g, w_in, pool_w, pool_scale, mem_norm_g, w_mem_kv, w_branch, w_out, rel_bias,
    final_g, meta_tokens_2, norm1_w_2, w_in_2, dn_conv_w_2, A_log_2, dt_bias_2, dn_norm_w_2,
    sc_conv_w_2, w_branch_dn_2, w_branch_sc_2, w_out_2, norm2_w_2, w_gate_up_2, w_down_2,
    final_norm_w_2,
):
    x = first_block(
        x, mem, norm_g, w_in, pool_w, pool_scale, mem_norm_g, w_mem_kv, w_branch, w_out,
        rel_bias, final_g,
    )
    return second_block(
        x, meta_tokens_2, norm1_w_2, w_in_2, dn_conv_w_2, A_log_2, dt_bias_2, dn_norm_w_2,
        sc_conv_w_2, w_branch_dn_2, w_branch_sc_2, w_out_2, norm2_w_2, w_gate_up_2, w_down_2,
        final_norm_w_2,
    )


_drawn_inputs = setup_inputs


def setup_inputs(seed=0):
    import zlib

    import numpy as np

    out = dict(_drawn_inputs(seed))
    spreads = {}
    factors = {'pool_scale': 4.281,
     'mem_norm_g': 8.0,
     'norm1_w_2': 2.824,
     'dn_norm_w_2': 37.203,
     'norm2_w_2': 13.901,
     'final_norm_w_2': 8.267}
    for name, (base, spread) in spreads.items():
        noise = np.random.default_rng([zlib.crc32(name.encode()), seed]).standard_normal(out[name].shape)
        drawn = base * np.exp(spread * noise) if base else spread * noise
        out[name] = __import__('jax').numpy.asarray(drawn.astype(out[name].dtype))
    for name, factor in factors.items():
        out[name] = (out[name] * factor).astype(out[name].dtype)
    return out
```

```python
import math
from contextlib import ExitStack

import numpy as np

import concourse.bass as bass
from concourse import mybir
from concourse.alu_op_type import AluOpType as ALU

ACT = mybir.ActivationFunctionType
AX = mybir.AxisListType.X
F32 = mybir.dt.float32
F32R = mybir.dt.float32r
BF16 = mybir.dt.bfloat16

P = 128
D = 1024
KT = D // P
S = 256
NM = 16
T = NM + S
LAYERS = 2
HEADS, HD = 8, 64
TOPK = 64
MHEADS = 4
POOLG = 4
POOL_WINDOWS = (2, 4, 8, 16)
PAD = 8
ATTN_SCALE = HD ** -0.5
IDX_W_SCALE = (HD ** -0.5) * (HEADS ** -0.5)
MEM_SCALE = P ** -0.5
EPS = 1e-6
NEG = -1e30
TAKEN = -3e38
SLOTS = 4
BLK = KT * P
AHEAD = 2
MEM_GROUPS = 4
LAYER_GROUPS = 20
ACT_EVACS = 60
DVE_EVACS = 20
G_NORM, G_MEM, G_POOL, G_FINAL = 0, 16, 32, 40
G_NORM1, G_NORM2, G_FINAL2, G_DN = 48, 56, 64, 72
G_CONV, G_SC = 73, 73 + 24 * 5
G_COLS = G_SC + 8 * 3

DN = 8
C = 64
STEPS = 5
TP = STEPS * C
PADS = TP - T
FT = 22
C2_COLS = 6 * P + 13 * C
LEVELS = 6
G2 = MEM_GROUPS + LAYERS * LAYER_GROUPS
G_Z, G_SCX, G_BR, G_WO, G_GU, G_DOWN = G2 + 6, G2 + 14, G2 + 18, G2 + 22, G2 + 24, G2 + 35
E2 = 4 * MEM_GROUPS + LAYERS * ACT_EVACS
D2 = LAYERS * DVE_EVACS
DN_SCALE = P ** -0.5


def build(nc, a, out):
    with ExitStack() as ctx:
        def sb(name, shape, dt=F32, scope=ctx):
            return scope.enter_context(nc.sbuf_tensor(name, shape, dt))

        def sem(name):
            return ctx.enter_context(nc.semaphore(name))

        stream_ps = [ctx.enter_context(nc.psum_tensor(f"stream_ps{s}", [P, 512], F32)) for s in range(SLOTS)]
        free_ps = [ctx.enter_context(nc.psum_tensor(f"free_ps{i}", [P, 512], F32)) for i in range(4)]

        xT = sb("xT", [P, KT, T])
        h_hi = sb("h_hi", [P, KT, T], F32R)
        h_lo = sb("h_lo", [P, KT, T], F32R)
        wide = sb("wide", [P, KT, T])
        raw = sb("raw", [P, SLOTS, BLK])
        w_hi = [sb(f"w_hi{s}", [P, KT, P], F32R) for s in range(SLOTS)]
        w_lo = [sb(f"w_lo{s}", [P, KT, P], F32R) for s in range(SLOTS)]
        cst = sb("cst", [P, 2 * P])
        ident, ones = cst[:, 0:P], cst[:, P:2 * P]
        ident_bf = sb("ident_bf", [P, P], BF16)
        gains = sb("gains", [P, G_COLS])
        rstd = sb("rstd", [P, T])
        eps_col = sb("eps_col", [P, 1])
        iqT, qT, merged = wide[:, 0:4, 0:S], wide[:, 4:8, 0:S], wide[:, :, 0:S]
        mqT = iqT

        with ExitStack() as one:
            bias = sb("bias", [P, HEADS, S], scope=one)
            mkT = sb("mkT", [P, LAYERS * MHEADS, S], scope=one)
            mv = sb("mv", [P, LAYERS, 2, 512], scope=one)
            with ExitStack() as pro:
                mem_raw = sb("mem_raw", [P, KT, S], scope=pro)
                mem_f = sb("mem_f", [P, KT, S], scope=pro)
                mem_hi = [sb(f"mem_hi{l}", [P, KT, S], F32R, pro) for l in range(LAYERS)]
                mem_lo = [sb(f"mem_lo{l}", [P, KT, S], F32R, pro) for l in range(LAYERS)]
                rel_cst = sb("rel_cst", [P, P + 512], scope=pro)
                rel_sb = sb("rel_sb", [32, HEADS], scope=pro)
                rel_f = sb("rel_f", [HEADS, 512], scope=pro)
                hankel = sb("hankel", [P, HEADS, S], scope=pro)
            flip, bucket_hot = rel_cst[:, 0:P], rel_cst[0:32, P:P + 512]
            gates = sb("gates", [P, 24, S], scope=one)
            h32 = gates[:, 0:KT, :]
            with ExitStack() as win:
                y01_hi = sb("y01_hi", [P, 2, 4, S], F32R, win)
                sum_a = sb("sum_a", [P, POOLG, PAD + S], scope=win)
                sum_b = sb("sum_b", [P, POOLG, PAD + S], scope=win)
            y_hi = sb("y_hi", [P, 3, 4, S], F32R, one)
            y_lo = sb("y_lo", [P, 3, 4, S], F32R, one)
            az, pz, mz = (sb(n, [P, 4, S], scope=one) for n in ("az", "pz", "mz"))
            kT = sb("kT", [P, 4, S], scope=one)
            v = sb("v", [P, 2, 512], scope=one)
            pu = sb("pu", [P, POOLG, PAD + S], scope=one)
            soft = sb("soft", [P, 2, 512], scope=one)
            softT = sb("softT", [P, 2, 512], scope=one)
            idx_r, idx_s, idx_w = soft[:, :, 0:384], softT[:, 0, 0:384], softT[:, 1, 0:384]
            stage = sb("stage", [P, KT * 136], scope=one)
            wik = stage[:, :].rearrange("p (k n) -> p k n", k=KT)
            st_q, st_k = stage[:, 0:S], stage[:, S:2 * S]
            st_v = stage[:, 2 * S:3 * S].rearrange("p (t n) -> p t n", t=2)
            st_mq = stage[:, 0:512].rearrange("p (h n) -> p h n", h=2)
            st_mv = stage[:, 512:1024].rearrange("p (t n) -> p t n", t=2)
            pool_w = sb("pool_w", [P, POOLG, P], scope=one)
            ikT = sb("ikT", [P, S], scope=one)
            iw = sb("iw", [P, 2, HEADS], scope=one)
            admit = sb("admit", [P, 384 + POOLG * 16], scope=one)
            mask = sb("mask", [P, 384], BF16, one)
            top8 = sb("top8", [P, 2, 8], scope=one)
            stat = sb("stat", [P, 4, 4], scope=one)
            edge = admit[:, 384:].rearrange("p (g t) -> p g t", g=POOLG)

        with ExitStack() as two:
            cst2 = sb("cst2", [P, C2_COLS], scope=two)
            wba = sb("wba", [P, KT, 4 * DN], scope=two)
            adt = sb("adt", [P, 2 * DN], scope=two)
            oT = sb("oT", [P, KT, TP], scope=two)
            scal = sb("scal", [P, STEPS, 6 * DN], scope=two)
            beta_t, dt_u, sp, log_decay = (sb(n, [P, STEPS, DN], scope=two) for n in ("beta_t", "dt_u", "sp", "log_decay"))
            exg = sb("exg", [P, 5, STEPS, DN], scope=two)
            gcol = sb("gcol", [P, STEPS * DN], scope=two)
            ea = sb("ea", [P, DN], scope=two)
            with ExitStack() as dn:
                qkvT = sb("qkvT", [P, 3, DN, TP], scope=dn)
                decay = sb("decay", [P, STEPS * DN, C], scope=dn)
                with ExitStack() as conv:
                    st_raw = sb("st_raw", [P, SLOTS, T + 4], scope=conv)
                    k_sq = sb("k_sq", [P, DN, T], scope=conv)
                    beta_strict = sb("beta_strict", [P, STEPS * DN, C], scope=conv)
                lvl = sb("lvl", [P, 6, DN, C], scope=dn)
                xy = sb("xy", [P, 2, 2, 4, C], scope=dn)
                n1 = sb("n1", [P, 2, 4, C], scope=dn)
                vb = sb("vb", [P, DN, P], scope=dn)
                kdec = sb("kdec", [P, DN, P], scope=dn)
                kqs = sb("kqs", [P, DN, 6, C], scope=dn)
                vs = sb("vs", [P, DN, 2, C], scope=dn)
                sc = sb("sc", [P, 6 * DN], scope=dn)
                state = sb("state", [P, 2, DN, P], scope=dn)
                at = sb("at", [P, 2, DN, C], scope=dn)
            with ExitStack() as br2:
                sz, ga, gb = (sb(n, [P, KT, T], scope=br2) for n in ("sz", "ga", "gb"))
                cx = sb("cx", [P, KT, T + 2], scope=br2)
                bcv = sb("bcv", [P, 2, T], scope=br2)
                yd_hi, yd_lo, ys_hi, ys_lo = (sb(n, [P, KT, T], F32R, br2) for n in ("yd_hi", "yd_lo", "ys_hi", "ys_lo"))
            f_hi = sb("f_hi", [P, FT, T], F32R, two)
            f_lo = sb("f_lo", [P, FT, T], F32R, two)
            f_act, f_val = (sb(n, [P, 2, T], scope=two) for n in ("f_act", "f_val"))
        h32p = oT
        h32t = oT[:, :, TP - T:]
        vo = wide[:, :, :].rearrange("p k n -> p (k n)")[:, 0:2 * DN * P].rearrange("p (d h n) -> p d h n", d=2, h=DN)
        mat = lambda i: cst2[:, i * P:(i + 1) * P]
        col = lambda i: cst2[:, 6 * P + i * C:6 * P + (i + 1) * C]
        tri, tri_swap, after, rows_f, rows_b, same = (mat(i) for i in range(6))
        tri_c, sigma, strict, upper, eye_c = (col(i) for i in range(5))

        x_in, mem_in, gains_in, cst_in, rel_in, admit_in, wik_in, poolw_in = (
            sem(n) for n in ("x_in", "mem_in", "gains_in", "cst_in", "rel_in", "admit_in", "wik_in", "poolw_in"))
        w_in = [sem(f"w_in{s}") for s in range(SLOTS)]
        hi_ready, lo_ready, blk_done, act_evac, dve_evac = (
            sem(n) for n in ("hi_ready", "lo_ready", "blk_done", "act_evac", "dve_evac"))
        sq_ready, ss_ready, rstd_ready, n32_ready, nhi_ready, nlo_ready = (
            sem(n) for n in ("sq_ready", "ss_ready", "rstd_ready", "n32_ready", "nhi_ready", "nlo_ready"))
        mem32_ready, memhi_ready, memlo_ready = (sem(n) for n in ("mem32_ready", "memhi_ready", "memlo_ready"))
        ident_ready, relf_done, relf_ready, relf_out, hankel_in, flip_done, bias_ready = (
            sem(n) for n in ("ident_ready", "relf_done", "relf_ready", "relf_out", "hankel_in", "flip_done", "bias_ready"))
        ikw_done, ikw_ready, idx_done, idx_relu, idx_used, mask_ready = (
            sem(n) for n in ("ikw_done", "ikw_ready", "idx_done", "idx_relu", "idx_used", "mask_ready"))
        qk_staged, v_staged, logit_done, max_ready, exp_ready, prob_ready, softT_done, softT_ready, pv_done, pv_used = (
            sem(n) for n in ("qk_staged", "v_staged", "logit_done", "max_ready", "exp_ready", "prob_ready",
                             "softT_done", "softT_ready", "pv_done", "pv_used"))
        pads_ready, pooled_ready, mixed_done, mixed_used, y_ready = (
            sem(n) for n in ("pads_ready", "pooled_ready", "mixed_done", "mixed_used", "y_ready"))
        part_used, mhi_ready, mlo_ready = (sem(n) for n in ("part_used", "mhi_ready", "mlo_ready"))
        stored = sem("stored")
        c2_in, wba_in, ba_done, th_ready, u_ready, ewu_ready, g_ready, gsum_done, gsum_ready, scal_ready = (
            sem(n) for n in ("c2_in", "wba_in", "ba_done", "th_ready", "u_ready", "ewu_ready", "g_ready", "gsum_done",
                             "gsum_ready", "scal_ready"))
        gd_ready, e_done, e_used, e_ready, expe_ready, decay_ready = (
            sem(n) for n in ("gd_ready", "e_done", "e_used", "e_ready", "expe_ready", "decay_ready"))
        zeros_ready, conv_done, silu_ready, l2sq_ready, l2_done, l2_used, l2rs_ready, l2_ready = (
            sem(n) for n in ("zeros_ready", "conv_done", "silu_ready", "l2sq_ready", "l2_done", "l2_used", "l2rs_ready", "l2_ready"))
        dn_staged, kkq_done, kkq_used, lvl_ready, at_ready, vk_done, vk_used, ks_done, r_ready = (
            sem(n) for n in ("dn_staged", "kkq_done", "kkq_used", "lvl_ready", "at_ready", "vk_done", "vk_used", "ks_done", "r_ready"))
        n1_done, n1_ready, yx_done, yx_ready, vnew_done, vnew_ready, o_done, o_used, su_done, sdec_ready, s_ready = (
            sem(n) for n in ("n1_done", "n1_ready", "yx_done", "yx_ready", "vnew_done", "vnew_ready", "o_done", "o_used",
                             "su_done", "sdec_ready", "s_ready"))
        osq_ready, oss_done, oss_used, ors_ready, yd_ready, ydhi_ready, ydlo_ready, yshi_ready, yslo_ready = (
            sem(n) for n in ("osq_ready", "oss_done", "oss_used", "ors_ready", "yd_ready", "ydhi_ready", "ydlo_ready",
                             "yshi_ready", "yslo_ready"))
        fact_ready, fhi_ready, flo_ready = (sem(n) for n in ("fact_ready", "fhi_ready", "flo_ready"))
        held = sem("held")
        bank = (stream_ps, free_ps)
        e_bank = [free_ps[i] for i in (3, 0, 1, 3, 0)]

        block = ctx.enter_context(nc.Block())
        rel_dram = a["rel_scratch"]

        def split_hi(act, G, s):
            act.wait_ge(w_in[s], 16 * (G + 1))
            act.wait_ge(blk_done, 4 * G + s + 1)
            nc.scalar.activation(w_hi[s][:, :, :], raw[:, s, :].rearrange("p (k n) -> p k n", k=KT),
                                 ACT.Copy).then_inc(hi_ready, 1)

        def split_lo(dve, G, s):
            dve.wait_ge(hi_ready, 4 * G + s + 1)
            nc.vector.tensor_tensor(w_lo[s][:, :, :], raw[:, s, :].rearrange("p (k n) -> p k n", k=KT),
                                    w_hi[s][:, :, :].bitcast(F32), ALU.subtract).then_inc(lo_ready, 1)

        def ahead(split, eng, G, s):
            split(eng, G + (s + AHEAD) // SLOTS, (s + AHEAD) % SLOTS)

        def mm3(ps, l_hi, l_lo, r_hi, r_lo, first, last):
            nc.tensor.matmul(ps, l_hi, r_hi, start=first, stop=False)
            nc.tensor.matmul(ps, l_hi, r_lo, start=False, stop=False)
            return nc.tensor.matmul(ps, l_lo, r_hi, start=False, stop=last)

        def block_cols(pe, G, s, free, free_at, r_hi, r_lo):
            pe.wait_ge(lo_ready, 4 * G + s + 1 + SLOTS)
            pe.wait_ge(free, free_at)
            n = r_hi.shape[-1]
            for k in range(KT):
                mm = mm3(stream_ps[s][:, 0:n], w_hi[s][:, k, :], w_lo[s][:, k, :], r_hi[:, k, :], r_lo[:, k, :],
                         k == 0, k == KT - 1)
            mm.then_inc(blk_done, 1)

        def block_rows(pe, G, s, free, free_at, l_hi, l_lo):
            pe.wait_ge(lo_ready, 4 * G + s + 1 + SLOTS)
            pe.wait_ge(free, free_at)
            for t in range(2):
                for k in range(KT):
                    tok = slice(t * P, (t + 1) * P)
                    mm = mm3(stream_ps[s][:, tok], l_hi[:, k, tok], l_lo[:, k, tok], w_hi[s][:, k, :], w_lo[s][:, k, :],
                             k == 0, k == KT - 1)
            mm.then_inc(blk_done, 1)

        def evac(act, G, s, dst, func=ACT.Copy, scale=1.0):
            act.wait_ge(blk_done, 4 * G + s + 1 + SLOTS)
            n = dst.shape[-1] if len(dst.shape) == 2 else dst.shape[-1] * dst.shape[-2]
            src = stream_ps[s][:, 0:n]
            if len(dst.shape) == 3:
                src = src.rearrange("p (t n) -> p t n", n=dst.shape[-1])
            nc.scalar.activation(dst, src, func, scale=scale).then_inc(act_evac, 1)

        tok = slice(NM, T)
        xS, hS_hi, hS_lo, wideS = xT[:, :, tok], h_hi[:, :, tok], h_lo[:, :, tok], wide[:, :, tok]
        G0 = MEM_GROUPS

        def rstd_of(act, i, n):
            act.wait_ge(ss_ready, i + 1)
            nc.scalar.activation(rstd[:, 0:n], free_ps[0][:, 0:n], ACT.Ln, bias=eps_col[:, 0:1], scale=1.0 / D)
            nc.scalar.drain()
            nc.scalar.activation(rstd[:, 0:n], rstd[:, 0:n], ACT.Exp, scale=-0.5).then_inc(rstd_ready, 1)

        def sum_squares(pe, sq, i, sq_at):
            n = sq.shape[-1]
            for k in range(KT):
                pe.wait_ge(sq_ready, sq_at + k + 1)
                mm = nc.tensor.matmul(free_ps[0][:, 0:n], ones, sq[:, k, :], start=k == 0, stop=k == KT - 1)
            mm.then_inc(ss_ready, 1)

        def scale_rows(dve, dst, src, gain, half, ready):
            n = src.shape[-1]
            for k in range(4 * half, 4 * half + 4):
                op = nc.vector.scalar_tensor_tensor(out=dst[:, k, :], in0=src[:, k, :], scalar=gain(k),
                                                    in1=rstd[:, 0:n], op0=ALU.mult, op1=ALU.mult)
            op.then_inc(ready, 1)

        def gain_col(base, l=0):
            return lambda k: gains[:, bass.ds(base + KT * l + k, 1)]

        consts_ready = sem("consts_ready")

        @block.sync
        def _(sp):
            with sp.Fori(0, a["groups"]) as G:
                for s in range(SLOTS):
                    sp.wait_ge(lo_ready, 4 * G + s + 1)
                    sp.dma_start(raw[:, s, :], a["stream"][4 * G + s]).then_inc(w_in[s], 16)
            for s in range(AHEAD):
                sp.wait_ge(lo_ready, 4 * a["groups"] + s + 1)
                sp.dma_start(raw[:, s, :], a["stream"][4 * a["groups"] + s]).then_inc(w_in[s], 16)
            sp.wait_ge(stored, 32)

        @block.gpsimd
        def _(pool):
            nc.gpsimd.memset(eps_col[:, :], EPS).then_inc(consts_ready, 1)
            pool.wait_ge(relf_ready, 1)
            pool.dma_start(rel_dram, rel_f[:, :]).then_inc(relf_out, 16)
            pool.wait_ge(relf_out, 16)
            pool.dma_start(hankel[:, :, :], bass.AP(rel_dram.tensor, 0, [[1, P], [512, HEADS], [1, S]])).then_inc(hankel_in, 16)
            pool.sem_inc(part_used, 2)
            pool.wait_ge(flip_done, HEADS)
            nc.gpsimd.memset(pu[:, :, 0:PAD], 0.0)
            nc.gpsimd.drain()
            with pool.Fori(0, LAYERS) as l:
                E0 = SLOTS + 4 * MEM_GROUPS + ACT_EVACS * l
                pool.wait_ge(blk_done, SLOTS + 4 * (G0 + LAYER_GROUPS * l))
                pool.wait_ge(act_evac, E0 + 32)
                src, dst = pu, sum_a
                for i in range(POOLG):
                    w = 1 << i
                    nc.gpsimd.tensor_tensor(dst[:, i:, PAD:], src[:, i:, PAD:], src[:, i:, PAD - w:PAD + S - w], ALU.add)
                    if i == 0:
                        nc.gpsimd.memset(sum_a[:, :, 0:PAD], 0.0)
                        nc.gpsimd.memset(sum_b[:, :, 0:PAD], 0.0)
                    nc.gpsimd.drain()
                    src, dst = dst, (sum_b if dst is sum_a else sum_a)
                nc.gpsimd.drain()
                for g in range(POOLG):
                    total = (sum_a, sum_b)[g % 2]
                    nc.gpsimd.tensor_tensor(total[:, g, PAD:PAD + 16], total[:, g, PAD:PAD + 16], edge[:, g, :], ALU.mult)
                    nc.gpsimd.tensor_scalar(total[:, g, PAD + 16:], total[:, g, PAD + 16:], 1.0 / POOL_WINDOWS[g], 0.0, ALU.mult, ALU.add)
                nc.gpsimd.drain()
                for g in range(POOLG):
                    total = (sum_a, sum_b)[g % 2]
                    op = nc.gpsimd.tensor_tensor(pu[:, g, PAD:], total[:, g, PAD:], pu[:, g, PAD:], ALU.subtract)
                op.then_inc(pooled_ready, 1)
                with pool.Fori(0, 4) as hp:
                    pool.wait_ge(logit_done, 6 * l + hp + 1)
                    nc.gpsimd.tensor_copy(st_q, qT[:, bass.ds(hp, 1), :])
                    nc.gpsimd.tensor_copy(st_k, kT[:, bass.ds(hp, 1), :]).then_inc(qk_staged, 1)
                    pool.wait_ge(pv_done, 6 * l + hp + 1)
                    nc.gpsimd.tensor_copy(st_v, v[:, :, bass.ds(hp * P, P)]).then_inc(v_staged, 1)
                with pool.Fori(0, 2) as mp:
                    pool.wait_ge(pv_done, 6 * l + 4 + mp + 1)
                    nc.gpsimd.tensor_copy(st_mq, mqT[:, bass.ds(2 * mp, 2), :]).then_inc(qk_staged, 1)
                    nc.gpsimd.tensor_copy(st_mv, mv[:, bass.ds(l, 1), :, bass.ds(mp * 2 * P, 2 * P)]).then_inc(v_staged, 1)
                nc.gpsimd.drain()
                nc.gpsimd.memset(merged, 0.0)
                nc.gpsimd.drain()
                with pool.Fori(0, 3) as br:
                    for s in range(SLOTS):
                        pool.wait_ge(dve_evac, SLOTS + DVE_EVACS * l + 4 * br + s + 1)
                        mg = merged[:, 2 * s:2 * s + 2, :]
                        nc.gpsimd.tensor_tensor(mg, mg, soft[:, s % 2, :].rearrange("p (k n) -> p k n", k=2),
                                                ALU.add).then_inc(part_used, 1)
                    nc.gpsimd.drain()

            pool.wait_ge(n32_ready, 2 * LAYERS + 2)
            for zeros in (st_raw[:, :, 0:2], st_raw[:, :, T + 2:], h32p[:, :, 0:PADS], qkvT[:, :, :, 0:PADS]):
                op = nc.gpsimd.memset(zeros, 0.0)
            op.then_inc(zeros_ready, 1)
            nc.gpsimd.memset(state[:, :, :, :], 0.0)
            pool.wait_ge(c2_in, 16)
            for d in range(2):
                nc.gpsimd.tensor_copy(at[:, d, :, :], eye_c.unsqueeze(1).broadcast_to([P, DN, C]))
            pool.wait_ge(scal_ready, 1)
            nc.gpsimd.tensor_tensor(beta_strict[:, :, :], strict.unsqueeze(1).broadcast_to([P, STEPS * DN, C]),
                                    beta_t[:, :, :].rearrange("p t h -> p (t h)").unsqueeze(2).broadcast_to([P, STEPS * DN, C]), ALU.mult)
            nc.gpsimd.drain()
            nc.gpsimd.tensor_tensor(beta_strict[:, :, :], beta_strict[:, :, :], upper.unsqueeze(1).broadcast_to([P, STEPS * DN, C]), ALU.add)
            nc.gpsimd.drain()
            pool.wait_ge(expe_ready, 1)
            nc.gpsimd.tensor_tensor(decay[:, :, :], decay[:, :, :], beta_strict[:, :, :], ALU.mult).then_inc(decay_ready, 1)
            for i, dst in enumerate((wide, k_sq)):
                pool.wait_ge(silu_ready, i + 1)
                for half in range(2):
                    hs = slice(4 * half, 4 * half + 4)
                    src = qkvT[:, i, hs, PADS:]
                    nc.gpsimd.tensor_tensor(dst[:, hs, :], src, src, ALU.mult).then_inc(l2sq_ready, 1)
            pool.wait_ge(l2_ready, 4)
            pool.wait_ge(silu_ready, 3)
            with pool.Fori(0, STEPS) as t:
                nc.gpsimd.drain()
                pool.wait_ge(r_ready, 2 * t + 1)
                pool.wait_ge(vk_used, 2 * t + 1)
                f, b = bass.ds(C * t, C), bass.ds(C * (STEPS - 1) - C * t, C)
                for slot, src, chunk in ((0, 1, f), (1, 1, b), (2, 0, b), (3, 1, b), (4, 1, f), (5, 0, f)):
                    nc.gpsimd.tensor_copy(kqs[:, :, slot, :], qkvT[:, src, :, chunk])
                nc.gpsimd.tensor_copy(vs[:, :, 0, :], qkvT[:, 2, :, f])
                nc.gpsimd.tensor_copy(vs[:, :, 1, :], qkvT[:, 2, :, b])
                nc.gpsimd.tensor_copy(sc[:, :], scal[:, bass.ds(t, 1), :].rearrange("p a n -> p (a n)")).then_inc(dn_staged, 1)
                for level in range(LEVELS):
                    if level == LEVELS - 1:
                        nc.gpsimd.drain()
                    for half in range(2):
                        hs = slice(4 * half, 4 * half + 4)
                        if level == 0:
                            pool.wait_ge(kkq_used, 2 * t + half + 1)
                        nc.gpsimd.tensor_tensor(lvl[:, level, hs, :], lvl[:, LEVELS - 1, hs, :],
                                                col(5 + level).unsqueeze(1).broadcast_to([P, 4, C]), ALU.mult).then_inc(lvl_ready, 1)
                for half in range(2):
                    hs = slice(4 * half, 4 * half + 4)
                    for d in range(2):
                        op = nc.gpsimd.tensor_tensor(at[:, d, hs, :], at[:, d, hs, :], col(11 + d).unsqueeze(1).broadcast_to([P, 4, C]), ALU.mult)
                    op.then_inc(at_ready, 1)
                for half in range(2):
                    hs = slice(4 * half, 4 * half + 4)
                    pool.wait_ge(ks_done, 2 * t + half + 1)
                    for d in range(2):
                        decay_s = sc[:, (4 + d) * DN + 4 * half:(4 + d) * DN + 4 * half + 4].unsqueeze(2).broadcast_to([P, 4, P])
                        op = nc.gpsimd.tensor_tensor(state[:, d, hs, :], state[:, d, hs, :], decay_s, ALU.mult)
                    op.then_inc(sdec_ready, 1)

        @block.scalar
        def _(act):
            act.dma_start(mem_raw[:, :, :], a["memT"]).then_inc(mem_in, 16)
            act.dma_start(xT[:, :, :], a["xT"]).then_inc(x_in, 16)
            act.dma_start(cst[:, :], a["cst"]).then_inc(cst_in, 16)
            act.dma_start(gains[:, :], a["gains"]).then_inc(gains_in, 16)
            act.dma_start(rel_cst[:, :], a["rel_cst"]).then_inc(rel_in, 16)
            act.dma_start(rel_sb[:, :], a["rel_bias"]).then_inc(rel_in, 16)
            act.dma_start(admit[:, :], a["admit"]).then_inc(admit_in, 16)
            act.sem_inc(act_evac, SLOTS)
            act.wait_ge(mem_in, 16)
            for k in range(KT):
                nc.scalar.activation(mem_f[:, k, :], mem_raw[:, k, :], ACT.Square).then_inc(sq_ready, 1)
            act.wait_ge(x_in, 16)
            for k in range(KT):
                nc.scalar.activation(wide[:, k, :], xT[:, k, :], ACT.Square).then_inc(sq_ready, 1)
            for s in range(AHEAD):
                split_hi(act, 0, s)
            act.wait_ge(consts_ready, 1)
            rstd_of(act, 0, S)
            for l in range(LAYERS):
                for half in range(2):
                    act.wait_ge(mem32_ready, 2 * l + half + 1)
                    ks = slice(4 * half, 4 * half + 4)
                    nc.scalar.activation(mem_hi[l][:, ks, :], mem_f[:, ks, :], ACT.Copy).then_inc(memhi_ready, 1)
            act.wait_ge(relf_done, 1)
            nc.scalar.activation(rel_f[:, :], free_ps[1][0:HEADS, :], ACT.Copy).then_inc(relf_ready, 1)
            for l in range(LAYERS):
                for s in range(SLOTS):
                    ahead(split_hi, act, 2 * l, s)
                    evac(act, 2 * l, s, mkT[:, 4 * l + s, :])
                for s in range(SLOTS):
                    ahead(split_hi, act, 2 * l + 1, s)
                    evac(act, 2 * l + 1, s, mv[:, l, :, s * P:(s + 1) * P])

            act.wait_ge(bias_ready, HEADS)
            with act.Fori(0, LAYERS) as l:
                G = G0 + LAYER_GROUPS * l
                act.wait_ge(pv_done, 6 * l + 1)
                act.dma_start(wik, a["wik"][l]).then_inc(wik_in, 16)
                act.wait_ge(mixed_used, l + 1)
                act.dma_start(pool_w[:, :, :], a["pool_w"][l]).then_inc(poolw_in, 16)
                rstd_of(act, 1 + l, S)
                for half in range(2):
                    act.wait_ge(n32_ready, 2 * l + half + 1)
                    ks = slice(4 * half, 4 * half + 4)
                    nc.scalar.activation(hS_hi[:, ks, :], h32[:, ks, :], ACT.Copy).then_inc(nhi_ready, 1)
                for s in range(SLOTS):
                    ahead(split_hi, act, G, s)
                    evac(act, G, s, iqT[:, s, :])
                act.wait_ge(ikw_done, l + 1)
                nc.scalar.activation(ikT[:, :], free_ps[1][:, 0:S], ACT.Copy)
                nc.scalar.activation(iw[:, :, :], free_ps[2][:, 0:2 * HEADS].rearrange("p (t h) -> p t h", t=2),
                                     ACT.Copy, scale=IDX_W_SCALE).then_inc(ikw_ready, 1)
                for s in range(SLOTS):
                    ahead(split_hi, act, G + 1, s)
                    evac(act, G + 1, s, qT[:, s, :])
                for half, dst in ((0, kT), (1, v)):
                    for s in range(SLOTS):
                        ahead(split_hi, act, G + 2 + half, s)
                        h = 4 * half + s
                        act.wait_ge(idx_done, HEADS * l + h + 1)
                        act.wait_ge(idx_used, HEADS * l + h + 1)
                        nc.scalar.activation(idx_r[:, h % 2, :], free_ps[h % 4][:, 0:384], ACT.Relu).then_inc(idx_relu, 1)
                        evac(act, G + 2 + half, s, kT[:, s, :] if half == 0 else v[:, :, s * P:(s + 1) * P])
                for i, dst in enumerate((az, pz, mz)):
                    for s in range(SLOTS):
                        ahead(split_hi, act, G + 4 + i, s)
                        evac(act, G + 4 + i, s, dst[:, s, :], ACT.Silu)
                for s in range(SLOTS):
                    ahead(split_hi, act, G + 7, s)
                    evac(act, G + 7, s, pu[:, s, PAD:])
                for s in range(SLOTS):
                    ahead(split_hi, act, G + 8, s)
                    evac(act, G + 8, s, mqT[:, s, :])

                with act.Fori(0, 4) as hp:
                    for s in range(SLOTS):
                        ahead(split_hi, act, G + 9 + hp, s)
                        if s == 0:
                            act.wait_ge(max_ready, 6 * l + hp + 1)
                            for j in range(2):
                                for t, cols in ((0, slice(0, P)), (1, slice(P, 3 * P))):
                                    op = nc.scalar.activation(soft[:, j, cols], soft[:, j, cols], ACT.Exp,
                                                              bias=stat[:, 0, 2 * t + j:2 * t + j + 1],
                                                              accum_out=stat[:, 1, 2 * t + j:2 * t + j + 1])
                            op.then_inc(exp_ready, 1)
                        evac(act, G + 9 + hp, s, gates[:, bass.ds(4 * hp + s, 1), :].rearrange("p a n -> p (a n)"), ACT.Tanh, 0.5)
                        if s == 2:
                            act.wait_ge(softT_done, 6 * l + hp + 1)
                            for j in range(2):
                                op = nc.scalar.activation(softT[:, j, 0:384], free_ps[2 + j][:, 0:384], ACT.Copy)
                            op.then_inc(softT_ready, 1)
                with act.Fori(0, 2) as mp:
                    for s in range(SLOTS):
                        ahead(split_hi, act, G + 13 + mp, s)
                        if s == 0:
                            act.wait_ge(max_ready, 6 * l + 4 + mp + 1)
                            for j in range(2):
                                for t in range(2):
                                    c = slice(t * S, (t + 1) * S)
                                    op = nc.scalar.activation(soft[:, j, c], free_ps[j][:, c], ACT.Exp,
                                                              bias=stat[:, 0, 2 * j + t:2 * j + t + 1], scale=MEM_SCALE,
                                                              accum_out=stat[:, 1, 2 * j + t:2 * j + t + 1])
                            op.then_inc(exp_ready, 1)
                        evac(act, G + 13 + mp, s, gates[:, bass.ds(16 + 4 * mp + s, 1), :].rearrange("p a n -> p (a n)"), ACT.Tanh, 0.5)
                        if s == 2:
                            act.wait_ge(softT_done, 6 * l + 4 + mp + 1)
                            for j in range(2):
                                op = nc.scalar.activation(softT[:, j, :], free_ps[2 + j][:, :], ACT.Copy)
                            op.then_inc(softT_ready, 1)
                with act.Fori(0, 3) as br:
                    for s in range(SLOTS):
                        ahead(split_hi, act, G + 15 + br, s)
                act.wait_ge(blk_done, SLOTS + 4 * (G + 18))
                for half in range(2):
                    act.wait_ge(part_used, 12 * l + 12 - 2 + 2 * half + 2)
                    ks = slice(4 * half, 4 * half + 4)
                    nc.scalar.activation(hS_hi[:, ks, :], merged[:, ks, :], ACT.Copy, scale=0.5).then_inc(mhi_ready, 1)
                with act.Fori(0, 2) as w:
                    for s in range(SLOTS):
                        ahead(split_hi, act, G + 18 + w, s)
                        act.wait_ge(dve_evac, SLOTS + DVE_EVACS * l + 12 + 4 * w + s + 1)
                        act.wait_ge(mlo_ready, 2 * l + 2)
                        nc.scalar.activation(wideS[:, bass.ds(4 * w + s, 1), :], xS[:, bass.ds(4 * w + s, 1), :],
                                             ACT.Square).then_inc(sq_ready, 1)
            rstd_of(act, 1 + LAYERS, S)
            act.wait_ge(n32_ready, 2 * LAYERS + 1)
            for k in range(KT):
                if k == 4:
                    act.wait_ge(n32_ready, 2 * LAYERS + 2)
                    act.dma_start(cst2[:, :], a["cst2"]).then_inc(c2_in, 16)
                    act.dma_start(wba[:, :, :], a["wba"]).then_inc(wba_in, 16)
                    act.dma_start(adt[:, :], a["adt"]).then_inc(wba_in, 16)
                nc.scalar.activation(wide[:, k, :], xT[:, k, :], ACT.Square).then_inc(sq_ready, 1)
            rstd_of(act, 2 + LAYERS, T)

            def split_norm_hi(at):
                for half in range(2):
                    act.wait_ge(n32_ready, at + half + 1)
                    ks = slice(4 * half, 4 * half + 4)
                    nc.scalar.activation(h_hi[:, ks, :], h32t[:, ks, :], ACT.Copy).then_inc(nhi_ready, 1)

            split_norm_hi(2 * LAYERS + 2)
            act.wait_ge(wba_in, 32)
            nc.scalar.activation(ea[:, :], adt[:, 0:DN], ACT.Exp)
            act.wait_ge(ba_done, 1)
            ba = free_ps[1][:, 0:STEPS * 2 * DN].rearrange("p (t n) -> p t n", t=STEPS)
            nc.scalar.activation(beta_t[:, :, :], ba[:, :, 0:DN], ACT.Tanh, scale=0.5).then_inc(th_ready, 1)
            act.wait_ge(u_ready, 1)
            nc.scalar.activation(sp[:, :, :], sp[:, :, :], ACT.Exp)
            nc.scalar.drain()
            nc.scalar.activation(sp[:, :, :], sp[:, :, :], ACT.Ln, bias=ones[:, 0:1]).then_inc(ewu_ready, 1)
            act.wait_ge(gsum_done, 1)
            nc.scalar.activation(gcol[:, :], free_ps[2][:, 0:STEPS * DN], ACT.Copy)
            nc.scalar.activation(exg[:, :, :, :], free_ps[2][:, 0:5 * STEPS * DN].rearrange("p (i t h) -> p i t h", i=5, t=STEPS),
                                 ACT.Exp).then_inc(gsum_ready, 1)
            act.wait_ge(e_ready, 1)
            nc.scalar.activation(decay[:, :, :], decay[:, :, :], ACT.Exp).then_inc(expe_ready, 1)
            with act.Fori(0, 3) as i:
                for n in range(KT):
                    ahead(split_hi, act, G2 + 2 * i + n // SLOTS, n % SLOTS)
                    s = n % SLOTS
                    act.wait_ge(blk_done, SLOTS + 4 * G2 + 8 * i + n + 1)
                    if n >= SLOTS:
                        act.wait_ge(conv_done, 8 * i + n - SLOTS + 1)
                    nc.scalar.activation(st_raw[:, s, 2:T + 2], stream_ps[s][:, 0:T], ACT.Copy)
                    nc.scalar.activation(qkvT[:, bass.ds(i, 1), n, PADS:].rearrange("p a n -> p (a n)"), stream_ps[s][:, 0:T], ACT.Copy,
                                         scale=gains[:, bass.ds(G_CONV + 40 * i + 5 * n + 2, 1)]).then_inc(act_evac, 1)
                act.wait_ge(conv_done, 8 * i + 8)
                act.sem_inc(held, 1)
                qkv = qkvT[:, bass.ds(i, 1), :, PADS:].rearrange("p a h n -> p (a h) n")
                nc.scalar.activation(qkv, qkv, ACT.Silu).then_inc(silu_ready, 1)
            for n in range(4):
                sq, hs = (wide, k_sq)[n // 2], slice(4 * (n % 2), 4 * (n % 2) + 4)
                act.wait_ge(l2_done, n + 1)
                for j in range(4):
                    op = nc.scalar.activation(sq[:, hs.start + j, :], free_ps[j][:, 0:T], ACT.Ln, bias=eps_col[:, 0:1])
                op.then_inc(l2_used, 1)
                nc.scalar.drain()
                nc.scalar.activation(sq[:, hs, :], sq[:, hs, :], ACT.Exp, scale=-0.5).then_inc(l2rs_ready, 1)
            act.sem_inc(vnew_ready, 2)
            act.sem_inc(vk_used, 1)
            with act.Fori(0, STEPS) as t:
                for half in range(2):
                    b = bank[half]
                    act.wait_ge(vk_done, 2 * t + half + 1)
                    act.wait_ge(su_done, 2 * t + half + 1)
                    for j in range(4):
                        h = 4 * half + j
                        nc.scalar.activation(vb[:, h, :], b[1][:, j * P:(j + 1) * P], ACT.Copy, scale=sc[:, h:h + 1])
                        op = nc.scalar.activation(kdec[:, h, :], b[2][:, j * P:(j + 1) * P], ACT.Copy, scale=sc[:, 3 * DN + h:3 * DN + h + 1])
                    op.then_inc(vk_used, 1)
                for level in range(1, LEVELS):
                    for half in range(2):
                        act.wait_ge(n1_done, 12 * t + 2 * level + half + 1)
                        nc.scalar.activation(n1[:, half, :, :], bank[half][1][:, 0:4 * C].rearrange("p (h c) -> p h c", h=4),
                                             ACT.Copy).then_inc(n1_ready, 1)
                for half in range(2):
                    hs = slice(4 * half, 4 * half + 4)
                    act.wait_ge(vnew_done, 2 * t + half + 1)
                    for d, rows in ((0, slice(0, C)), (1, slice(C, P))):
                        op = nc.scalar.activation(vo[rows, d, hs, :], bank[half][3][rows, :].rearrange("p (h n) -> p h n", h=4), ACT.Copy)
                    op.then_inc(vnew_ready, 1)
            act.wait_ge(s_ready, 2 + 2 * STEPS)
            act.wait_ge(o_used, 2 + 2 * STEPS)
            for i, (dst, func, scale) in enumerate(((sz, ACT.Silu, 1.0), (ga, ACT.Tanh, 0.5), (gb, ACT.Tanh, 0.5),
                                                    (cx[:, :, 1:T + 1], ACT.Copy, 1.0))):
                with act.Fori(0, 2) as w:
                    for s in range(SLOTS):
                        ahead(split_hi, act, G_Z + 2 * i + w, s)
                        evac(act, G_Z + 2 * i + w, s, dst[:, bass.ds(4 * w + s, 1), :].rearrange("p a n -> p (a n)"), func, scale)
                if i == 0:
                    for k in range(KT):
                        nc.scalar.activation(wide[:, k, :], oT[:, k, PADS:], ACT.Square).then_inc(osq_ready, 1)
                    for n in range(2):
                        act.wait_ge(oss_done, n + 1)
                        hs = slice(4 * n, 4 * n + 4)
                        for j in range(4):
                            op = nc.scalar.activation(wide[:, 4 * n + j, :], free_ps[j][:, 0:T], ACT.Ln, bias=eps_col[:, 0:1], scale=1.0 / P)
                        op.then_inc(oss_used, 1)
                        nc.scalar.drain()
                        nc.scalar.activation(wide[:, hs, :], wide[:, hs, :], ACT.Exp, scale=-0.5).then_inc(ors_ready, 1)
                if i == 1:
                    act.wait_ge(yd_ready, 1)
                    nc.scalar.activation(yd_hi[:, :, :], oT[:, :, PADS:], ACT.Copy).then_inc(ydhi_ready, 1)
            with act.Fori(0, 4) as w:
                for s in range(SLOTS):
                    ahead(split_hi, act, G_SCX + w, s)
            act.wait_ge(dve_evac, SLOTS + D2 + 16)
            nc.scalar.activation(ys_hi[:, :, :], cx[:, :, 1:T + 1], ACT.Copy).then_inc(yshi_ready, 1)
            with act.Fori(0, 4) as w:
                for s in range(SLOTS):
                    ahead(split_hi, act, G_BR + w, s)
            for half in range(2):
                act.wait_ge(dve_evac, SLOTS + D2 + 28 + 4 * half)
                ks = slice(4 * half, 4 * half + 4)
                nc.scalar.activation(h_hi[:, ks, :], wide[:, ks, :], ACT.Copy, scale=0.5).then_inc(mhi_ready, 1)

            def squares(G, D_at):
                with act.Fori(0, 2) as w:
                    for s in range(SLOTS):
                        ahead(split_hi, act, G + w, s)
                        act.wait_ge(dve_evac, SLOTS + D_at + 4 * w + s + 1)
                        act.wait_ge(mlo_ready, 2 * LAYERS + 2)
                        nc.scalar.activation(wide[:, bass.ds(4 * w + s, 1), :], xT[:, bass.ds(4 * w + s, 1), :],
                                             ACT.Square).then_inc(sq_ready, 1)

            squares(G_WO, D2 + 32)
            rstd_of(act, 3 + LAYERS, T)
            split_norm_hi(2 * LAYERS + 4)
            with act.Fori(0, FT // 2) as w:
                for s in range(SLOTS):
                    ahead(split_hi, act, G_GU + w, s)
                    if s % 2 == 0:
                        act.wait_ge(blk_done, SLOTS + 4 * (G_GU + w) + s + 1)
                        nc.scalar.activation(f_act[:, s // 2, :], stream_ps[s][:, 0:T], ACT.Silu).then_inc(fact_ready, 1)
                    else:
                        act.wait_ge(dve_evac, SLOTS + D2 + 40 + 4 * w + s + 1)
                        nc.scalar.activation(f_hi[:, bass.ds(2 * w + s // 2, 1), :].rearrange("p a n -> p (a n)"), f_val[:, s // 2, :],
                                             ACT.Copy).then_inc(fhi_ready, 1)
            with act.Fori(0, 2) as w:
                for n in range(12):
                    ahead(split_hi, act, G_DOWN + 3 * w + n // SLOTS, n % SLOTS)
                    if n % 3 == 2:
                        act.wait_ge(dve_evac, SLOTS + D2 + 84 + 4 * w + n // 3 + 1)
                        nc.scalar.activation(wide[:, bass.ds(4 * w + n // 3, 1), :], xT[:, bass.ds(4 * w + n // 3, 1), :],
                                             ACT.Square).then_inc(sq_ready, 1)
            rstd_of(act, 4 + LAYERS, T)
            for half in range(2):
                ks = slice(4 * half, 4 * half + 4)
                act.wait_ge(n32_ready, 2 * LAYERS + 6 + half + 1)
                act.dma_start(out[:, ks, :], h32t[:, ks, NM:]).then_inc(stored, 16)

        @block.vector
        def _(dve):
            dve.sem_inc(lo_ready, SLOTS)
            dve.sem_inc(dve_evac, SLOTS)
            dve.sem_inc(idx_used, 2)
            dve.sem_inc(pv_used, 1)
            dve.sem_inc(mixed_used, 1)
            dve.wait_ge(cst_in, 16)
            nc.vector.tensor_copy(ident_bf[:, :], ident).then_inc(ident_ready, 1)
            dve.wait_ge(gains_in, 16)
            for s in range(AHEAD):
                split_lo(dve, 0, s)
            dve.wait_ge(rstd_ready, 1)
            for l in range(LAYERS):
                for half in range(2):
                    if l:
                        dve.wait_ge(memlo_ready, half + 1)
                    scale_rows(dve, mem_f, mem_raw, gain_col(G_MEM, l), half, mem32_ready)
                for half in range(2):
                    dve.wait_ge(memhi_ready, 2 * l + half + 1)
                    ks = slice(4 * half, 4 * half + 4)
                    nc.vector.tensor_tensor(mem_lo[l][:, ks, :], mem_f[:, ks, :], mem_hi[l][:, ks, :].bitcast(F32),
                                            ALU.subtract).then_inc(memlo_ready, 1)
            for g in range(MEM_GROUPS):
                for s in range(SLOTS):
                    ahead(split_lo, dve, g, s)
            for h in range(HEADS):
                dve.wait_ge(flip_done, h + 1)
                nc.vector.tensor_copy(bias[:, h, :], free_ps[h % 4][:, 0:S]).then_inc(bias_ready, 1)
            dve.wait_ge(admit_in, 16)

            with dve.Fori(0, LAYERS) as l:
                G = G0 + LAYER_GROUPS * l
                dve.wait_ge(rstd_ready, 2 + l)
                for half in range(2):
                    scale_rows(dve, h32, xS, gain_col(G_NORM, l), half, n32_ready)
                for half in range(2):
                    dve.wait_ge(nhi_ready, 2 * l + half + 1)
                    ks = slice(4 * half, 4 * half + 4)
                    nc.vector.tensor_tensor(hS_lo[:, ks, :], h32[:, ks, :], hS_hi[:, ks, :].bitcast(F32),
                                            ALU.subtract).then_inc(nlo_ready, 1)
                for g in range(2):
                    for s in range(SLOTS):
                        ahead(split_lo, dve, G + g, s)
                dve.wait_ge(ikw_ready, l + 1)
                for g in range(2):
                    for s in range(SLOTS):
                        ahead(split_lo, dve, G + 2 + g, s)
                        h = 4 * g + s
                        nc.vector.drain()
                        dve.wait_ge(idx_relu, HEADS * l + h + 1)
                        for t, cols in ((0, slice(0, P)), (1, slice(P, 3 * P))):
                            op = nc.vector.scalar_tensor_tensor(
                                out=idx_s[:, cols], in0=idx_r[:, h % 2, cols], scalar=iw[:, t, h:h + 1],
                                in1=admit[:, cols] if h == 0 else idx_s[:, cols], op0=ALU.mult, op1=ALU.add)
                        op.then_inc(idx_used, 1)
                for g in range(3):
                    for s in range(SLOTS):
                        ahead(split_lo, dve, G + 4 + g, s)
                        i = 4 * g + s
                        if i < TOPK // 8:
                            src = idx_s if i == 0 else idx_w
                            nc.vector.drain()
                            for t, cols in ((0, slice(0, P)), (1, slice(P, 3 * P))):
                                nc.vector.max(top8[:, t, :], src[:, cols])
                            nc.vector.drain()
                            for t, cols in ((0, slice(0, P)), (1, slice(P, 3 * P))):
                                nc.vector.match_replace(idx_w[:, cols], top8[:, t, :], src[:, cols], TAKEN)
                        if i == TOPK // 8:
                            nc.vector.drain()
                            nc.vector.tensor_scalar(mask[:, :], idx_w, TAKEN / 2, NEG, ALU.is_gt, ALU.mult).then_inc(mask_ready, 1)
                for g in range(2):
                    for s in range(SLOTS):
                        ahead(split_lo, dve, G + 7 + g, s)

                def normalise(i, parts):
                    dve.wait_ge(exp_ready, i)
                    nc.vector.reciprocal(stat[:, 2, :], stat[:, 1, :])
                    nc.vector.drain()
                    for j, cols, c in parts:
                        op = nc.vector.tensor_scalar(soft[:, j, cols], soft[:, j, cols], stat[:, 2, c:c + 1], None, ALU.mult)
                    op.then_inc(prob_ready, 1)

                def split_y(src, dst_hi, dst_lo):
                    nc.vector.drain()
                    nc.vector.tensor_copy(dst_hi, src)
                    nc.vector.drain()
                    return nc.vector.tensor_tensor(dst_lo, src, dst_hi.bitcast(F32), ALU.subtract)

                with dve.Fori(0, 4) as hp:
                    for s in range(SLOTS):
                        ahead(split_lo, dve, G + 9 + hp, s)
                        if s == 0:
                            dve.wait_ge(logit_done, 6 * l + hp + 2)
                            for j in range(2):
                                head = bias[:, bass.ds(2 * hp + j, 1), :].rearrange("p a n -> p (a n)")
                                nc.vector.scalar_tensor_tensor(out=soft[:, j, 0:P], in0=free_ps[j][:, 0:P], scalar=ATTN_SCALE,
                                                               in1=head[:, P:2 * P], op0=ALU.mult, op1=ALU.add)
                                nc.vector.scalar_tensor_tensor(out=soft[:, j, P:3 * P], in0=free_ps[j][:, P:3 * P], scalar=ATTN_SCALE,
                                                               in1=head, op0=ALU.mult, op1=ALU.add)
                            nc.vector.drain()
                            nc.vector.tensor_reduce(stat[:, 3, 0:2], soft[:, :, 0:P], AX, ALU.max)
                            nc.vector.tensor_reduce(stat[:, 3, 2:4], soft[:, :, P:3 * P], AX, ALU.max)
                            nc.vector.drain()
                            nc.vector.tensor_scalar(stat[:, 0, :], stat[:, 3, :], -1.0, None, ALU.mult).then_inc(max_ready, 1)
                        if s == 1:
                            normalise(6 * l + hp + 1, [(j, c, 2 * t + j) for j in range(2)
                                                       for t, c in ((0, slice(0, P)), (1, slice(P, 3 * P)))])
                    dve.wait_ge(pv_done, 6 * l + hp + 2)
                    nc.vector.tensor_tensor(soft[:, 0, 0:S], free_ps[0][:, 0:S],
                                            az[:, bass.ds(hp, 1), :].rearrange("p a n -> p (a n)"), ALU.mult).then_inc(pv_used, 1)
                    split_y(soft[:, 0, 0:S], y_hi[:, 1, bass.ds(hp, 1), :].rearrange("p a n -> p (a n)"),
                            y_lo[:, 1, bass.ds(hp, 1), :].rearrange("p a n -> p (a n)")).then_inc(y_ready, 1)
                    nc.vector.drain()
                dve.wait_ge(mixed_done, l + 1)
                for i in range(2):
                    for j in range(2):
                        g = 2 * i + j
                        nc.vector.scalar_tensor_tensor(out=soft[:, i, j * S:(j + 1) * S], in0=free_ps[2 + i][:, j * S:(j + 1) * S],
                                                       scalar=gains[:, bass.ds(G_POOL + POOLG * l + g, 1)], in1=pz[:, g, :],
                                                       op0=ALU.mult, op1=ALU.mult)
                op = split_y(soft[:, :, :].rearrange("p i (j n) -> p (i j) n", j=2), y_hi[:, 0, :, :], y_lo[:, 0, :, :])
                op.then_inc(mixed_used, 1)
                nc.vector.drain()
                with dve.Fori(0, 2) as mp:
                    for s in range(SLOTS):
                        ahead(split_lo, dve, G + 13 + mp, s)
                        if s == 0:
                            dve.wait_ge(logit_done, 6 * l + 4 + mp + 2)
                            for j in range(2):
                                nc.vector.tensor_reduce(stat[:, 3, 2 * j:2 * j + 2], free_ps[j][:, :].rearrange("p (t n) -> p t n", t=2),
                                                        AX, ALU.max)
                            nc.vector.drain()
                            nc.vector.tensor_scalar(stat[:, 0, :], stat[:, 3, :], -MEM_SCALE, None, ALU.mult).then_inc(max_ready, 1)
                        if s == 1:
                            normalise(6 * l + 4 + mp + 1, [(j, slice(t * S, (t + 1) * S), 2 * j + t) for j in range(2) for t in range(2)])
                    dve.wait_ge(pv_done, 6 * l + 4 + mp + 2)
                    nc.vector.tensor_tensor(soft[:, 0, :].rearrange("p (h n) -> p h n", h=2),
                                            free_ps[0][:, :].rearrange("p (h n) -> p h n", h=2),
                                            mz[:, bass.ds(2 * mp, 2), :], ALU.mult).then_inc(pv_used, 1)
                    split_y(soft[:, 0, :].rearrange("p (h n) -> p h n", h=2), y_hi[:, 2, bass.ds(2 * mp, 2), :],
                            y_lo[:, 2, bass.ds(2 * mp, 2), :]).then_inc(y_ready, 1)
                    nc.vector.drain()
                with dve.Fori(0, 3) as br:
                    for s in range(SLOTS):
                        ahead(split_lo, dve, G + 15 + br, s)
                        dve.wait_ge(blk_done, SLOTS + 4 * (G + 15 + br) + s + 1)
                        dve.wait_ge(part_used, 12 * l + 4 * br + s + 1)
                        nc.vector.scalar_tensor_tensor(out=soft[:, s % 2, :].rearrange("p (k n) -> p k n", k=2),
                                                       in0=gates[:, bass.ds(8 * br + 2 * s, 2), :], scalar=1.0,
                                                       in1=stream_ps[s][:, :].rearrange("p (k n) -> p k n", k=2),
                                                       op0=ALU.add, op1=ALU.mult).then_inc(dve_evac, 1)
                for half in range(2):
                    dve.wait_ge(mhi_ready, 2 * l + half + 1)
                    ks = slice(4 * half, 4 * half + 4)
                    nc.vector.scalar_tensor_tensor(out=hS_lo[:, ks, :], in0=merged[:, ks, :], scalar=0.5,
                                                   in1=hS_hi[:, ks, :].bitcast(F32), op0=ALU.mult, op1=ALU.subtract).then_inc(mlo_ready, 1)
                with dve.Fori(0, 2) as w:
                    for s in range(SLOTS):
                        ahead(split_lo, dve, G + 18 + w, s)
                        dve.wait_ge(blk_done, SLOTS + 4 * (G + 18 + w) + s + 1)
                        xt = xS[:, bass.ds(4 * w + s, 1), :].rearrange("p a n -> p (a n)")
                        nc.vector.tensor_tensor(xt, stream_ps[s][:, 0:S], xt, ALU.add).then_inc(dve_evac, 1)
            dve.wait_ge(rstd_ready, 2 + LAYERS)
            for half in range(2):
                scale_rows(dve, xS, xS, gain_col(G_FINAL), half, n32_ready)

            def split_norm(i, gain, at):
                dve.wait_ge(rstd_ready, i + 1)
                for half in range(2):
                    scale_rows(dve, h32t, xT, gain_col(gain), half, n32_ready)
                for half in range(2):
                    dve.wait_ge(nhi_ready, at + half + 1)
                    ks = slice(4 * half, 4 * half + 4)
                    nc.vector.tensor_tensor(h_lo[:, ks, :], h32t[:, ks, :], h_hi[:, ks, :].bitcast(F32),
                                            ALU.subtract).then_inc(nlo_ready, 1)

            split_norm(2 + LAYERS, G_NORM1, 2 * LAYERS)
            dve.wait_ge(th_ready, 1)
            dve.wait_ge(wba_in, 32)
            ba = free_ps[1][:, 0:STEPS * 2 * DN].rearrange("p (t n) -> p t n", t=STEPS)
            nc.vector.tensor_tensor(dt_u[:, :, :], ba[:, :, DN:], adt[:, DN:].unsqueeze(1).broadcast_to([P, STEPS, DN]), ALU.add)
            nc.vector.drain()
            nc.vector.scalar_tensor_tensor(out=sp[:, :, :], in0=dt_u[:, :, :], scalar=-1.0, in1=dt_u[:, :, :], op0=ALU.mult,
                                           op1=ALU.min).then_inc(u_ready, 1)
            nc.vector.tensor_scalar(beta_t[:, :, :], beta_t[:, :, :], 1.0, 0.5, ALU.add, ALU.mult)
            nc.vector.drain()
            dve.wait_ge(ewu_ready, 1)
            nc.vector.scalar_tensor_tensor(out=sp[:, :, :], in0=dt_u[:, :, :], scalar=0.0, in1=sp[:, :, :], op0=ALU.max, op1=ALU.add)
            nc.vector.drain()
            nc.vector.scalar_tensor_tensor(out=log_decay[:, :, :], in0=sp[:, :, :], scalar=-1.0,
                                           in1=ea[:, :].unsqueeze(1).broadcast_to([P, STEPS, DN]),
                                           op0=ALU.mult, op1=ALU.mult).then_inc(g_ready, 1)
            nc.vector.drain()
            dve.wait_ge(c2_in, 16)
            flat_g = log_decay[:, :, :].rearrange("p t h -> p (t h)")
            nc.vector.tensor_tensor(decay[:, :, :], tri_c.unsqueeze(1).broadcast_to([P, STEPS * DN, C]),
                                    flat_g.unsqueeze(2).broadcast_to([P, STEPS * DN, C]), ALU.mult).then_inc(gd_ready, 1)
            dve.wait_ge(gsum_ready, 1)
            factor = lambda i, rows=slice(0, P): scal[rows, :, i * DN:(i + 1) * DN]
            f_rows, b_rows = slice(0, C), slice(C, P)
            nc.vector.tensor_copy(factor(0), beta_t[:, :, :])
            for i, own, other in ((1, f_rows, b_rows), (2, b_rows, f_rows)):
                nc.vector.scalar_tensor_tensor(out=factor(i, own), in0=beta_t[own, :, :], scalar=-1.0, in1=exg[own, 0, :, :],
                                               op0=ALU.mult, op1=ALU.mult)
                nc.vector.tensor_copy(factor(i, other), exg[other, 1, :, :])
            for i in range(3):
                op = nc.vector.tensor_copy(factor(3 + i), exg[:, 2 + i, :, :])
            op.then_inc(scal_ready, 1)
            for t in range(STEPS):
                steps = slice(t * DN, (t + 1) * DN)
                dve.wait_ge(e_done, t + 1)
                nc.vector.tensor_tensor(decay[:, steps, :], e_bank[t][:, :].rearrange("p (h c) -> p h c", h=DN),
                                        gcol[:, steps].unsqueeze(2).broadcast_to([P, DN, C]), ALU.subtract).then_inc(e_used, 1)
            nc.vector.drain()
            nc.vector.tensor_tensor(decay[:, :, :], decay[:, :, :], sigma.unsqueeze(1).broadcast_to([P, STEPS * DN, C]),
                                    ALU.mult).then_inc(e_ready, 1)
            dve.wait_ge(zeros_ready, 1)
            with dve.Fori(0, 3) as i:
                for n in range(KT):
                    ahead(split_lo, dve, G2 + 2 * i + n // SLOTS, n % SLOTS)
                    dve.wait_ge(act_evac, SLOTS + E2 + 8 * i + n + 1)
                    acc = qkvT[:, bass.ds(i, 1), n, PADS:].rearrange("p a n -> p (a n)")
                    for tap in (0, 1, 3, 4):
                        op = nc.vector.scalar_tensor_tensor(out=acc, in0=st_raw[:, n % SLOTS, tap:tap + T],
                                                            scalar=gains[:, bass.ds(G_CONV + 40 * i + 5 * n + tap, 1)],
                                                            in1=acc, op0=ALU.mult, op1=ALU.add)
                        if tap < 4:
                            nc.vector.drain()
                    op.then_inc(conv_done, 1)
            for n in range(4):
                i, hs = n // 2, slice(4 * (n % 2), 4 * (n % 2) + 4)
                x = qkvT[:, i, hs, PADS:]
                dve.wait_ge(l2rs_ready, n + 1)
                nc.vector.scalar_tensor_tensor(out=x, in0=x, scalar=DN_SCALE if i == 0 else 1.0, in1=(wide, k_sq)[i][:, hs, :],
                                               op0=ALU.mult, op1=ALU.mult).then_inc(l2_ready, 1)
            nc.vector.memset(oT[:, :, :], 0.0)
            dve.sem_inc(o_used, 2)
            dve.sem_inc(r_ready, 1)
            dve.sem_inc(s_ready, 2)
            dve.wait_ge(decay_ready, 1)
            with dve.Fori(0, STEPS) as t:
                for half in range(2):
                    hs = slice(4 * half, 4 * half + 4)
                    kkq = bank[half][0][:, :].rearrange("p (h i c) -> p h i c", h=4, i=2)
                    dec = decay[:, bass.ds(DN * t + 4 * half, 4), :]
                    dve.wait_ge(kkq_done, 2 * t + half + 1)
                    nc.vector.tensor_tensor(lvl[:, LEVELS - 1, hs, :], kkq[:, :, 0, :], dec, ALU.mult)
                    for d, rows in ((0, f_rows), (1, b_rows)):
                        op = nc.vector.tensor_tensor(at[rows, d, hs, :], kkq[rows, :, 1, :], decay[rows, bass.ds(DN * t + 4 * half, 4), :], ALU.mult)
                    op.then_inc(kkq_used, 1)
                for half in range(2):
                    hs = slice(4 * half, 4 * half + 4)
                    dve.wait_ge(ks_done, 2 * t + half + 1)
                    for d in range(2):
                        c = (1 + d) * DN + 4 * half
                        nc.vector.tensor_tensor(vo[:, d, hs, :], bank[half][3 - 3 * d][:, :].rearrange("p (h n) -> p h n", h=4),
                                                sc[:, c:c + 4].unsqueeze(2).broadcast_to([P, 4, P]), ALU.mult)
                    nc.vector.drain()
                    dve.wait_ge(vk_used, 2 * t + half + 2)
                    for d, rows in ((0, f_rows), (1, b_rows)):
                        op = nc.vector.tensor_tensor(vb[rows, hs, :], vb[rows, hs, :], vo[rows, d, hs, :], ALU.add)
                    op.then_inc(r_ready, 1)
                eye4 = eye_c.unsqueeze(1).broadcast_to([P, 4, C])
                for half in range(2):
                    dve.wait_ge(n1_done, 12 * t + half + 1)
                    nc.vector.tensor_tensor(xy[:, half, 0, :, :], eye4, bank[half][1][:, 0:4 * C].rearrange("p (h c) -> p h c", h=4), ALU.subtract)
                    nc.vector.tensor_tensor(xy[:, half, 1, :, :], eye4, lvl[:, 0, 4 * half:4 * half + 4, :], ALU.subtract).then_inc(yx_ready, 1)
                for level in range(1, LEVELS):
                    sides = 2 if level < LEVELS - 1 else 1
                    for half in range(2):
                        dve.wait_ge(yx_done, 10 * t + 2 * (level - 1) + half + 1)
                        part = xy[:, half, 0:sides, :, :].rearrange("p i h c -> p (i h c)")
                        nc.vector.tensor_tensor(part, part, bank[half][2][:, 0:sides * 4 * C], ALU.subtract).then_inc(yx_ready, 1)
                for half in range(2):
                    hs = slice(4 * half, 4 * half + 4)
                    dve.wait_ge(o_done, 2 * t + half + 1)
                    for d, at_tok in ((0, C * t), (1, C * (STEPS - 1) - C * t)):
                        o = oT[:, hs, bass.ds(at_tok, C)]
                        op = nc.vector.tensor_tensor(o, o, bank[half][0][:, d * 4 * C:(d + 1) * 4 * C].rearrange("p (h c) -> p h c", h=4), ALU.add)
                        if d == 0:
                            nc.vector.drain()
                    op.then_inc(o_used, 1)
                for half in range(2):
                    hs = slice(4 * half, 4 * half + 4)
                    dve.wait_ge(su_done, 2 + 2 * t + half + 1)
                    dve.wait_ge(sdec_ready, 2 * t + half + 1)
                    for d in range(2):
                        op = nc.vector.tensor_tensor(state[:, d, hs, :], state[:, d, hs, :],
                                                     bank[half][1 + d][:, :].rearrange("p (h n) -> p h n", h=4), ALU.add)
                    op.then_inc(s_ready, 1)
            with dve.Fori(0, 2) as w:
                for s in range(SLOTS):
                    ahead(split_lo, dve, G_Z + w, s)
            dve.wait_ge(act_evac, SLOTS + E2 + 32)
            for n in range(2):
                dve.wait_ge(ors_ready, n + 1)
                o, hs = oT[:, 4 * n:4 * n + 4, PADS:], slice(4 * n, 4 * n + 4)
                nc.vector.scalar_tensor_tensor(out=o, in0=o, scalar=gains[:, G_DN:G_DN + 1], in1=wide[:, hs, :], op0=ALU.mult, op1=ALU.mult)
                nc.vector.drain()
                op = nc.vector.tensor_tensor(o, o, sz[:, hs, :], ALU.mult)
            op.then_inc(yd_ready, 1)
            for i in range(3):
                with dve.Fori(0, 2) as w:
                    for s in range(SLOTS):
                        ahead(split_lo, dve, G_Z + 2 + 2 * i + w, s)
                if i == 1:
                    dve.wait_ge(ydhi_ready, 1)
                    nc.vector.tensor_tensor(yd_lo[:, :, :], oT[:, :, PADS:], yd_hi[:, :, :].bitcast(F32), ALU.subtract).then_inc(ydlo_ready, 1)
            nc.vector.memset(cx[:, :, 0:1], 0.0)
            nc.vector.memset(cx[:, :, T + 1:], 0.0)
            with dve.Fori(0, 2) as w:
                for s in range(SLOTS):
                    ahead(split_lo, dve, G_SCX + w, s)
                    dve.wait_ge(blk_done, SLOTS + 4 * (G_SCX + w) + s + 1)
                    dve.wait_ge(act_evac, SLOTS + E2 + 56)
                    x = cx[:, bass.ds(4 * w + s, 1), 1:T + 1].rearrange("p a n -> p (a n)")
                    nc.vector.tensor_tensor(x, stream_ps[s][:, 0:T], x, ALU.mult).then_inc(dve_evac, 1)
            nc.vector.drain()
            with dve.Fori(0, 2) as w:
                for s in range(SLOTS):
                    ahead(split_lo, dve, G_SCX + 2 + w, s)
                    k = 4 * w + s
                    x = lambda at: cx[:, bass.ds(k, 1), at:at + T].rearrange("p a n -> p (a n)")
                    acc = bcv[:, s % 2, :]
                    nc.vector.tensor_scalar(acc, x(0), gains[:, bass.ds(G_SC + 3 * k, 1)], None, ALU.mult)
                    for tap in (1, 2):
                        nc.vector.drain()
                        nc.vector.scalar_tensor_tensor(out=acc, in0=x(tap), scalar=gains[:, bass.ds(G_SC + 3 * k + tap, 1)], in1=acc,
                                                       op0=ALU.mult, op1=ALU.add)
                    nc.vector.drain()
                    dve.wait_ge(blk_done, SLOTS + 4 * (G_SCX + 2 + w) + s + 1)
                    nc.vector.tensor_tensor(x(1), stream_ps[s][:, 0:T], acc, ALU.mult).then_inc(dve_evac, 1)
            dve.wait_ge(yshi_ready, 1)
            nc.vector.tensor_tensor(ys_lo[:, :, :], cx[:, :, 1:T + 1], ys_hi[:, :, :].bitcast(F32), ALU.subtract).then_inc(yslo_ready, 1)
            with dve.Fori(0, 2) as w:
                for s in range(SLOTS):
                    ahead(split_lo, dve, G_BR + w, s)
                    k = bass.ds(4 * w + s, 1)
                    dve.wait_ge(blk_done, SLOTS + 4 * (G_BR + w) + s + 1)
                    nc.vector.scalar_tensor_tensor(out=wide[:, k, :].rearrange("p a n -> p (a n)"), in0=ga[:, k, :].rearrange("p a n -> p (a n)"),
                                                   scalar=1.0, in1=stream_ps[s][:, 0:T], op0=ALU.add, op1=ALU.mult).then_inc(dve_evac, 1)
            with dve.Fori(0, 2) as w:
                for s in range(SLOTS):
                    ahead(split_lo, dve, G_BR + 2 + w, s)
                    k = bass.ds(4 * w + s, 1)
                    part, merge = (x[:, k, :].rearrange("p a n -> p (a n)") for x in (gb, wide))
                    dve.wait_ge(blk_done, SLOTS + 4 * (G_BR + 2 + w) + s + 1)
                    nc.vector.scalar_tensor_tensor(out=part, in0=part, scalar=1.0, in1=stream_ps[s][:, 0:T], op0=ALU.add, op1=ALU.mult)
                    nc.vector.drain()
                    nc.vector.tensor_tensor(merge, merge, part, ALU.add).then_inc(dve_evac, 1)
            for half in range(2):
                dve.wait_ge(mhi_ready, 2 * LAYERS + half + 1)
                ks = slice(4 * half, 4 * half + 4)
                nc.vector.scalar_tensor_tensor(out=h_lo[:, ks, :], in0=wide[:, ks, :], scalar=0.5, in1=h_hi[:, ks, :].bitcast(F32),
                                               op0=ALU.mult, op1=ALU.subtract).then_inc(mlo_ready, 1)
            with dve.Fori(0, 2) as w:
                for s in range(SLOTS):
                    ahead(split_lo, dve, G_WO + w, s)
                    dve.wait_ge(blk_done, SLOTS + 4 * (G_WO + w) + s + 1)
                    xt = xT[:, bass.ds(4 * w + s, 1), :].rearrange("p a n -> p (a n)")
                    nc.vector.tensor_tensor(xt, stream_ps[s][:, 0:T], xt, ALU.add).then_inc(dve_evac, 1)
            split_norm(3 + LAYERS, G_NORM2, 2 * LAYERS + 2)
            with dve.Fori(0, FT // 2) as w:
                for s in range(SLOTS):
                    ahead(split_lo, dve, G_GU + w, s)
                    if s % 2 == 1:
                        f = bass.ds(2 * w + s // 2, 1)
                        dve.wait_ge(blk_done, SLOTS + 4 * (G_GU + w) + s + 1)
                        dve.wait_ge(fact_ready, 2 * w + s // 2 + 1)
                        nc.vector.tensor_tensor(f_val[:, s // 2, :], stream_ps[s][:, 0:T], f_act[:, s // 2, :], ALU.mult).then_inc(dve_evac, 2)
                        dve.wait_ge(fhi_ready, 2 * w + s // 2 + 1)
                        nc.vector.tensor_tensor(f_lo[:, f, :].rearrange("p a n -> p (a n)"), f_val[:, s // 2, :],
                                                f_hi[:, f, :].rearrange("p a n -> p (a n)").bitcast(F32), ALU.subtract).then_inc(flo_ready, 1)
            with dve.Fori(0, 2) as w:
                for n in range(12):
                    ahead(split_lo, dve, G_DOWN + 3 * w + n // SLOTS, n % SLOTS)
                    if n % 3 == 2:
                        dve.wait_ge(blk_done, SLOTS + 4 * G_DOWN + 12 * w + n + 1)
                        xt = xT[:, bass.ds(4 * w + n // 3, 1), :].rearrange("p a n -> p (a n)")
                        nc.vector.tensor_tensor(xt, stream_ps[n // 3][:, 0:T], xt, ALU.add).then_inc(dve_evac, 1)
            dve.wait_ge(rstd_ready, 5 + LAYERS)
            for half in range(2):
                scale_rows(dve, h32t, xT, gain_col(G_FINAL2), half, n32_ready)

        @block.tensor
        def _(pe):
            pe.sem_inc(blk_done, SLOTS)
            pe.sem_inc(logit_done, 1)
            pe.sem_inc(pv_done, 1)
            pe.wait_ge(cst_in, 16)
            sum_squares(pe, mem_f, 0, 0)
            pe.wait_ge(rel_in, 32)
            nc.tensor.matmul(free_ps[1][0:HEADS, :], rel_sb[:, :], bucket_hot, start=True, stop=True).then_inc(relf_done, 1)
            for l in range(LAYERS):
                pe.wait_ge(memlo_ready, 2 * l + 2)
                for s in range(SLOTS):
                    block_cols(pe, 2 * l, s, act_evac, 8 * l + s + 1, mem_hi[l], mem_lo[l])
                for s in range(SLOTS):
                    block_rows(pe, 2 * l + 1, s, act_evac, 8 * l + 4 + s + 1, mem_hi[l], mem_lo[l])
            pe.wait_ge(hankel_in, 16)
            pe.wait_ge(relf_ready, 1)
            pe.wait_ge(rstd_ready, 1)
            for h in range(HEADS):
                if h >= 4:
                    pe.wait_ge(bias_ready, h - 3)
                nc.tensor.matmul(free_ps[h % 4][:, 0:S], flip, hankel[:, h, :], start=True, stop=True).then_inc(flip_done, 1)
            pe.wait_ge(bias_ready, HEADS)
            pe.wait_ge(ident_ready, 1)

            with pe.Fori(0, LAYERS) as l:
                G = G0 + LAYER_GROUPS * l
                E = 4 * MEM_GROUPS + ACT_EVACS * l
                pe.wait_ge(pv_used, 6 * l + 1)
                sum_squares(pe, wideS, 1 + l, 8 + 8 * l)
                pe.wait_ge(nlo_ready, 2 * l + 2)
                pe.wait_ge(dve_evac, SLOTS + DVE_EVACS * l)
                for s in range(SLOTS):
                    block_cols(pe, G, s, act_evac, E + s + 1, hS_hi, hS_lo)
                pe.wait_ge(wik_in, 16 * (l + 1))
                for k in range(KT):
                    nc.tensor.matmul(free_ps[1][:, 0:S], wik[:, k, 0:P], h32[:, k, :], start=k == 0, stop=k == KT - 1)
                for t in range(2):
                    for k in range(KT):
                        mm = nc.tensor.matmul(free_ps[2][:, t * HEADS:(t + 1) * HEADS], h32[:, k, t * P:(t + 1) * P],
                                              wik[:, k, P:P + HEADS], start=k == 0, stop=k == KT - 1)
                mm.then_inc(ikw_done, 1)
                for s in range(SLOTS):
                    block_cols(pe, G + 1, s, act_evac, E + 4 + s + 1, hS_hi, hS_lo)

                def index_products(h):
                    rows, q = slice(HD * (h % 2), HD * (h % 2) + HD), iqT[:, h // 2, :]
                    nc.tensor.matmul(free_ps[h % 4][:, 0:P], q[rows, 0:P], ikT[rows, 0:P], start=True, stop=True)
                    nc.tensor.matmul(free_ps[h % 4][:, P:3 * P], q[rows, P:S], ikT[rows, :], start=True, stop=True).then_inc(idx_done, 1)

                pe.wait_ge(ikw_ready, l + 1)
                pe.wait_ge(act_evac, SLOTS + E + 4)
                for h in range(4):
                    index_products(h)
                for s in range(SLOTS):
                    block_cols(pe, G + 2, s, act_evac, E + 8 + s + 1, hS_hi, hS_lo)
                for h in range(4, HEADS):
                    pe.wait_ge(idx_relu, HEADS * l + h - 3)
                    index_products(h)
                for s in range(SLOTS):
                    block_rows(pe, G + 3, s, act_evac, E + 12 + s + 1, hS_hi, hS_lo)
                with pe.Fori(0, 5) as g:
                    for s in range(SLOTS):
                        block_cols(pe, G + 4 + g, s, act_evac, E + 16 + 4 * g + s + 1, hS_hi, hS_lo)
                with pe.Fori(0, 4) as hp:
                    pe.wait_ge(mask_ready, l + 1)
                    pe.wait_ge(idx_relu, HEADS * (l + 1))
                    pe.wait_ge(qk_staged, 6 * l + hp + 1)
                    pe.wait_ge(pv_used, 6 * l + hp + 1)
                    for j in range(2):
                        rows = slice(HD * j, HD * j + HD)
                        nc.tensor.matmul(free_ps[j][:, 0:P], st_q[rows, 0:P], st_k[rows, 0:P], start=True, stop=False)
                        nc.tensor.matmul(free_ps[j][:, 0:P], ident_bf[:, :], mask[:, 0:P], start=False, stop=True)
                        nc.tensor.matmul(free_ps[j][:, P:3 * P], st_q[rows, P:S], st_k[rows, :], start=True, stop=False)
                        mm = nc.tensor.matmul(free_ps[j][:, P:3 * P], ident_bf[:, :], mask[:, P:3 * P], start=False, stop=True)
                    mm.then_inc(logit_done, 1)
                    for s in range(SLOTS):
                        block_cols(pe, G + 9 + hp, s, act_evac, E + 36 + 4 * hp + s + 1, hS_hi, hS_lo)
                        if s == 2:
                            pe.wait_ge(prob_ready, 6 * l + hp + 1)
                            for j in range(2):
                                for c in range(3):
                                    mm = nc.tensor.transpose(free_ps[2 + j][:, c * P:(c + 1) * P], soft[:, j, c * P:(c + 1) * P], ident)
                            mm.then_inc(softT_done, 1)
                    pe.wait_ge(softT_ready, 6 * l + hp + 1)
                    pe.wait_ge(v_staged, 6 * l + hp + 1)
                    for j in range(2):
                        o, vc = free_ps[0][HD * j:HD * j + HD, :], slice(HD * j, HD * j + HD)
                        nc.tensor.matmul(o[:, 0:P], st_v[:, 0, vc], softT[:, j, 0:P], start=True, stop=True)
                        nc.tensor.matmul(o[:, P:S], st_v[:, 0, vc], softT[:, j, P:2 * P], start=True, stop=False)
                        mm = nc.tensor.matmul(o[:, P:S], st_v[:, 1, vc], softT[:, j, 2 * P:3 * P], start=False, stop=True)
                    mm.then_inc(pv_done, 1)
                pe.wait_ge(pooled_ready, l + 1)
                pe.wait_ge(poolw_in, 16 * (l + 1))
                for g in range(POOLG):
                    mm = nc.tensor.matmul(free_ps[2 + g // 2][:, (g % 2) * S:(g % 2 + 1) * S], pool_w[:, g, :], pu[:, g, PAD:],
                                          start=True, stop=True)
                mm.then_inc(mixed_done, 1)
                with pe.Fori(0, 2) as mp:
                    pe.wait_ge(qk_staged, 6 * l + 4 + mp + 1)
                    pe.wait_ge(pv_used, 6 * l + 4 + mp + 1)
                    for j in range(2):
                        for t in range(2):
                            mm = nc.tensor.matmul(free_ps[j][:, t * S:(t + 1) * S], st_mq[:, j, t * P:(t + 1) * P],
                                                  mkT[:, bass.ds(4 * l + 2 * mp + j, 1), :].rearrange("p a n -> p (a n)"), start=True, stop=True)
                    mm.then_inc(logit_done, 1)
                    for s in range(SLOTS):
                        block_cols(pe, G + 13 + mp, s, act_evac, E + 52 + 4 * mp + s + 1, hS_hi, hS_lo)
                        if s == 2:
                            pe.wait_ge(prob_ready, 6 * l + 4 + mp + 1)
                            pe.wait_ge(mixed_used, l + 2)
                            for j in range(2):
                                for c in range(4):
                                    mm = nc.tensor.transpose(free_ps[2 + j][:, c * P:(c + 1) * P], soft[:, j, c * P:(c + 1) * P], ident)
                            mm.then_inc(softT_done, 1)
                    pe.wait_ge(softT_ready, 6 * l + 4 + mp + 1)
                    pe.wait_ge(v_staged, 6 * l + 4 + mp + 1)
                    for j in range(2):
                        for t in range(2):
                            o = free_ps[0][:, j * S + t * P:j * S + (t + 1) * P]
                            for m in range(2):
                                mm = nc.tensor.matmul(o, st_mv[:, m, j * P:(j + 1) * P], softT[:, j, (2 * t + m) * P:(2 * t + m + 1) * P],
                                                      start=m == 0, stop=m == 1)
                    mm.then_inc(pv_done, 1)
                with pe.Fori(0, 3) as br:
                    pe.wait_ge(act_evac, SLOTS + E + ACT_EVACS)
                    pe.wait_ge(mixed_used, l + 2)
                    pe.wait_ge(y_ready, 6 * l + 6)
                    for s in range(SLOTS):
                        pe.wait_ge(lo_ready, 4 * (G + 15 + br) + s + 1 + SLOTS)
                        pe.wait_ge(dve_evac, DVE_EVACS * l + 4 * br + s + 1)
                        for c in range(2):
                            for k in range(4):
                                y = (y_hi[:, bass.ds(br, 1), k, :].rearrange("p a n -> p (a n)"),
                                     y_lo[:, bass.ds(br, 1), k, :].rearrange("p a n -> p (a n)"))
                                mm = mm3(stream_ps[s][:, c * S:(c + 1) * S], w_hi[s][:, 4 * c + k, :], w_lo[s][:, 4 * c + k, :],
                                         *y, k == 0, k == 3)
                        mm.then_inc(blk_done, 1)
                with pe.Fori(0, 2) as w:
                    pe.wait_ge(mlo_ready, 2 * l + 2)
                    for s in range(SLOTS):
                        block_cols(pe, G + 18 + w, s, dve_evac, DVE_EVACS * l + 12 + 4 * w + s + 1, hS_hi, hS_lo)
            sum_squares(pe, wideS, 1 + LAYERS, 8 + 8 * LAYERS)
            sum_squares(pe, wide, 2 + LAYERS, 16 + 8 * LAYERS)
            pe.wait_ge(n32_ready, 2 * LAYERS + 4)
            pe.wait_ge(zeros_ready, 1)
            pe.wait_ge(wba_in, 32)
            for t in range(STEPS):
                for d, chunk in ((0, t), (1, STEPS - 1 - t)):
                    for k in range(KT):
                        mm = nc.tensor.matmul(free_ps[1][d * C:(d + 1) * C, t * 2 * DN:(t + 1) * 2 * DN], h32p[:, k, chunk * C:(chunk + 1) * C],
                                              wba[:, k, d * 2 * DN:(d + 1) * 2 * DN], start=k == 0, stop=k == KT - 1)
            mm.then_inc(ba_done, 1)
            pe.wait_ge(g_ready, 1)
            pe.wait_ge(c2_in, 16)
            for i, m in enumerate((tri, tri_swap, after, rows_f, rows_b)):
                mm = nc.tensor.matmul(free_ps[2][:, i * STEPS * DN:(i + 1) * STEPS * DN], m,
                                      log_decay[:, :, :].rearrange("p t h -> p (t h)"), start=True, stop=True)
            mm.then_inc(gsum_done, 1)
            pe.wait_ge(gd_ready, 1)
            for t in range(STEPS):
                if t >= 3:
                    pe.wait_ge(e_used, t - 2)
                nc.tensor.matmul(e_bank[t][:, :], same, decay[:, t * DN:(t + 1) * DN, :], start=True, stop=True).then_inc(e_done, 1)
            pe.wait_ge(nlo_ready, 2 * LAYERS + 2)
            pe.wait_ge(dve_evac, SLOTS + D2)
            with pe.Fori(0, 6) as w:
                for s in range(SLOTS):
                    block_cols(pe, G2 + w, s, act_evac, E2 + 4 * w + s + 1, h_hi, h_lo)
            pe.wait_ge(e_used, STEPS)
            for n in range(4):
                pe.wait_ge(l2sq_ready, n + 1)
                if n:
                    pe.wait_ge(l2_used, n)
                for j in range(4):
                    mm = nc.tensor.matmul(free_ps[j][:, 0:T], ones, (wide, k_sq)[n // 2][:, 4 * (n % 2) + j, :], start=True, stop=True)
                mm.then_inc(l2_done, 1)
            pe.wait_ge(l2_used, 4)
            pe.wait_ge(act_evac, SLOTS + E2 + 24)
            pe.sem_inc(su_done, 2)
            with pe.Fori(0, STEPS) as t:
                f_rows, b_rows = slice(0, C), slice(C, P)
                dirs = ((0, f_rows), (1, b_rows))
                heads = [(j, slice(j * P, (j + 1) * P), slice(j * C, (j + 1) * C)) for j in range(4)]
                for half in range(2):
                    pe.wait_ge(dn_staged, t + 1)
                    pe.wait_ge(o_used, 2 * t + half + 1)
                    for j, wide_j, _ in heads:
                        for rows, keys, kq in ((f_rows, 4, 4), (b_rows, 1, 1)):
                            mm = nc.tensor.matmul(bank[half][0][rows, wide_j], kqs[:, 4 * half + j, keys, :],
                                                  kqs[:, 4 * half + j, kq:kq + 2, :].rearrange("p i c -> p (i c)"), start=True, stop=True)
                    mm.then_inc(kkq_done, 1)
                for half in range(2):
                    pe.wait_ge(s_ready, 2 * t + half + 1)
                    for j, wide_j, _ in heads:
                        h = 4 * half + j
                        nc.tensor.transpose(bank[half][1][:, wide_j], vs[:, h, :, :].rearrange("p i c -> p (i c)"), ident)
                        mm = nc.tensor.transpose(bank[half][2][:, wide_j], kqs[:, h, 0:2, :].rearrange("p i c -> p (i c)"), ident)
                    mm.then_inc(vk_done, 1)
                for half in range(2):
                    pe.wait_ge(vnew_ready, 2 * t + half + 1)
                    pe.wait_ge(kkq_used, 2 * t + half + 1)
                    for j, wide_j, _ in heads:
                        h = 4 * half + j
                        nc.tensor.matmul(bank[half][3][:, wide_j], kqs[:, h, 4:6, :].rearrange("p i c -> p (i c)"), state[:, 0, h, :], start=True, stop=True)
                        mm = nc.tensor.matmul(bank[half][0][:, wide_j], kqs[:, h, 2:4, :].rearrange("p i c -> p (i c)"), state[:, 1, h, :], start=True, stop=True)
                    mm.then_inc(ks_done, 1)
                for level in range(LEVELS):
                    sides = 2 if level < LEVELS - 1 else 1
                    for half in range(2):
                        pe.wait_ge(lvl_ready, 12 * t + 2 * level + half + 1)
                        if level == 0:
                            pe.wait_ge(vk_used, 2 * t + half + 2)
                        else:
                            pe.wait_ge(yx_ready, 12 * t + 2 * (level - 1) + half + 1)
                        pe.sem_inc(held, 1)
                        for j, _, c in heads:
                            for d, rows in dirs:
                                rhs = eye_c[rows, :] if level == 0 else xy[rows, half, 0, j, :]
                                mm = nc.tensor.matmul(bank[half][1][rows, c], lvl[rows, level, 4 * half + j, :], rhs, start=True, stop=True)
                        mm.then_inc(n1_done, 1)
                    for half in range(2 if level else 0):
                        pe.wait_ge(n1_ready, 10 * t + 2 * (level - 1) + half + 1)
                        pe.sem_inc(held, 1)
                        for j, _, c in heads:
                            for d, rows in dirs:
                                mm = nc.tensor.matmul(bank[half][2][rows, c], xy[rows, half, 1, j, :], n1[rows, half, j, :], start=True, stop=True)
                                if sides == 2:
                                    mm = nc.tensor.matmul(bank[half][2][rows, 4 * C + c.start:4 * C + c.stop], n1[rows, half, j, :],
                                                          xy[rows, half, 1, j, :], start=True, stop=True)
                        mm.then_inc(yx_done, 1)
                for half in range(2):
                    pe.wait_ge(yx_ready, 12 * t + 2 * (LEVELS - 1) + half + 1)
                    pe.wait_ge(r_ready, 2 * t + half + 2)
                    pe.sem_inc(held, 1)
                    for j, wide_j, _ in heads:
                        for d, rows in dirs:
                            mm = nc.tensor.matmul(bank[half][3][rows, wide_j], xy[rows, half, 0, j, :], vb[rows, 4 * half + j, :], start=True, stop=True)
                    mm.then_inc(vnew_done, 1)
                for half in range(2):
                    pe.wait_ge(vnew_ready, 2 + 2 * t + half + 1)
                    pe.wait_ge(at_ready, 2 * t + half + 1)
                    for j, _, c in heads:
                        for d, rows in dirs:
                            mm = nc.tensor.matmul(bank[half][0][:, d * 4 * C + c.start:d * 4 * C + c.stop], vo[:, d, 4 * half + j, :],
                                                  at[:, d, 4 * half + j, :], start=True, stop=True)
                    mm.then_inc(o_done, 1)
                for half in range(2):
                    for j, wide_j, _ in heads:
                        for d, rows in dirs:
                            mm = nc.tensor.matmul(bank[half][1 + d][:, wide_j], kdec[rows, 4 * half + j, :], vo[rows, d, 4 * half + j, :],
                                                  start=True, stop=True)
                    mm.then_inc(su_done, 1)
            pe.wait_ge(s_ready, 2 + 2 * STEPS)
            pe.wait_ge(o_used, 2 + 2 * STEPS)
            with pe.Fori(0, 2) as w:
                for s in range(SLOTS):
                    block_cols(pe, G_Z + w, s, act_evac, E2 + 24 + 4 * w + s + 1, h_hi, h_lo)
            for n in range(2):
                pe.wait_ge(osq_ready, 4 * n + 4)
                if n:
                    pe.wait_ge(oss_used, n)
                for j in range(4):
                    mm = nc.tensor.matmul(free_ps[j][:, 0:T], ones, wide[:, 4 * n + j, :], start=True, stop=True)
                mm.then_inc(oss_done, 1)
            with pe.Fori(0, 6) as w:
                for s in range(SLOTS):
                    block_cols(pe, G_Z + 2 + w, s, act_evac, E2 + 32 + 4 * w + s + 1, h_hi, h_lo)
            pe.wait_ge(act_evac, SLOTS + E2 + 56)
            with pe.Fori(0, 4) as w:
                for s in range(SLOTS):
                    block_cols(pe, G_SCX + w, s, dve_evac, D2 + 4 * w + s + 1, h_hi, h_lo)
            for i, (y_ok, hi, lo) in enumerate(((ydlo_ready, yd_hi, yd_lo), (yslo_ready, ys_hi, ys_lo))):
                pe.wait_ge(y_ok, 1)
                with pe.Fori(0, 2) as w:
                    for s in range(SLOTS):
                        block_cols(pe, G_BR + 2 * i + w, s, dve_evac, D2 + 16 + 8 * i + 4 * w + s + 1, hi, lo)
            pe.wait_ge(mlo_ready, 2 * LAYERS + 2)
            with pe.Fori(0, 2) as w:
                for s in range(SLOTS):
                    block_cols(pe, G_WO + w, s, dve_evac, D2 + 32 + 4 * w + s + 1, h_hi, h_lo)
            sum_squares(pe, wide, 3 + LAYERS, 24 + 8 * LAYERS)
            pe.wait_ge(nlo_ready, 2 * LAYERS + 4)
            with pe.Fori(0, FT // 2) as w:
                for s in range(SLOTS):
                    block_cols(pe, G_GU + w, s, dve_evac, D2 + 40 + 4 * w + s + 1, h_hi, h_lo)
            pe.wait_ge(flo_ready, FT)
            with pe.Fori(0, 2) as w:
                for n in range(12):
                    c, s = n // 3, n % SLOTS
                    pe.wait_ge(lo_ready, 4 * G_DOWN + 12 * w + n + 1 + SLOTS)
                    if n % 3 == 0:
                        pe.wait_ge(dve_evac, D2 + 84 + 4 * w + c + 1)
                    for k in range(min(KT, FT - KT * (n % 3))):
                        kf = KT * (n % 3) + k
                        mm = mm3(stream_ps[c][:, 0:T], w_hi[s][:, k, :], w_lo[s][:, k, :], f_hi[:, kf, :], f_lo[:, kf, :],
                                 kf == 0, kf == FT - 1)
                    mm.then_inc(blk_done, 1)
            sum_squares(pe, wide, 4 + LAYERS, 32 + 8 * LAYERS)


def rel_buckets():
    n = np.abs(np.arange(512) - 255)
    pos = np.arange(512) > 255
    large = 8 + (np.log(np.maximum(n, 1).astype(np.float32) / 8) / math.log(128) * 8).astype(np.int32)
    b = np.where(pos, 16, 0) + np.where(n < 8, n, np.minimum(large, 15))
    return (b[None, :] == np.arange(32)[:, None]).astype(np.float32)


def constants_first():
    cst = np.concatenate([np.eye(P), np.ones((P, P))], 1).astype(np.float32)
    rel = np.zeros((P, P + 512), np.float32)
    rel[:, 0:P] = np.eye(P)[::-1]
    rel[0:32, P:] = rel_buckets()
    q, s = np.arange(P)[:, None], np.arange(S)[None, :]
    admit = np.concatenate([np.where(s[:, 0:P] < (q // 64 + 1) * 64, 0.0, NEG),
                            np.where(s < ((q + P) // 64 + 1) * 64, 0.0, NEG)], 1)
    edge = [1.0 / np.minimum(np.arange(16) + 1, w) for w in POOL_WINDOWS]
    admit = np.concatenate([admit, np.broadcast_to(np.concatenate(edge), (P, POOLG * 16))], 1).astype(np.float32)
    return cst, rel, admit


def constants_second():
    r = np.arange(P)
    half, pos = r // C, np.where(r < C, r, P - 1 - r)
    same = half[:, None] == half[None, :]
    tri = same & (pos[:, None] <= pos[None, :])
    mats = [tri, np.roll(tri, C, 1), same & (pos[:, None] > pos[None, :]),
            np.broadcast_to(half[:, None] == 0, (P, P)), np.broadcast_to(half[:, None] == 1, (P, P)), same]
    pr = pos[:, None]
    pc = np.where(half[:, None] == 0, np.arange(C)[None, :], C - 1 - np.arange(C)[None, :])
    cols = [pr <= pc, np.where(pr > pc, -1, 1), pr > pc, pr <= pc, pr == pc]
    cols += [(pr // (2 * m) == pc // (2 * m)) & (pr // m % 2 == 1) & (pc // m % 2 == 0) for m in (1, 2, 4, 8, 16, 32)]
    cols += [(pr <= pc) | (half[:, None] != d) for d in range(2)]
    return np.concatenate(mats + cols, 1).astype(np.float32)


def tiles(w, cols):
    w = w[:, cols]
    return w.reshape(w.shape[0] // P, P, -1).transpose(1, 0, 2).reshape(P, -1)


def blocks(w, start, count):
    return [tiles(w, slice(start + P * j, start + P * (j + 1))) for j in range(count)]


def channels(v):
    return v.reshape(-1, P).T


def pack_stream(i):
    out = []
    for l in range(LAYERS):
        out += blocks(i["w_mem_kv"][l], 0, 8)
    for l in range(LAYERS):
        w = i["w_in"][l]
        u, z, q, k, v, az, iq, ik, iw, mq, mz, g = np.cumsum([0, 512, 512, 512, 512, 512, 512, 512, 64, 8, 512, 512])
        for start in (iq, q, k, v, az, z, mz, u, mq):
            out += blocks(w, start, 4)
        out += blocks(w, g, 24)
        for b in range(3):
            for d in range(4):
                pair = [tiles(i["w_branch"][l, b], slice(P * c, P * (c + 1))) for c in (2 * d, 2 * d + 1)]
                out.append(np.concatenate(pair, 1))
        out += blocks(i["w_out"][l], 0, 8)
    w = i["w_in_2"][0]
    q, k, v, z, b, a, scb, scc, scx, ga, gb = np.cumsum([0, D, D, D, D, 16, 16, D, D, D, D])
    for start in (q, k, v, z, ga, gb, scc, scx, scb):
        out += blocks(w, start, KT)
    for n in ("w_branch_dn_2", "w_branch_sc_2", "w_out_2"):
        out += blocks(i[n][0], 0, KT)
    w = i["w_gate_up_2"][0]
    for j in range(FT):
        out += blocks(w, P * j, 1) + blocks(w, P * (FT + j), 1)
    for j in range(KT):
        col = tiles(i["w_down_2"][0], slice(P * j, P * (j + 1)))
        col = np.concatenate([col, np.zeros((P, 3 * BLK - FT * P), np.float32)], 1)
        out += [col[:, BLK * c:BLK * (c + 1)] for c in range(3)]
    out += [np.zeros((P, BLK), np.float32)] * AHEAD
    return np.stack(out)


def kernel(**inputs):
    import concourse.bacc as bacc
    from concourse.bass_utils import run_bass_kernel_spmd

    i = {n: np.asarray(v) for n, v in inputs.items()}
    cst, rel, admit = constants_first()
    w_in = i["w_in"]
    ik = w_in[:, :, 3584:3656]
    wik = np.concatenate([ik[:, :, 0:64], ik[:, :, 0:64], ik[:, :, 64:72]], 2)
    gains = [channels(i["norm_g"].reshape(-1)), channels(i["mem_norm_g"].reshape(-1)), channels(i["pool_scale"].reshape(-1)),
             channels(i["final_g"]), channels(i["norm1_w_2"][0]), channels(i["norm2_w_2"][0]), channels(i["final_norm_w_2"]),
             channels(i["dn_norm_w_2"][0]),
             i["dn_conv_w_2"][0].reshape(5, 24, P).transpose(2, 1, 0).reshape(P, -1),
             i["sc_conv_w_2"][0].reshape(3, 8, P).transpose(2, 1, 0).reshape(P, -1)]
    ba = i["w_in_2"][0][:, 4 * D:4 * D + 4 * DN].reshape(D, 2, 2, DN)
    wba = ba.transpose(0, 2, 1, 3)
    tokens = np.concatenate([i["meta_tokens_2"], i["x"][0]], 0)
    arrays = {
        "stream": pack_stream(i),
        "xT": tokens.T.reshape(KT, P, T).transpose(1, 0, 2),
        "memT": i["mem"][0].T.reshape(KT, P, S).transpose(1, 0, 2),
        "gains": np.concatenate(gains, 1),
        "cst": cst, "rel_cst": rel, "admit": admit,
        "rel_bias": i["rel_bias"],
        "wik": wik.reshape(LAYERS, KT, P, 136).transpose(0, 2, 1, 3),
        "pool_w": i["pool_w"].transpose(0, 2, 1, 3),
        "cst2": constants_second(),
        "wba": wba.reshape(KT, P, 4 * DN).transpose(1, 0, 2),
        "adt": np.repeat(np.concatenate([i["A_log_2"][0], i["dt_bias_2"][0]], 1), C, 0),
    }
    nc = bacc.Bacc("TRN2", target_bir_lowering=False, num_devices=1)
    arrays = {f"{n}_dram": np.ascontiguousarray(v) for n, v in arrays.items()}
    a = {n[:-5]: nc.dram_tensor(n, v.shape, F32, kind="ExternalInput").ap() for n, v in arrays.items()}
    a["rel_scratch"] = nc.dram_tensor("rel_scratch", (HEADS, 512), F32, kind="Internal").ap()
    a["groups"] = (arrays["stream_dram"].shape[0] - AHEAD) // SLOTS
    out = nc.dram_tensor("out", (P, KT, S), F32, kind="ExternalOutput").ap()
    build(nc, a, out)
    r = run_bass_kernel_spmd(nc, [arrays], core_ids=[0])
    return np.ascontiguousarray(r.results[0]["out"].transpose(2, 1, 0).reshape(1, S, D))
```

```python
import math
from contextlib import ExitStack

import numpy as np

import concourse.bass as bass
from concourse import mybir
from concourse.alu_op_type import AluOpType as ALU

ACT = mybir.ActivationFunctionType
AX = mybir.AxisListType.X
F32 = mybir.dt.float32
F32R = mybir.dt.float32r
BF16 = mybir.dt.bfloat16

P = 128
D = 1024
KT = D // P
S = 256
NM = 16
T = NM + S
LAYERS = 2
HEADS, HD = 8, 64
TOPK = 64
MHEADS = 4
POOLG = 4
POOL_WINDOWS = (2, 4, 8, 16)
PAD = 8
ATTN_SCALE = HD ** -0.5
IDX_W_SCALE = (HD ** -0.5) * (HEADS ** -0.5)
MEM_SCALE = P ** -0.5
EPS = 1e-6
NEG = -1e30
TAKEN = -3e38
SLOTS = 4
BLK = KT * P
AHEAD = 2
MEM_GROUPS = 4
LAYER_GROUPS = 20
ACT_EVACS = 60
DVE_EVACS = 20
G_NORM, G_MEM, G_POOL, G_FINAL = 0, 16, 32, 40
G_NORM1, G_NORM2, G_FINAL2, G_DN = 48, 56, 64, 72
G_CONV, G_SC = 73, 73 + 24 * 5
G_COLS = G_SC + 8 * 3

DN = 8
C = 64
STEPS = 5
TP = STEPS * C
PADS = TP - T
FT = 22
C2_COLS = 6 * P + 13 * C
LEVELS = 6
G2 = MEM_GROUPS + LAYERS * LAYER_GROUPS
G_U, G_GATE, G_BR, G_WO, G_GU, G_DOWN = G2 + 6, G2 + 14, G2 + 18, G2 + 22, G2 + 24, G2 + 35
E2 = 4 * MEM_GROUPS + LAYERS * ACT_EVACS
D2 = LAYERS * DVE_EVACS
DN_SCALE = P ** -0.5
UNITS = 8


def build(nc, a, out):
    with ExitStack() as ctx:
        def sb(name, shape, dt=F32, scope=ctx):
            return scope.enter_context(nc.sbuf_tensor(name, shape, dt))

        def sem(name):
            return ctx.enter_context(nc.semaphore(name))

        stream_ps = [ctx.enter_context(nc.psum_tensor(f"stream_ps{s}", [P, 512], F32)) for s in range(SLOTS)]
        free_ps = [ctx.enter_context(nc.psum_tensor(f"free_ps{i}", [P, 512], F32)) for i in range(4)]

        xT = sb("xT", [P, KT, T])
        h_hi = sb("h_hi", [P, KT, T], F32R)
        h_lo = sb("h_lo", [P, KT, T], F32R)
        wide = sb("wide", [P, KT, T])
        raw = sb("raw", [P, SLOTS, BLK])
        w_hi_all = sb("w_hi", [P, SLOTS, KT, P], F32R)
        w_lo_all = sb("w_lo", [P, SLOTS, KT, P], F32R)
        w_hi, w_lo = ([w[:, s, :, :] for s in range(SLOTS)] for w in (w_hi_all, w_lo_all))
        cst = sb("cst", [P, 2 * P])
        ident, ones = cst[:, 0:P], cst[:, P:2 * P]
        ident_bf = sb("ident_bf", [P, P], BF16)
        gains = sb("gains", [P, G_COLS])
        rstd = sb("rstd", [P, T])
        eps_col = sb("eps_col", [P, 1])
        iqT, qT, merged = wide[:, 0:4, 0:S], wide[:, 4:8, 0:S], wide[:, :, 0:S]
        mqT = iqT

        with ExitStack() as one:
            bias = sb("bias", [P, HEADS, S], scope=one)
            mkT = sb("mkT", [P, LAYERS * MHEADS, S], scope=one)
            mv = sb("mv", [P, LAYERS, 2, 512], scope=one)
            with ExitStack() as pro:
                mem_raw = sb("mem_raw", [P, KT, S], scope=pro)
                mem_f = sb("mem_f", [P, KT, S], scope=pro)
                mem_hi = [sb(f"mem_hi{l}", [P, KT, S], F32R, pro) for l in range(LAYERS)]
                mem_lo = [sb(f"mem_lo{l}", [P, KT, S], F32R, pro) for l in range(LAYERS)]
                rel_cst = sb("rel_cst", [P, P + 512], scope=pro)
                rel_sb = sb("rel_sb", [32, HEADS], scope=pro)
                rel_f = sb("rel_f", [HEADS, 512], scope=pro)
                hankel = sb("hankel", [P, HEADS, S], scope=pro)
            flip, bucket_hot = rel_cst[:, 0:P], rel_cst[0:32, P:P + 512]
            gates = sb("gates", [P, 24, S], scope=one)
            h32 = gates[:, 0:KT, :]
            with ExitStack() as win:
                y01_hi = sb("y01_hi", [P, 2, 4, S], F32R, win)
                sum_a = sb("sum_a", [P, POOLG, PAD + S], scope=win)
                sum_b = sb("sum_b", [P, POOLG, PAD + S], scope=win)
            y_hi = sb("y_hi", [P, 3, 4, S], F32R, one)
            y_lo = sb("y_lo", [P, 3, 4, S], F32R, one)
            az, pz, mz = (sb(n, [P, 4, S], scope=one) for n in ("az", "pz", "mz"))
            kT = sb("kT", [P, 4, S], scope=one)
            v = sb("v", [P, 2, 512], scope=one)
            pu = sb("pu", [P, POOLG, PAD + S], scope=one)
            soft = sb("soft", [P, 2, 512], scope=one)
            softT = sb("softT", [P, 2, 512], scope=one)
            idx_r, idx_s, idx_w = soft[:, :, 0:384], softT[:, 0, 0:384], softT[:, 1, 0:384]
            stage = sb("stage", [P, KT * 136], scope=one)
            wik = stage[:, :].rearrange("p (k n) -> p k n", k=KT)
            st_q, st_k = stage[:, 0:S], stage[:, S:2 * S]
            st_v = stage[:, 2 * S:3 * S].rearrange("p (t n) -> p t n", t=2)
            st_mq = stage[:, 0:512].rearrange("p (h n) -> p h n", h=2)
            st_mv = stage[:, 512:1024].rearrange("p (t n) -> p t n", t=2)
            pool_w = sb("pool_w", [P, POOLG, P], scope=one)
            ikT = sb("ikT", [P, S], scope=one)
            iw = sb("iw", [P, 2, HEADS], scope=one)
            admit = sb("admit", [P, 384 + POOLG * 16], scope=one)
            mask = sb("mask", [P, 384], BF16, one)
            top8 = sb("top8", [P, 2, 8], scope=one)
            stat = sb("stat", [P, 4, 4], scope=one)
            edge = admit[:, 384:].rearrange("p (g t) -> p g t", g=POOLG)

        with ExitStack() as two:
            cst2 = sb("cst2", [P, C2_COLS], scope=two)
            oT = sb("oT", [P, KT, TP], scope=two)
            scal = sb("scal", [P, STEPS, 6 * DN], scope=two)
            cx = sb("cx", [P, KT, T + 2], scope=two)
            bcv = sb("bcv", [P, 2, T], scope=two)
            with ExitStack() as dn:
                qkvT = sb("qkvT", [P, 3, DN, TP], scope=dn)
                decay = sb("decay", [P, STEPS * DN, C], scope=dn)
                with ExitStack() as conv:
                    st_raw = sb("st_raw", [P, SLOTS, T + 4], scope=conv)
                    k_sq = sb("k_sq", [P, DN, T], scope=conv)
                    beta_strict = sb("beta_strict", [P, STEPS * DN, C], scope=conv)
                    wba = sb("wba", [P, KT, 4 * DN], scope=conv)
                    adt = sb("adt", [P, 2 * DN], scope=conv)
                    beta_t, dt_u, sp, log_decay = (sb(n, [P, STEPS, DN], scope=conv) for n in ("beta_t", "dt_u", "sp", "log_decay"))
                    exg = sb("exg", [P, 5, STEPS, DN], scope=conv)
                    gcol = sb("gcol", [P, STEPS * DN], scope=conv)
                    ea = sb("ea", [P, DN], scope=conv)
                lvl = sb("lvl", [P, 4, DN, C], scope=dn)
                n1 = [sb(f"n1_{m}", [P, 2, 4, C], scope=dn) for m in range(1, LEVELS - 1)]
                n1_last = sb("n1_last", [P, 2, 4, C // 2], scope=dn)
                xy = sb("xy", [P, 2, 2, 4, C], scope=dn)
                vb = sb("vb", [P, DN, P], scope=dn)
                kdec = sb("kdec", [P, DN, P], scope=dn)
                kqs = sb("kqs", [P, DN, 6, C], scope=dn)
                sc = sb("sc", [P, 6 * DN], scope=dn)
                state = sb("state", [P, 2, DN, P], scope=dn)
                at = sb("at", [P, 2, DN, C], scope=dn)
            with ExitStack() as br2:
                ga, gb = (sb(n, [P, KT, T], scope=br2) for n in ("ga", "gb"))
                yd_hi, yd_lo, ys_hi, ys_lo = (sb(n, [P, KT, T], F32R, br2) for n in ("yd_hi", "yd_lo", "ys_hi", "ys_lo"))
            f_hi = sb("f_hi", [P, FT, T], F32R, two)
            f_lo = sb("f_lo", [P, FT, T], F32R, two)
            f_act, f_val = (sb(n, [P, 2, T], scope=two) for n in ("f_act", "f_val"))
        h32p = oT
        h32t = oT[:, :, TP - T:]
        sz = xT
        vs = vb[:, :, :].rearrange("p h (d c) -> p h d c", d=2)
        vo = wide[:, :, :].rearrange("p k n -> p (k n)")[:, 0:2 * DN * P].rearrange("p (d h n) -> p d h n", d=2, h=DN)
        mat = lambda i: cst2[:, i * P:(i + 1) * P]
        col = lambda i: cst2[:, 6 * P + i * C:6 * P + (i + 1) * C]
        tri, tri_swap, after, rows_f, rows_b, same = (mat(i) for i in range(6))
        tri_c, sigma, strict, upper, eye_c = (col(i) for i in range(5))

        x_in, mem_in, gains_in, cst_in, rel_in, admit_in, wik_in, poolw_in = (
            sem(n) for n in ("x_in", "mem_in", "gains_in", "cst_in", "rel_in", "admit_in", "wik_in", "poolw_in"))
        w_in = [sem(f"w_in{s}") for s in range(SLOTS)]
        hi_ready, lo_ready, blk_done, act_evac, dve_evac = (
            sem(n) for n in ("hi_ready", "lo_ready", "blk_done", "act_evac", "dve_evac"))
        sq_ready, ss_ready, rstd_ready, n32_ready, nhi_ready, nlo_ready = (
            sem(n) for n in ("sq_ready", "ss_ready", "rstd_ready", "n32_ready", "nhi_ready", "nlo_ready"))
        mem32_ready, memhi_ready, memlo_ready = (sem(n) for n in ("mem32_ready", "memhi_ready", "memlo_ready"))
        ident_ready, relf_done, relf_ready, relf_out, hankel_in, flip_done, bias_ready = (
            sem(n) for n in ("ident_ready", "relf_done", "relf_ready", "relf_out", "hankel_in", "flip_done", "bias_ready"))
        ikw_done, ikw_ready, idx_done, idx_relu, idx_used, mask_ready = (
            sem(n) for n in ("ikw_done", "ikw_ready", "idx_done", "idx_relu", "idx_used", "mask_ready"))
        qk_staged, v_staged, logit_done, max_ready, exp_ready, prob_ready, softT_done, softT_ready, pv_done, pv_used = (
            sem(n) for n in ("qk_staged", "v_staged", "logit_done", "max_ready", "exp_ready", "prob_ready",
                             "softT_done", "softT_ready", "pv_done", "pv_used"))
        pads_ready, pooled_ready, mixed_done, mixed_used, y_ready = (
            sem(n) for n in ("pads_ready", "pooled_ready", "mixed_done", "mixed_used", "y_ready"))
        part_used, mhi_ready, mlo_ready = (sem(n) for n in ("part_used", "mhi_ready", "mlo_ready"))
        stored = sem("stored")
        c2_in, wba_in, ba_done, th_ready, u_ready, ewu_ready, g_ready, gsum_done, gsum_ready, scal_ready = (
            sem(n) for n in ("c2_in", "wba_in", "ba_done", "th_ready", "u_ready", "ewu_ready", "g_ready", "gsum_done",
                             "gsum_ready", "scal_ready"))
        gd_ready, e_done, e_used, e_ready, expe_ready, decay_ready = (
            sem(n) for n in ("gd_ready", "e_done", "e_used", "e_ready", "expe_ready", "decay_ready"))
        zeros_ready, conv_done, silu_ready, l2sq_ready, l2_done, l2_used, l2rs_ready, l2_ready, x_out, x_back = (
            sem(n) for n in ("zeros_ready", "conv_done", "silu_ready", "l2sq_ready", "l2_done", "l2_used", "l2rs_ready", "l2_ready", "x_out", "x_back"))
        dn_staged, dnv_staged, kkq_done, kkq_used, lvl_ready, at_ready, vk_done, vk_used, ks_done, r_ready = (
            sem(n) for n in ("dn_staged", "dnv_staged", "kkq_done", "kkq_used", "lvl_ready", "at_ready", "vk_done", "vk_used",
                             "ks_done", "r_ready"))
        n1_done, n1_ready, yx_done, yx_ready, vnew_done, vnew_ready, o_done, o_used, su_done, sdec_ready, s_ready = (
            sem(n) for n in ("n1_done", "n1_ready", "yx_done", "yx_ready", "vnew_done", "vnew_ready", "o_done", "o_used",
                             "su_done", "sdec_ready", "s_ready"))
        osq_ready, oss_done, oss_used, ors_ready, yd_ready, ydhi_ready, ydlo_ready, yshi_ready, yslo_ready = (
            sem(n) for n in ("osq_ready", "oss_done", "oss_used", "ors_ready", "yd_ready", "ydhi_ready", "ydlo_ready", "yshi_ready", "yslo_ready"))
        fact_ready, fhi_ready, flo_ready = (sem(n) for n in ("fact_ready", "fhi_ready", "flo_ready"))
        held = sem("held")
        bank = ((stream_ps[2], stream_ps[3], free_ps[0]), tuple(free_ps[1:]))
        lvl_slot = lambda level: 1 + level % 3 if level < LEVELS - 1 else 0
        e_bank = [free_ps[i] for i in (3, 0, 1, 2, 3)]

        block = ctx.enter_context(nc.Block())
        rel_dram = a["rel_scratch"]

        def split_hi(act, G, s):
            act.wait_ge(w_in[s], 16 * (G + 1))
            act.wait_ge(blk_done, 4 * G + s + 1)
            nc.scalar.activation(w_hi[s][:, :, :], raw[:, s, :].rearrange("p (k n) -> p k n", k=KT),
                                 ACT.Copy).then_inc(hi_ready, 1)

        def split_lo(dve, G, s):
            dve.wait_ge(hi_ready, 4 * G + s + 1)
            nc.vector.tensor_tensor(w_lo[s][:, :, :], raw[:, s, :].rearrange("p (k n) -> p k n", k=KT),
                                    w_hi[s][:, :, :].bitcast(F32), ALU.subtract).then_inc(lo_ready, 1)

        def ahead(split, eng, G, s):
            split(eng, G + (s + AHEAD) // SLOTS, (s + AHEAD) % SLOTS)

        def mm3(ps, l_hi, l_lo, r_hi, r_lo, first, last):
            nc.tensor.matmul(ps, l_hi, r_hi, start=first, stop=False)
            nc.tensor.matmul(ps, l_hi, r_lo, start=False, stop=False)
            return nc.tensor.matmul(ps, l_lo, r_hi, start=False, stop=last)

        def block_cols(pe, G, s, free, free_at, r_hi, r_lo, parts=None):
            pe.wait_ge(lo_ready, 4 * G + s + 1 + SLOTS)
            pe.wait_ge(free, free_at)
            n = r_hi.shape[-1]
            for k in range(KT):
                if parts and k % 4 == 0:
                    pe.wait_ge(parts[0], parts[1] + k // 4)
                mm = mm3(stream_ps[s][:, 0:n], w_hi[s][:, k, :], w_lo[s][:, k, :], r_hi[:, k, :], r_lo[:, k, :],
                         k == 0, k == KT - 1)
            mm.then_inc(blk_done, 1)

        def block_rows(pe, G, s, free, free_at, l_hi, l_lo):
            pe.wait_ge(lo_ready, 4 * G + s + 2 + SLOTS)
            pe.wait_ge(free, free_at + 1)
            for t in range(2):
                for k in range(KT):
                    tok = slice(t * P, (t + 1) * P)
                    mm = mm3(stream_ps[s][:, t * S:(t + 1) * S].rearrange("p (j n) -> p j n", j=2), l_hi[:, k, tok], l_lo[:, k, tok],
                             w_hi_all[:, s:s + 2, k, :], w_lo_all[:, s:s + 2, k, :], k == 0, k == KT - 1)
            mm.then_inc(blk_done, 2)

        def evac(act, G, s, dst, func=ACT.Copy, scale=1.0):
            act.wait_ge(blk_done, 4 * G + s + 1 + SLOTS)
            n = dst.shape[-1] if len(dst.shape) == 2 else dst.shape[-1] * dst.shape[-2]
            src = stream_ps[s][:, 0:n]
            if len(dst.shape) == 3:
                src = src.rearrange("p (t n) -> p t n", n=dst.shape[-1])
            nc.scalar.activation(dst, src, func, scale=scale).then_inc(act_evac, 1)

        def evac_rows(act, G, s, dst):
            act.wait_ge(blk_done, 4 * G + s + 1 + SLOTS)
            src = stream_ps[s - s % 2][:, :].rearrange("p (t j n) -> p t j n", t=2, j=2)[:, :, s % 2, :]
            nc.scalar.activation(dst, src, ACT.Copy).then_inc(act_evac, 1)

        tok = slice(NM, T)
        xS, hS_hi, hS_lo, wideS = xT[:, :, tok], h_hi[:, :, tok], h_lo[:, :, tok], wide[:, :, tok]
        G0 = MEM_GROUPS

        def rstd_of(act, i, n):
            act.wait_ge(ss_ready, i + 1)
            nc.scalar.activation(rstd[:, 0:n], free_ps[0][:, 0:n], ACT.Ln, bias=eps_col[:, 0:1], scale=1.0 / D)
            nc.scalar.drain()
            nc.scalar.activation(rstd[:, 0:n], rstd[:, 0:n], ACT.Exp, scale=-0.5).then_inc(rstd_ready, 1)

        def sum_squares(pe, sq, i, sq_at):
            n = sq.shape[-1]
            for k in range(KT):
                pe.wait_ge(sq_ready, sq_at + k + 1)
                mm = nc.tensor.matmul(free_ps[0][:, 0:n], ones, sq[:, k, :], start=k == 0, stop=k == KT - 1)
            mm.then_inc(ss_ready, 1)

        def scale_rows(dve, dst, src, gain, half, ready):
            n = src.shape[-1]
            for k in range(4 * half, 4 * half + 4):
                op = nc.vector.scalar_tensor_tensor(out=dst[:, k, :], in0=src[:, k, :], scalar=gain(k),
                                                    in1=rstd[:, 0:n], op0=ALU.mult, op1=ALU.mult)
            op.then_inc(ready, 1)

        def gain_col(base, l=0):
            return lambda k: gains[:, bass.ds(base + KT * l + k, 1)]

        consts_ready = sem("consts_ready")

        @block.sync
        def _(sp):
            with sp.Fori(0, a["groups"]) as G:
                for s in range(SLOTS):
                    sp.wait_ge(lo_ready, 4 * G + s + 1)
                    sp.dma_start(raw[:, s, :], a["stream"][4 * G + s]).then_inc(w_in[s], 16)
            for s in range(AHEAD):
                sp.wait_ge(lo_ready, 4 * a["groups"] + s + 1)
                sp.dma_start(raw[:, s, :], a["stream"][4 * a["groups"] + s]).then_inc(w_in[s], 16)
            sp.wait_ge(stored, 32)

        @block.gpsimd
        def _(pool):
            nc.gpsimd.memset(eps_col[:, :], EPS).then_inc(consts_ready, 1)
            pool.wait_ge(relf_ready, 1)
            pool.dma_start(rel_dram, rel_f[:, :]).then_inc(relf_out, 16)
            pool.wait_ge(relf_out, 16)
            pool.dma_start(hankel[:, :, :], bass.AP(rel_dram.tensor, 0, [[1, P], [512, HEADS], [1, S]])).then_inc(hankel_in, 16)
            pool.sem_inc(part_used, 2)
            pool.wait_ge(flip_done, HEADS)
            nc.gpsimd.memset(pu[:, :, 0:PAD], 0.0)
            nc.gpsimd.drain()
            with pool.Fori(0, LAYERS) as l:
                E0 = SLOTS + 4 * MEM_GROUPS + ACT_EVACS * l
                pool.wait_ge(blk_done, SLOTS + 4 * (G0 + LAYER_GROUPS * l))
                pool.wait_ge(act_evac, E0 + 32)
                src, dst = pu, sum_a
                for i in range(POOLG):
                    w = 1 << i
                    nc.gpsimd.tensor_tensor(dst[:, i:, PAD:], src[:, i:, PAD:], src[:, i:, PAD - w:PAD + S - w], ALU.add)
                    if i == 0:
                        nc.gpsimd.memset(sum_a[:, :, 0:PAD], 0.0)
                        nc.gpsimd.memset(sum_b[:, :, 0:PAD], 0.0)
                    nc.gpsimd.drain()
                    src, dst = dst, (sum_b if dst is sum_a else sum_a)
                nc.gpsimd.drain()
                for g in range(POOLG):
                    total = (sum_a, sum_b)[g % 2]
                    nc.gpsimd.tensor_tensor(total[:, g, PAD:PAD + 16], total[:, g, PAD:PAD + 16], edge[:, g, :], ALU.mult)
                    nc.gpsimd.tensor_scalar(total[:, g, PAD + 16:], total[:, g, PAD + 16:], 1.0 / POOL_WINDOWS[g], 0.0, ALU.mult, ALU.add)
                nc.gpsimd.drain()
                for g in range(POOLG):
                    total = (sum_a, sum_b)[g % 2]
                    op = nc.gpsimd.tensor_tensor(pu[:, g, PAD:], total[:, g, PAD:], pu[:, g, PAD:], ALU.subtract)
                op.then_inc(pooled_ready, 1)
                with pool.Fori(0, 4) as hp:
                    pool.wait_ge(logit_done, 6 * l + hp + 1)
                    nc.gpsimd.tensor_copy(st_q, qT[:, bass.ds(hp, 1), :])
                    nc.gpsimd.tensor_copy(st_k, kT[:, bass.ds(hp, 1), :]).then_inc(qk_staged, 1)
                    pool.wait_ge(pv_done, 6 * l + hp + 1)
                    nc.gpsimd.tensor_copy(st_v, v[:, :, bass.ds(hp * P, P)]).then_inc(v_staged, 1)
                with pool.Fori(0, 2) as mp:
                    pool.wait_ge(pv_done, 6 * l + 4 + mp + 1)
                    nc.gpsimd.tensor_copy(st_mq, mqT[:, bass.ds(2 * mp, 2), :]).then_inc(qk_staged, 1)
                    nc.gpsimd.tensor_copy(st_mv, mv[:, bass.ds(l, 1), :, bass.ds(mp * 2 * P, 2 * P)]).then_inc(v_staged, 1)
                nc.gpsimd.drain()
                nc.gpsimd.memset(merged, 0.0)
                nc.gpsimd.drain()
                with pool.Fori(0, 3) as br:
                    for s in range(SLOTS):
                        pool.wait_ge(dve_evac, SLOTS + DVE_EVACS * l + 4 * br + s + 1)
                        mg = merged[:, 2 * s:2 * s + 2, :]
                        nc.gpsimd.tensor_tensor(mg, mg, soft[:, s % 2, :].rearrange("p (k n) -> p k n", k=2),
                                                ALU.add).then_inc(part_used, 1)
                    nc.gpsimd.drain()

            pool.wait_ge(mlo_ready, 2 * LAYERS)
            for zeros in (st_raw[:, :, 0:2], st_raw[:, :, T + 2:], h32p[:, :, 0:PADS], qkvT[:, :, :, 0:PADS], cx[:, :, 0:1], cx[:, :, T + 1:]):
                op = nc.gpsimd.memset(zeros, 0.0)
            op.then_inc(zeros_ready, 1)
            nc.gpsimd.memset(state[:, :, :, :], 0.0)
            pool.wait_ge(c2_in, 16)
            for d in range(2):
                nc.gpsimd.tensor_copy(at[:, d, :, :], eye_c.unsqueeze(1).broadcast_to([P, DN, C]))
            pool.wait_ge(g_ready, 1)
            by_step = lambda x: x.unsqueeze(1).broadcast_to([P, STEPS * DN, C])
            by_col = lambda x: x[:, :, :].rearrange("p t h -> p (t h)").unsqueeze(2).broadcast_to([P, STEPS * DN, C])
            nc.gpsimd.tensor_tensor(decay[:, :, :], by_step(tri_c), by_col(log_decay), ALU.mult).then_inc(gd_ready, 1)
            nc.gpsimd.tensor_tensor(beta_strict[:, :, :], by_step(strict), by_col(beta_t), ALU.mult)
            nc.gpsimd.drain()
            nc.gpsimd.tensor_tensor(beta_strict[:, :, :], beta_strict[:, :, :], by_step(upper), ALU.add)
            nc.gpsimd.drain()
            pool.wait_ge(e_used, STEPS)
            nc.gpsimd.tensor_tensor(decay[:, :, :], decay[:, :, :], by_step(sigma), ALU.mult).then_inc(e_ready, 1)
            for i, dst in enumerate((wide, k_sq)):
                pool.wait_ge(silu_ready, i + 1)
                for half in range(2):
                    hs = slice(4 * half, 4 * half + 4)
                    src = qkvT[:, i, hs, PADS:]
                    nc.gpsimd.tensor_tensor(dst[:, hs, :], src, src, ALU.mult).then_inc(l2sq_ready, 1)
                if i == 0:
                    pool.wait_ge(expe_ready, 1)
                    nc.gpsimd.tensor_tensor(decay[:, :, :], decay[:, :, :], beta_strict[:, :, :], ALU.mult).then_inc(decay_ready, 1)
            pool.wait_ge(l2_ready, 2)
            for buffer in n1:
                nc.gpsimd.memset(buffer[:, :, :, :], 0.0)
            pool.wait_ge(silu_ready, 3)
            with pool.Fori(0, STEPS) as t:
                nc.gpsimd.drain()
                pool.wait_ge(r_ready, 2 * t + 1)
                pool.wait_ge(vk_used, 2 * t + 1)
                f, b = bass.ds(C * t, C), bass.ds(C * (STEPS - 1) - C * t, C)
                for slot, src, chunk in ((0, 1, f), (1, 1, b), (2, 0, b), (3, 1, b), (4, 1, f), (5, 0, f)):
                    nc.gpsimd.tensor_copy(kqs[:, :, slot, :], qkvT[:, src, :, chunk])
                nc.gpsimd.tensor_copy(sc[:, :], scal[:, bass.ds(t, 1), :].rearrange("p a n -> p (a n)")).then_inc(dn_staged, 1)
                pool.wait_ge(su_done, 2 * t + 2)
                pool.sem_inc(held, 1)
                nc.gpsimd.tensor_copy(vs[:, :, 0, :], qkvT[:, 2, :, f])
                nc.gpsimd.tensor_copy(vs[:, :, 1, :], qkvT[:, 2, :, b]).then_inc(dnv_staged, 1)
                for level in range(LEVELS):
                    if level == LEVELS - 1:
                        nc.gpsimd.drain()
                    for half in range(2):
                        hs = slice(4 * half, 4 * half + 4)
                        if level == 0:
                            pool.wait_ge(kkq_used, 2 * t + half + 1)
                        elif 3 <= level < LEVELS - 1:
                            pool.wait_ge(yx_ready, 12 * t + 2 * (level - 3) + half + 1)
                        nc.gpsimd.tensor_tensor(lvl[:, lvl_slot(level), hs, :], lvl[:, 0, hs, :],
                                                col(5 + level).unsqueeze(1).broadcast_to([P, 4, C]), ALU.mult).then_inc(lvl_ready, 1)
                    if level == 2:
                        for half in range(2):
                            hs = slice(4 * half, 4 * half + 4)
                            for d in range(2):
                                op = nc.gpsimd.tensor_tensor(at[:, d, hs, :], at[:, d, hs, :], col(11 + d).unsqueeze(1).broadcast_to([P, 4, C]), ALU.mult)
                            op.then_inc(at_ready, 1)
                for half in range(2):
                    hs = slice(4 * half, 4 * half + 4)
                    pool.wait_ge(ks_done, 2 * t + half + 1)
                    for d in range(2):
                        decay_s = sc[:, (4 + d) * DN + 4 * half:(4 + d) * DN + 4 * half + 4].unsqueeze(2).broadcast_to([P, 4, P])
                        op = nc.gpsimd.tensor_tensor(state[:, d, hs, :], state[:, d, hs, :], decay_s, ALU.mult)
                    op.then_inc(sdec_ready, 1)

        @block.scalar
        def _(act):
            act.dma_start(mem_raw[:, :, :], a["memT"]).then_inc(mem_in, 16)
            act.dma_start(xT[:, :, :], a["xT"]).then_inc(x_in, 16)
            act.dma_start(cst[:, :], a["cst"]).then_inc(cst_in, 16)
            act.dma_start(gains[:, :], a["gains"]).then_inc(gains_in, 16)
            act.dma_start(rel_cst[:, :], a["rel_cst"]).then_inc(rel_in, 16)
            act.dma_start(rel_sb[:, :], a["rel_bias"]).then_inc(rel_in, 16)
            act.dma_start(admit[:, :], a["admit"]).then_inc(admit_in, 16)
            act.sem_inc(act_evac, SLOTS)
            act.wait_ge(mem_in, 16)
            for k in range(KT):
                nc.scalar.activation(mem_f[:, k, :], mem_raw[:, k, :], ACT.Square).then_inc(sq_ready, 1)
            act.wait_ge(x_in, 16)
            for k in range(KT):
                nc.scalar.activation(wide[:, k, :], xT[:, k, :], ACT.Square).then_inc(sq_ready, 1)
            for s in range(AHEAD):
                split_hi(act, 0, s)
            act.wait_ge(consts_ready, 1)
            rstd_of(act, 0, S)
            for l in range(LAYERS):
                for half in range(2):
                    act.wait_ge(mem32_ready, 2 * l + half + 1)
                    ks = slice(4 * half, 4 * half + 4)
                    nc.scalar.activation(mem_hi[l][:, ks, :], mem_f[:, ks, :], ACT.Copy).then_inc(memhi_ready, 1)
            act.wait_ge(relf_done, 1)
            nc.scalar.activation(rel_f[:, :], free_ps[1][0:HEADS, :], ACT.Copy).then_inc(relf_ready, 1)
            for l in range(LAYERS):
                for s in range(SLOTS):
                    ahead(split_hi, act, 2 * l, s)
                    evac(act, 2 * l, s, mkT[:, 4 * l + s, :])
                for s in range(SLOTS):
                    ahead(split_hi, act, 2 * l + 1, s)
                    evac_rows(act, 2 * l + 1, s, mv[:, l, :, s * P:(s + 1) * P])

            act.wait_ge(bias_ready, HEADS)
            with act.Fori(0, LAYERS) as l:
                G = G0 + LAYER_GROUPS * l
                act.wait_ge(pv_done, 6 * l + 1)
                act.dma_start(wik, a["wik"][l]).then_inc(wik_in, 16)
                act.wait_ge(mixed_used, l + 1)
                act.dma_start(pool_w[:, :, :], a["pool_w"][l]).then_inc(poolw_in, 16)
                rstd_of(act, 1 + l, S)
                for half in range(2):
                    act.wait_ge(n32_ready, 2 * l + half + 1)
                    ks = slice(4 * half, 4 * half + 4)
                    nc.scalar.activation(hS_hi[:, ks, :], h32[:, ks, :], ACT.Copy).then_inc(nhi_ready, 1)
                for s in range(SLOTS):
                    ahead(split_hi, act, G, s)
                    evac(act, G, s, iqT[:, s, :])
                act.wait_ge(ikw_done, l + 1)
                nc.scalar.activation(ikT[:, :], free_ps[1][:, 0:S], ACT.Copy)
                nc.scalar.activation(iw[:, :, :], free_ps[2][:, 0:2 * HEADS].rearrange("p (t h) -> p t h", t=2),
                                     ACT.Copy, scale=IDX_W_SCALE).then_inc(ikw_ready, 1)
                for s in range(SLOTS):
                    ahead(split_hi, act, G + 1, s)
                    evac(act, G + 1, s, qT[:, s, :])
                for half, dst in ((0, kT), (1, v)):
                    for s in range(SLOTS):
                        ahead(split_hi, act, G + 2 + half, s)
                        h = 4 * half + s
                        act.wait_ge(idx_done, HEADS * l + h + 1)
                        act.wait_ge(idx_used, HEADS * l + h + 1)
                        nc.scalar.activation(idx_r[:, h % 2, :], free_ps[h % 4][:, 0:384], ACT.Relu).then_inc(idx_relu, 1)
                        if half == 0:
                            evac(act, G + 2, s, kT[:, s, :])
                        else:
                            evac_rows(act, G + 3, s, v[:, :, s * P:(s + 1) * P])
                for i, dst in enumerate((az, pz, mz)):
                    for s in range(SLOTS):
                        ahead(split_hi, act, G + 4 + i, s)
                        evac(act, G + 4 + i, s, dst[:, s, :], ACT.Silu)
                for s in range(SLOTS):
                    ahead(split_hi, act, G + 7, s)
                    evac(act, G + 7, s, pu[:, s, PAD:])
                for s in range(SLOTS):
                    ahead(split_hi, act, G + 8, s)
                    evac(act, G + 8, s, mqT[:, s, :])

                with act.Fori(0, 4) as hp:
                    for s in range(SLOTS):
                        ahead(split_hi, act, G + 9 + hp, s)
                        if s == 0:
                            act.wait_ge(max_ready, 6 * l + hp + 1)
                            for j in range(2):
                                for t, cols in ((0, slice(0, P)), (1, slice(P, 3 * P))):
                                    op = nc.scalar.activation(soft[:, j, cols], soft[:, j, cols], ACT.Exp,
                                                              bias=stat[:, 0, 2 * t + j:2 * t + j + 1],
                                                              accum_out=stat[:, 1, 2 * t + j:2 * t + j + 1])
                            op.then_inc(exp_ready, 1)
                        evac(act, G + 9 + hp, s, gates[:, bass.ds(4 * hp + s, 1), :].rearrange("p a n -> p (a n)"), ACT.Tanh, 0.5)
                        if s == 2:
                            act.wait_ge(softT_done, 6 * l + hp + 1)
                            for j in range(2):
                                op = nc.scalar.activation(softT[:, j, 0:384], free_ps[2 + j][:, 0:384], ACT.Copy)
                            op.then_inc(softT_ready, 1)
                with act.Fori(0, 2) as mp:
                    for s in range(SLOTS):
                        ahead(split_hi, act, G + 13 + mp, s)
                        if s == 0:
                            act.wait_ge(max_ready, 6 * l + 4 + mp + 1)
                            for j in range(2):
                                for t in range(2):
                                    c = slice(t * S, (t + 1) * S)
                                    op = nc.scalar.activation(soft[:, j, c], free_ps[j][:, c], ACT.Exp,
                                                              bias=stat[:, 0, 2 * j + t:2 * j + t + 1], scale=MEM_SCALE,
                                                              accum_out=stat[:, 1, 2 * j + t:2 * j + t + 1])
                            op.then_inc(exp_ready, 1)
                        evac(act, G + 13 + mp, s, gates[:, bass.ds(16 + 4 * mp + s, 1), :].rearrange("p a n -> p (a n)"), ACT.Tanh, 0.5)
                        if s == 2:
                            act.wait_ge(softT_done, 6 * l + 4 + mp + 1)
                            for j in range(2):
                                op = nc.scalar.activation(softT[:, j, :], free_ps[2 + j][:, :], ACT.Copy)
                            op.then_inc(softT_ready, 1)
                with act.Fori(0, 3) as br:
                    for s in range(SLOTS):
                        ahead(split_hi, act, G + 15 + br, s)
                act.wait_ge(blk_done, SLOTS + 4 * (G + 18))
                for half in range(2):
                    act.wait_ge(part_used, 12 * l + 12 - 2 + 2 * half + 2)
                    ks = slice(4 * half, 4 * half + 4)
                    nc.scalar.activation(hS_hi[:, ks, :], merged[:, ks, :], ACT.Copy, scale=0.5).then_inc(mhi_ready, 1)
                with act.Fori(0, 2) as w:
                    for s in range(SLOTS):
                        ahead(split_hi, act, G + 18 + w, s)
                        act.wait_ge(dve_evac, SLOTS + DVE_EVACS * l + 12 + 4 * w + s + 1)
                        act.wait_ge(mlo_ready, 2 * l + 2)
                        nc.scalar.activation(wideS[:, bass.ds(4 * w + s, 1), :], xS[:, bass.ds(4 * w + s, 1), :],
                                             ACT.Square).then_inc(sq_ready, 1)
            rstd_of(act, 1 + LAYERS, S)
            act.wait_ge(mlo_ready, 2 * LAYERS)
            act.dma_start(cst2[:, :], a["cst2"]).then_inc(c2_in, 16)
            act.dma_start(wba[:, :, :], a["wba"]).then_inc(wba_in, 16)
            act.dma_start(adt[:, :], a["adt"]).then_inc(wba_in, 16)
            for k in range(KT):
                if k % 4 == 0:
                    act.wait_ge(n32_ready, 2 * LAYERS + k // 4 + 1)
                nc.scalar.activation(wide[:, k, :], xT[:, k, :], ACT.Square).then_inc(sq_ready, 1)
            rstd_of(act, 2 + LAYERS, T)
            act.dma_start(a["x_spill"], xT[:, :, :]).then_inc(x_out, 16)

            def split_norm_hi(at):
                for half in range(2):
                    act.wait_ge(n32_ready, at + half + 1)
                    ks = slice(4 * half, 4 * half + 4)
                    nc.scalar.activation(h_hi[:, ks, :], h32t[:, ks, :], ACT.Copy).then_inc(nhi_ready, 1)

            split_norm_hi(2 * LAYERS + 2)
            act.wait_ge(wba_in, 32)
            nc.scalar.activation(ea[:, :], adt[:, 0:DN], ACT.Exp)
            act.wait_ge(ba_done, 1)
            ba = free_ps[1][:, 0:STEPS * 2 * DN].rearrange("p (t n) -> p t n", t=STEPS)
            nc.scalar.activation(beta_t[:, :, :], ba[:, :, 0:DN], ACT.Tanh, scale=0.5).then_inc(th_ready, 1)
            act.wait_ge(u_ready, 1)
            nc.scalar.activation(sp[:, :, :], sp[:, :, :], ACT.Exp)
            nc.scalar.drain()
            nc.scalar.activation(sp[:, :, :], sp[:, :, :], ACT.Ln, bias=ones[:, 0:1]).then_inc(ewu_ready, 1)

            def qkv_channels(i):
                for n in range(KT):
                    ahead(split_hi, act, G2 + 2 * i + n // SLOTS, n % SLOTS)
                    s = n % SLOTS
                    act.wait_ge(blk_done, SLOTS + 4 * G2 + 8 * i + n + 1)
                    if n >= SLOTS:
                        act.wait_ge(conv_done, 8 * i + n - SLOTS + 1)
                    nc.scalar.activation(st_raw[:, s, 2:T + 2], stream_ps[s][:, 0:T], ACT.Copy)
                    nc.scalar.activation(qkvT[:, bass.ds(i, 1), n, PADS:].rearrange("p a n -> p (a n)"), stream_ps[s][:, 0:T], ACT.Copy,
                                         scale=gains[:, bass.ds(G_CONV + 40 * i + 5 * n + 2, 1)]).then_inc(act_evac, 1)
                act.wait_ge(conv_done, 8 * i + 8)
                act.sem_inc(held, 1)
                qkv = qkvT[:, bass.ds(i, 1), :, PADS:].rearrange("p a h n -> p (a h) n")
                nc.scalar.activation(qkv, qkv, ACT.Silu).then_inc(silu_ready, 1)

            qkv_channels(0)
            act.wait_ge(gsum_done, 1)
            nc.scalar.activation(gcol[:, :], free_ps[2][:, 0:STEPS * DN], ACT.Copy)
            nc.scalar.activation(exg[:, :, :, :], free_ps[2][:, 0:5 * STEPS * DN].rearrange("p (i t h) -> p i t h", i=5, t=STEPS),
                                 ACT.Exp).then_inc(gsum_ready, 1)
            with act.Fori(1, 2) as i:
                qkv_channels(i)
            act.wait_ge(e_ready, 1)
            nc.scalar.activation(decay[:, :, :], decay[:, :, :], ACT.Exp).then_inc(expe_ready, 1)
            with act.Fori(2, 3) as i:
                qkv_channels(i)

            def unit(j, s):
                ahead(split_hi, act, G_U + j, s)
                if s in (0, 3):
                    dst = (cx[:, bass.ds(j, 1), 1:T + 1] if s == 0 else sz[:, bass.ds(j, 1), :]).rearrange("p a n -> p (a n)")
                    act.wait_ge(blk_done, SLOTS + 4 * (G_U + j) + s + 1)
                    act.sem_inc(held, 1)
                    nc.scalar.activation(dst, stream_ps[s % 2][:, 0:T], ACT.Copy if s == 0 else ACT.Silu).then_inc(act_evac, 1)

            act.wait_ge(zeros_ready, 1)
            act.wait_ge(x_out, 16)
            for n in range(4):
                act.wait_ge(l2_done, n + 1)
                for h in range(4):
                    op = nc.scalar.activation((wide, k_sq)[n // 2][:, 4 * (n % 2) + h, :], free_ps[h][:, 0:T], ACT.Ln, bias=eps_col[:, 0:1])
                op.then_inc(l2_used, 1)
                if n < 3:
                    unit(0, n)
            nc.scalar.drain()
            for sq in (wide, k_sq):
                nc.scalar.activation(sq[:, :, :], sq[:, :, :], ACT.Exp, scale=-0.5).then_inc(l2rs_ready, 1)
            for m in range(3, 4 * (UNITS - STEPS)):
                unit(m // 4, m % 4)
            act.sem_inc(vk_used, 1)
            with act.Fori(0, STEPS) as t:
                j = UNITS - STEPS + t
                unit(j, 0)
                for half in range(2):
                    b = bank[half]
                    act.wait_ge(vk_done, 2 * t + half + 1)
                    act.wait_ge(su_done, 2 * t + half + 1)
                    for i in range(4):
                        h = 4 * half + i
                        nc.scalar.activation(vb[:, h, :], b[1][:, i * P:(i + 1) * P], ACT.Copy, scale=sc[:, h:h + 1])
                        op = nc.scalar.activation(kdec[:, h, :], b[2][:, i * P:(i + 1) * P], ACT.Copy, scale=sc[:, 3 * DN + h:3 * DN + h + 1])
                    op.then_inc(vk_used, 1)
                unit(j, 1)
                for level in range(1, LEVELS):
                    m = 1 << level
                    for half in range(2):
                        act.wait_ge(n1_done, 12 * t + 2 * level + half + 1)
                        src = bank[half][2][:, 0:2 * C]
                        if level < LEVELS - 1:
                            for d, rows in ((0, slice(0, C)), (1, slice(C, P))):
                                dst = n1[level - 1][rows, half, :, :].rearrange("p h (b i m) -> p (h b) i m", i=2, m=m)[:, :, 1 - d, :]
                                op = nc.scalar.activation(dst, src[rows, :].rearrange("p (n m) -> p n m", m=m), ACT.Copy)
                        else:
                            op = nc.scalar.activation(n1_last[:, half, :, :], src.rearrange("p (h c) -> p h c", h=4), ACT.Copy)
                        op.then_inc(n1_ready, 1)
                    if level == 2:
                        unit(j, 2)
                for half in range(2):
                    hs = slice(4 * half, 4 * half + 4)
                    act.wait_ge(vnew_done, 2 * t + half + 1)
                    for d, rows in ((0, slice(0, C)), (1, slice(C, P))):
                        op = nc.scalar.activation(vo[rows, d, hs, :], bank[half][0][rows, :].rearrange("p (h n) -> p h n", h=4), ACT.Copy)
                    op.then_inc(vnew_ready, 1)
                unit(j, 3)
            act.wait_ge(s_ready, 2 + 2 * STEPS)
            act.wait_ge(o_used, 2 + 2 * STEPS)
            for k in range(KT):
                nc.scalar.activation(wide[:, k, :], oT[:, k, PADS:], ACT.Square).then_inc(osq_ready, 1)
            for w in range(4):
                for s in range(SLOTS):
                    ahead(split_hi, act, G_GATE + w, s)
                    evac(act, G_GATE + w, s, (ga, gb)[w // 2][:, 4 * (w % 2) + s, :], ACT.Tanh, 0.5)
                if w < 2:
                    act.wait_ge(oss_done, w + 1)
                    for h in range(4):
                        op = nc.scalar.activation(wide[:, 4 * w + h, :], free_ps[h][:, 0:T], ACT.Ln, bias=eps_col[:, 0:1], scale=1.0 / P)
                    op.then_inc(oss_used, 1)
                if w == 1:
                    nc.scalar.drain()
                    nc.scalar.activation(wide[:, :, :], wide[:, :, :], ACT.Exp, scale=-0.5).then_inc(ors_ready, 1)
                if w == 2:
                    nc.scalar.activation(ys_hi[:, :, :], cx[:, :, 1:T + 1], ACT.Copy).then_inc(yshi_ready, 1)
            act.wait_ge(yd_ready, 1)
            nc.scalar.activation(yd_hi[:, :, :], oT[:, :, PADS:], ACT.Copy).then_inc(ydhi_ready, 1)
            act.dma_start(xT[:, :, :], a["x_spill"]).then_inc(x_back, 16)
            with act.Fori(0, 4) as w:
                for s in range(SLOTS):
                    ahead(split_hi, act, G_BR + w, s)
            for half in range(2):
                act.wait_ge(dve_evac, SLOTS + D2 + 28 + 4 * half)
                ks = slice(4 * half, 4 * half + 4)
                nc.scalar.activation(h_hi[:, ks, :], wide[:, ks, :], ACT.Copy, scale=0.5).then_inc(mhi_ready, 1)

            def squares(G, D_at):
                with act.Fori(0, 2) as w:
                    for s in range(SLOTS):
                        ahead(split_hi, act, G + w, s)
                        act.wait_ge(dve_evac, SLOTS + D_at + 4 * w + s + 1)
                        act.wait_ge(mlo_ready, 2 * LAYERS + 2)
                        nc.scalar.activation(wide[:, bass.ds(4 * w + s, 1), :], xT[:, bass.ds(4 * w + s, 1), :],
                                             ACT.Square).then_inc(sq_ready, 1)

            squares(G_WO, D2 + 32)
            rstd_of(act, 3 + LAYERS, T)
            split_norm_hi(2 * LAYERS + 4)
            with act.Fori(0, FT // 2) as w:
                for s in range(SLOTS):
                    ahead(split_hi, act, G_GU + w, s)
                    if s % 2 == 0:
                        act.wait_ge(blk_done, SLOTS + 4 * (G_GU + w) + s + 1)
                        nc.scalar.activation(f_act[:, s // 2, :], stream_ps[s][:, 0:T], ACT.Silu).then_inc(fact_ready, 1)
                    else:
                        act.wait_ge(dve_evac, SLOTS + D2 + 40 + 4 * w + s + 1)
                        nc.scalar.activation(f_hi[:, bass.ds(2 * w + s // 2, 1), :].rearrange("p a n -> p (a n)"), f_val[:, s // 2, :],
                                             ACT.Copy).then_inc(fhi_ready, 1)
            with act.Fori(0, 2) as w:
                for n in range(12):
                    ahead(split_hi, act, G_DOWN + 3 * w + n // SLOTS, n % SLOTS)
                    if n % 3 == 2:
                        act.wait_ge(dve_evac, SLOTS + D2 + 84 + 4 * w + n // 3 + 1)
                        nc.scalar.activation(wide[:, bass.ds(4 * w + n // 3, 1), :], xT[:, bass.ds(4 * w + n // 3, 1), :],
                                             ACT.Square).then_inc(sq_ready, 1)
            rstd_of(act, 4 + LAYERS, T)
            for half in range(2):
                ks = slice(4 * half, 4 * half + 4)
                act.wait_ge(n32_ready, 2 * LAYERS + 6 + half + 1)
                act.dma_start(out[:, ks, :], h32t[:, ks, NM:]).then_inc(stored, 16)

        @block.vector
        def _(dve):
            dve.sem_inc(lo_ready, SLOTS)
            dve.sem_inc(dve_evac, SLOTS)
            dve.sem_inc(idx_used, 2)
            dve.sem_inc(pv_used, 1)
            dve.sem_inc(mixed_used, 1)
            dve.wait_ge(cst_in, 16)
            nc.vector.tensor_copy(ident_bf[:, :], ident).then_inc(ident_ready, 1)
            dve.wait_ge(gains_in, 16)
            for s in range(AHEAD):
                split_lo(dve, 0, s)
            dve.wait_ge(rstd_ready, 1)
            for l in range(LAYERS):
                for half in range(2):
                    if l:
                        dve.wait_ge(memlo_ready, half + 1)
                    scale_rows(dve, mem_f, mem_raw, gain_col(G_MEM, l), half, mem32_ready)
                for half in range(2):
                    dve.wait_ge(memhi_ready, 2 * l + half + 1)
                    ks = slice(4 * half, 4 * half + 4)
                    nc.vector.tensor_tensor(mem_lo[l][:, ks, :], mem_f[:, ks, :], mem_hi[l][:, ks, :].bitcast(F32),
                                            ALU.subtract).then_inc(memlo_ready, 1)
            for g in range(MEM_GROUPS):
                for s in range(SLOTS):
                    ahead(split_lo, dve, g, s)
            for h in range(HEADS):
                dve.wait_ge(flip_done, h + 1)
                nc.vector.tensor_copy(bias[:, h, :], free_ps[h % 4][:, 0:S]).then_inc(bias_ready, 1)
            dve.wait_ge(admit_in, 16)

            with dve.Fori(0, LAYERS) as l:
                G = G0 + LAYER_GROUPS * l
                dve.wait_ge(rstd_ready, 2 + l)
                for half in range(2):
                    scale_rows(dve, h32, xS, gain_col(G_NORM, l), half, n32_ready)
                for half in range(2):
                    dve.wait_ge(nhi_ready, 2 * l + half + 1)
                    ks = slice(4 * half, 4 * half + 4)
                    nc.vector.tensor_tensor(hS_lo[:, ks, :], h32[:, ks, :], hS_hi[:, ks, :].bitcast(F32),
                                            ALU.subtract).then_inc(nlo_ready, 1)
                for g in range(2):
                    for s in range(SLOTS):
                        ahead(split_lo, dve, G + g, s)
                dve.wait_ge(ikw_ready, l + 1)
                for g in range(2):
                    for s in range(SLOTS):
                        ahead(split_lo, dve, G + 2 + g, s)
                        h = 4 * g + s
                        nc.vector.drain()
                        dve.wait_ge(idx_relu, HEADS * l + h + 1)
                        for t, cols in ((0, slice(0, P)), (1, slice(P, 3 * P))):
                            op = nc.vector.scalar_tensor_tensor(
                                out=idx_s[:, cols], in0=idx_r[:, h % 2, cols], scalar=iw[:, t, h:h + 1],
                                in1=admit[:, cols] if h == 0 else idx_s[:, cols], op0=ALU.mult, op1=ALU.add)
                        op.then_inc(idx_used, 1)
                for g in range(3):
                    for s in range(SLOTS):
                        ahead(split_lo, dve, G + 4 + g, s)
                        i = 4 * g + s
                        if i < TOPK // 8:
                            src = idx_s if i == 0 else idx_w
                            nc.vector.drain()
                            for t, cols in ((0, slice(0, P)), (1, slice(P, 3 * P))):
                                nc.vector.max(top8[:, t, :], src[:, cols])
                            nc.vector.drain()
                            for t, cols in ((0, slice(0, P)), (1, slice(P, 3 * P))):
                                nc.vector.match_replace(idx_w[:, cols], top8[:, t, :], src[:, cols], TAKEN)
                        if i == TOPK // 8:
                            nc.vector.drain()
                            nc.vector.tensor_scalar(mask[:, :], idx_w, TAKEN / 2, NEG, ALU.is_gt, ALU.mult).then_inc(mask_ready, 1)
                for g in range(2):
                    for s in range(SLOTS):
                        ahead(split_lo, dve, G + 7 + g, s)

                def normalise(i, parts):
                    dve.wait_ge(exp_ready, i)
                    nc.vector.reciprocal(stat[:, 2, :], stat[:, 1, :])
                    nc.vector.drain()
                    for j, cols, c in parts:
                        op = nc.vector.tensor_scalar(soft[:, j, cols], soft[:, j, cols], stat[:, 2, c:c + 1], None, ALU.mult)
                    op.then_inc(prob_ready, 1)

                def split_y(src, dst_hi, dst_lo):
                    nc.vector.drain()
                    nc.vector.tensor_copy(dst_hi, src)
                    nc.vector.drain()
                    return nc.vector.tensor_tensor(dst_lo, src, dst_hi.bitcast(F32), ALU.subtract)

                with dve.Fori(0, 4) as hp:
                    for s in range(SLOTS):
                        ahead(split_lo, dve, G + 9 + hp, s)
                        if s == 0:
                            dve.wait_ge(logit_done, 6 * l + hp + 2)
                            for j in range(2):
                                head = bias[:, bass.ds(2 * hp + j, 1), :].rearrange("p a n -> p (a n)")
                                nc.vector.scalar_tensor_tensor(out=soft[:, j, 0:P], in0=free_ps[j][:, 0:P], scalar=ATTN_SCALE,
                                                               in1=head[:, P:2 * P], op0=ALU.mult, op1=ALU.add)
                                nc.vector.scalar_tensor_tensor(out=soft[:, j, P:3 * P], in0=free_ps[j][:, P:3 * P], scalar=ATTN_SCALE,
                                                               in1=head, op0=ALU.mult, op1=ALU.add)
                            nc.vector.drain()
                            nc.vector.tensor_reduce(stat[:, 3, 0:2], soft[:, :, 0:P], AX, ALU.max)
                            nc.vector.tensor_reduce(stat[:, 3, 2:4], soft[:, :, P:3 * P], AX, ALU.max)
                            nc.vector.drain()
                            nc.vector.tensor_scalar(stat[:, 0, :], stat[:, 3, :], -1.0, None, ALU.mult).then_inc(max_ready, 1)
                        if s == 1:
                            normalise(6 * l + hp + 1, [(j, c, 2 * t + j) for j in range(2)
                                                       for t, c in ((0, slice(0, P)), (1, slice(P, 3 * P)))])
                    dve.wait_ge(pv_done, 6 * l + hp + 2)
                    nc.vector.tensor_tensor(soft[:, 0, 0:S], free_ps[0][:, 0:S],
                                            az[:, bass.ds(hp, 1), :].rearrange("p a n -> p (a n)"), ALU.mult).then_inc(pv_used, 1)
                    split_y(soft[:, 0, 0:S], y_hi[:, 1, bass.ds(hp, 1), :].rearrange("p a n -> p (a n)"),
                            y_lo[:, 1, bass.ds(hp, 1), :].rearrange("p a n -> p (a n)")).then_inc(y_ready, 1)
                    nc.vector.drain()
                dve.wait_ge(mixed_done, l + 1)
                for i in range(2):
                    for j in range(2):
                        g = 2 * i + j
                        nc.vector.scalar_tensor_tensor(out=soft[:, i, j * S:(j + 1) * S], in0=free_ps[2 + i][:, j * S:(j + 1) * S],
                                                       scalar=gains[:, bass.ds(G_POOL + POOLG * l + g, 1)], in1=pz[:, g, :],
                                                       op0=ALU.mult, op1=ALU.mult)
                op = split_y(soft[:, :, :].rearrange("p i (j n) -> p (i j) n", j=2), y_hi[:, 0, :, :], y_lo[:, 0, :, :])
                op.then_inc(mixed_used, 1)
                nc.vector.drain()
                with dve.Fori(0, 2) as mp:
                    for s in range(SLOTS):
                        ahead(split_lo, dve, G + 13 + mp, s)
                        if s == 0:
                            dve.wait_ge(logit_done, 6 * l + 4 + mp + 2)
                            for j in range(2):
                                nc.vector.tensor_reduce(stat[:, 3, 2 * j:2 * j + 2], free_ps[j][:, :].rearrange("p (t n) -> p t n", t=2),
                                                        AX, ALU.max)
                            nc.vector.drain()
                            nc.vector.tensor_scalar(stat[:, 0, :], stat[:, 3, :], -MEM_SCALE, None, ALU.mult).then_inc(max_ready, 1)
                        if s == 1:
                            normalise(6 * l + 4 + mp + 1, [(j, slice(t * S, (t + 1) * S), 2 * j + t) for j in range(2) for t in range(2)])
                    dve.wait_ge(pv_done, 6 * l + 4 + mp + 2)
                    nc.vector.tensor_tensor(soft[:, 0, :].rearrange("p (h n) -> p h n", h=2),
                                            free_ps[0][:, :].rearrange("p (h n) -> p h n", h=2),
                                            mz[:, bass.ds(2 * mp, 2), :], ALU.mult).then_inc(pv_used, 1)
                    split_y(soft[:, 0, :].rearrange("p (h n) -> p h n", h=2), y_hi[:, 2, bass.ds(2 * mp, 2), :],
                            y_lo[:, 2, bass.ds(2 * mp, 2), :]).then_inc(y_ready, 1)
                    nc.vector.drain()
                with dve.Fori(0, 3) as br:
                    for s in range(SLOTS):
                        ahead(split_lo, dve, G + 15 + br, s)
                        dve.wait_ge(blk_done, SLOTS + 4 * (G + 15 + br) + s + 1)
                        dve.wait_ge(part_used, 12 * l + 4 * br + s + 1)
                        nc.vector.scalar_tensor_tensor(out=soft[:, s % 2, :].rearrange("p (k n) -> p k n", k=2),
                                                       in0=gates[:, bass.ds(8 * br + 2 * s, 2), :], scalar=1.0,
                                                       in1=stream_ps[s][:, :].rearrange("p (k n) -> p k n", k=2),
                                                       op0=ALU.add, op1=ALU.mult).then_inc(dve_evac, 1)
                for half in range(2):
                    dve.wait_ge(mhi_ready, 2 * l + half + 1)
                    ks = slice(4 * half, 4 * half + 4)
                    nc.vector.scalar_tensor_tensor(out=hS_lo[:, ks, :], in0=merged[:, ks, :], scalar=0.5,
                                                   in1=hS_hi[:, ks, :].bitcast(F32), op0=ALU.mult, op1=ALU.subtract).then_inc(mlo_ready, 1)
                with dve.Fori(0, 2) as w:
                    for s in range(SLOTS):
                        ahead(split_lo, dve, G + 18 + w, s)
                        dve.wait_ge(blk_done, SLOTS + 4 * (G + 18 + w) + s + 1)
                        xt = xS[:, bass.ds(4 * w + s, 1), :].rearrange("p a n -> p (a n)")
                        nc.vector.tensor_tensor(xt, stream_ps[s][:, 0:S], xt, ALU.add).then_inc(dve_evac, 1)
            dve.wait_ge(rstd_ready, 2 + LAYERS)
            for half in range(2):
                scale_rows(dve, xS, xS, gain_col(G_FINAL), half, n32_ready)

            def split_norm(i, gain, at):
                dve.wait_ge(rstd_ready, i + 1)
                for half in range(2):
                    scale_rows(dve, h32t, xT, gain_col(gain), half, n32_ready)
                for half in range(2):
                    dve.wait_ge(nhi_ready, at + half + 1)
                    ks = slice(4 * half, 4 * half + 4)
                    nc.vector.tensor_tensor(h_lo[:, ks, :], h32t[:, ks, :], h_hi[:, ks, :].bitcast(F32),
                                            ALU.subtract).then_inc(nlo_ready, 1)

            split_norm(2 + LAYERS, G_NORM1, 2 * LAYERS)
            dve.wait_ge(th_ready, 1)
            dve.wait_ge(wba_in, 32)
            ba = free_ps[1][:, 0:STEPS * 2 * DN].rearrange("p (t n) -> p t n", t=STEPS)
            nc.vector.tensor_tensor(dt_u[:, :, :], ba[:, :, DN:], adt[:, DN:].unsqueeze(1).broadcast_to([P, STEPS, DN]), ALU.add)
            nc.vector.drain()
            nc.vector.scalar_tensor_tensor(out=sp[:, :, :], in0=dt_u[:, :, :], scalar=-1.0, in1=dt_u[:, :, :], op0=ALU.mult,
                                           op1=ALU.min).then_inc(u_ready, 1)
            nc.vector.tensor_scalar(beta_t[:, :, :], beta_t[:, :, :], 1.0, 0.5, ALU.add, ALU.mult)
            nc.vector.drain()
            dve.wait_ge(ewu_ready, 1)
            nc.vector.scalar_tensor_tensor(out=sp[:, :, :], in0=dt_u[:, :, :], scalar=0.0, in1=sp[:, :, :], op0=ALU.max, op1=ALU.add)
            nc.vector.drain()
            nc.vector.scalar_tensor_tensor(out=log_decay[:, :, :], in0=sp[:, :, :], scalar=-1.0,
                                           in1=ea[:, :].unsqueeze(1).broadcast_to([P, STEPS, DN]),
                                           op0=ALU.mult, op1=ALU.mult).then_inc(g_ready, 1)

            def qkv_taps(i):
                for n in range(0, KT, 2):
                    for m in (n, n + 1):
                        ahead(split_lo, dve, G2 + 2 * i + m // SLOTS, m % SLOTS)
                    dve.wait_ge(act_evac, SLOTS + E2 + 8 * i + n + 2)
                    for tap in (0, 1, 3, 4):
                        for m in (n, n + 1):
                            acc = qkvT[:, bass.ds(i, 1), m, PADS:].rearrange("p a n -> p (a n)")
                            op = nc.vector.scalar_tensor_tensor(out=acc, in0=st_raw[:, m % SLOTS, tap:tap + T],
                                                                scalar=gains[:, bass.ds(G_CONV + 40 * i + 5 * m + tap, 1)],
                                                                in1=acc, op0=ALU.mult, op1=ALU.add)
                            if tap == 4:
                                op.then_inc(conv_done, 1)
                        if tap < 4:
                            nc.vector.drain()

            dve.wait_ge(zeros_ready, 1)
            qkv_taps(0)
            dve.wait_ge(gsum_ready, 1)
            factor = lambda i, rows=slice(0, P): scal[rows, :, i * DN:(i + 1) * DN]
            f_rows, b_rows = slice(0, C), slice(C, P)
            dirs = ((0, f_rows), (1, b_rows))
            nc.vector.tensor_copy(factor(0), beta_t[:, :, :])
            for i, own, other in ((1, f_rows, b_rows), (2, b_rows, f_rows)):
                nc.vector.scalar_tensor_tensor(out=factor(i, own), in0=beta_t[own, :, :], scalar=-1.0, in1=exg[own, 0, :, :],
                                               op0=ALU.mult, op1=ALU.mult)
                nc.vector.tensor_copy(factor(i, other), exg[other, 1, :, :])
            for i in range(3):
                op = nc.vector.tensor_copy(factor(3 + i), exg[:, 2 + i, :, :])
            op.then_inc(scal_ready, 1)
            for t in range(STEPS):
                steps = slice(t * DN, (t + 1) * DN)
                dve.wait_ge(e_done, t + 1)
                nc.vector.tensor_tensor(decay[:, steps, :], e_bank[t][:, :].rearrange("p (h c) -> p h c", h=DN),
                                        gcol[:, steps].unsqueeze(2).broadcast_to([P, DN, C]), ALU.subtract).then_inc(e_used, 1)
            with dve.Fori(1, 3) as i:
                qkv_taps(i)

            def unit(j, s):
                ahead(split_lo, dve, G_U + j, s)
                x = lambda at: cx[:, bass.ds(j, 1), at:at + T].rearrange("p a n -> p (a n)")
                acc = bcv[:, 0, :]
                if s == 1:
                    dve.wait_ge(act_evac, SLOTS + E2 + 24 + 2 * j + 1)
                    dve.wait_ge(blk_done, SLOTS + 4 * (G_U + j) + s + 1)
                    nc.vector.tensor_tensor(x(1), stream_ps[s % 2][:, 0:T], x(1), ALU.mult).then_inc(dve_evac, 1)
                if s == 2:
                    nc.vector.drain()
                    nc.vector.tensor_scalar(acc, x(0), gains[:, bass.ds(G_SC + 3 * j, 1)], None, ALU.mult)
                    for tap in (1, 2):
                        nc.vector.drain()
                        nc.vector.scalar_tensor_tensor(out=acc, in0=x(tap), scalar=gains[:, bass.ds(G_SC + 3 * j + tap, 1)], in1=acc,
                                                       op0=ALU.mult, op1=ALU.add)
                    nc.vector.drain()
                    dve.wait_ge(blk_done, SLOTS + 4 * (G_U + j) + s + 1)
                    nc.vector.tensor_tensor(x(1), stream_ps[s % 2][:, 0:T], acc, ALU.mult).then_inc(dve_evac, 1)

            for n in range(4):
                unit(0, n)
            for i, inv in enumerate((wide, k_sq)):
                x = qkvT[:, i, :, PADS:]
                dve.wait_ge(l2rs_ready, i + 1)
                nc.vector.scalar_tensor_tensor(out=x, in0=x, scalar=DN_SCALE if i == 0 else 1.0, in1=inv[:, :, :],
                                               op0=ALU.mult, op1=ALU.mult).then_inc(l2_ready, 1)
            for m in range(4, 4 * (UNITS - STEPS)):
                unit(m // 4, m % 4)
            nc.vector.memset(oT[:, :, :], 0.0)
            dve.sem_inc(o_used, 2)
            dve.sem_inc(r_ready, 1)
            dve.sem_inc(s_ready, 2)
            dve.wait_ge(decay_ready, 1)
            with dve.Fori(0, STEPS) as t:
                j = UNITS - STEPS + t
                unit(j, 0)
                for half in range(2):
                    hs = slice(4 * half, 4 * half + 4)
                    kkq = bank[half][0][:, :].rearrange("p (h i c) -> p h i c", h=4, i=2)
                    dve.wait_ge(kkq_done, 2 * t + half + 1)
                    for d, rows in dirs:
                        dec = decay[rows, bass.ds(DN * t + 4 * half, 4), :]
                        nc.vector.tensor_tensor(lvl[rows, 0, hs, :], kkq[rows, :, d, :], dec, ALU.mult)
                        op = nc.vector.tensor_tensor(at[rows, d, hs, :], kkq[rows, :, 1 - d, :], dec, ALU.mult)
                    op.then_inc(kkq_used, 1)
                for half in range(2):
                    hs = slice(4 * half, 4 * half + 4)
                    dve.wait_ge(ks_done, 2 * t + half + 1)
                    for d in range(2):
                        c = (1 + d) * DN + 4 * half
                        nc.vector.tensor_tensor(vo[:, d, hs, :], bank[half][d][:, :].rearrange("p (h n) -> p h n", h=4),
                                                sc[:, c:c + 4].unsqueeze(2).broadcast_to([P, 4, P]), ALU.mult)
                    nc.vector.drain()
                    dve.wait_ge(vk_used, 2 * t + half + 2)
                    for d, rows in dirs:
                        op = nc.vector.tensor_tensor(vb[rows, hs, :], vb[rows, hs, :], vo[rows, d, hs, :], ALU.add)
                    op.then_inc(r_ready, 1)
                unit(j, 1)
                eye4 = eye_c.unsqueeze(1).broadcast_to([P, 4, C])
                for half in range(2):
                    dve.wait_ge(n1_done, 12 * t + half + 1)
                    nc.vector.tensor_tensor(xy[:, half, 0, :, :], eye4, bank[half][2][:, 0:4 * C].rearrange("p (h c) -> p h c", h=4), ALU.subtract)
                    nc.vector.tensor_tensor(xy[:, half, 1, :, :], eye4, lvl[:, lvl_slot(0), 4 * half:4 * half + 4, :], ALU.subtract).then_inc(yx_ready, 1)
                for level in range(1, LEVELS):
                    m = 1 << level
                    sides = 2 if level < LEVELS - 1 else 1
                    for half in range(2):
                        dve.wait_ge(yx_done, 10 * t + 2 * (level - 1) + half + 1)
                        for d, rows in dirs:
                            for side in range(sides):
                                part = xy[rows, half, side, :, :].rearrange("p h (b i m) -> p (h b) i m", i=2, m=m)[:, :, (1 + d + side) % 2, :]
                                src = bank[half][2][rows, (1 + side) * 2 * C:(2 + side) * 2 * C].rearrange("p (n m) -> p n m", m=m)
                                op = nc.vector.tensor_tensor(part, part, src, ALU.subtract)
                        op.then_inc(yx_ready, 1)
                    if level == 2:
                        unit(j, 2)
                unit(j, 3)
                for half in range(2):
                    hs = slice(4 * half, 4 * half + 4)
                    dve.wait_ge(o_done, 2 * t + half + 1)
                    for d, at_tok in ((0, C * t), (1, C * (STEPS - 1) - C * t)):
                        o = oT[:, hs, bass.ds(at_tok, C)]
                        op = nc.vector.tensor_tensor(o, o, bank[half][1][:, d * 4 * C:(d + 1) * 4 * C].rearrange("p (h c) -> p h c", h=4), ALU.add)
                        if d == 0:
                            nc.vector.drain()
                    op.then_inc(o_used, 1)
                for half in range(2):
                    hs = slice(4 * half, 4 * half + 4)
                    dve.wait_ge(su_done, 2 + 2 * t + half + 1)
                    dve.wait_ge(sdec_ready, 2 * t + half + 1)
                    for d in range(2):
                        op = nc.vector.tensor_tensor(state[:, d, hs, :], state[:, d, hs, :],
                                                     bank[half][2 - 2 * d][:, :].rearrange("p (h n) -> p h n", h=4), ALU.add)
                    op.then_inc(s_ready, 1)
            for w in range(4):
                for s in range(SLOTS):
                    ahead(split_lo, dve, G_GATE + w, s)
                if w == 2:
                    dve.wait_ge(ors_ready, 1)
                    for half in range(2):
                        o, hs = oT[:, 4 * half:4 * half + 4, PADS:], slice(4 * half, 4 * half + 4)
                        nc.vector.scalar_tensor_tensor(out=o, in0=o, scalar=gains[:, G_DN:G_DN + 1], in1=wide[:, hs, :], op0=ALU.mult, op1=ALU.mult)
                        nc.vector.drain()
                        op = nc.vector.tensor_tensor(o, o, sz[:, hs, :], ALU.mult)
                    op.then_inc(yd_ready, 1)
                if w == 3:
                    dve.wait_ge(yshi_ready, 1)
                    nc.vector.tensor_tensor(ys_lo[:, :, :], cx[:, :, 1:T + 1], ys_hi[:, :, :].bitcast(F32), ALU.subtract).then_inc(yslo_ready, 1)
            for i, gate in enumerate((gb, ga)):
                with dve.Fori(0, 2) as w:
                    for s in range(SLOTS):
                        ahead(split_lo, dve, G_BR + 2 * i + w, s)
                        k = bass.ds(4 * w + s, 1)
                        part, merge = (x[:, k, :].rearrange("p a n -> p (a n)") for x in (gate, wide))
                        dve.wait_ge(blk_done, SLOTS + 4 * (G_BR + 2 * i + w) + s + 1)
                        op = nc.vector.scalar_tensor_tensor(out=part if i else merge, in0=part, scalar=1.0, in1=stream_ps[s][:, 0:T],
                                                            op0=ALU.add, op1=ALU.mult)
                        if i:
                            nc.vector.drain()
                            op = nc.vector.tensor_tensor(merge, merge, part, ALU.add)
                        op.then_inc(dve_evac, 1)
                if i == 0:
                    dve.wait_ge(ydhi_ready, 1)
                    nc.vector.tensor_tensor(yd_lo[:, :, :], oT[:, :, PADS:], yd_hi[:, :, :].bitcast(F32), ALU.subtract).then_inc(ydlo_ready, 1)
            for half in range(2):
                dve.wait_ge(mhi_ready, 2 * LAYERS + half + 1)
                ks = slice(4 * half, 4 * half + 4)
                nc.vector.scalar_tensor_tensor(out=h_lo[:, ks, :], in0=wide[:, ks, :], scalar=0.5, in1=h_hi[:, ks, :].bitcast(F32),
                                               op0=ALU.mult, op1=ALU.subtract).then_inc(mlo_ready, 1)
            dve.wait_ge(x_back, 16)
            with dve.Fori(0, 2) as w:
                for s in range(SLOTS):
                    ahead(split_lo, dve, G_WO + w, s)
                    dve.wait_ge(blk_done, SLOTS + 4 * (G_WO + w) + s + 1)
                    xt = xT[:, bass.ds(4 * w + s, 1), :].rearrange("p a n -> p (a n)")
                    nc.vector.tensor_tensor(xt, stream_ps[s][:, 0:T], xt, ALU.add).then_inc(dve_evac, 1)
            split_norm(3 + LAYERS, G_NORM2, 2 * LAYERS + 2)
            with dve.Fori(0, FT // 2) as w:
                for s in range(SLOTS):
                    ahead(split_lo, dve, G_GU + w, s)
                    if s % 2 == 1:
                        f = bass.ds(2 * w + s // 2, 1)
                        dve.wait_ge(blk_done, SLOTS + 4 * (G_GU + w) + s + 1)
                        dve.wait_ge(fact_ready, 2 * w + s // 2 + 1)
                        nc.vector.tensor_tensor(f_val[:, s // 2, :], stream_ps[s][:, 0:T], f_act[:, s // 2, :], ALU.mult).then_inc(dve_evac, 2)
                        dve.wait_ge(fhi_ready, 2 * w + s // 2 + 1)
                        nc.vector.tensor_tensor(f_lo[:, f, :].rearrange("p a n -> p (a n)"), f_val[:, s // 2, :],
                                                f_hi[:, f, :].rearrange("p a n -> p (a n)").bitcast(F32), ALU.subtract).then_inc(flo_ready, 1)
            with dve.Fori(0, 2) as w:
                for n in range(12):
                    ahead(split_lo, dve, G_DOWN + 3 * w + n // SLOTS, n % SLOTS)
                    if n % 3 == 2:
                        dve.wait_ge(blk_done, SLOTS + 4 * G_DOWN + 12 * w + n + 1)
                        xt = xT[:, bass.ds(4 * w + n // 3, 1), :].rearrange("p a n -> p (a n)")
                        nc.vector.tensor_tensor(xt, stream_ps[n // 3][:, 0:T], xt, ALU.add).then_inc(dve_evac, 1)
            dve.wait_ge(rstd_ready, 5 + LAYERS)
            for half in range(2):
                scale_rows(dve, h32t, xT, gain_col(G_FINAL2), half, n32_ready)

        @block.tensor
        def _(pe):
            pe.sem_inc(blk_done, SLOTS)
            pe.sem_inc(logit_done, 1)
            pe.sem_inc(pv_done, 1)
            pe.wait_ge(cst_in, 16)
            sum_squares(pe, mem_f, 0, 0)
            pe.wait_ge(rel_in, 32)
            nc.tensor.matmul(free_ps[1][0:HEADS, :], rel_sb[:, :], bucket_hot, start=True, stop=True).then_inc(relf_done, 1)
            for l in range(LAYERS):
                for s in range(SLOTS):
                    block_cols(pe, 2 * l, s, act_evac, 8 * l + s + 1, mem_hi[l], mem_lo[l], (memlo_ready, 2 * l + 1) if s == 0 else None)
                for s in (0, 2):
                    block_rows(pe, 2 * l + 1, s, act_evac, 8 * l + 4 + s + 1, mem_hi[l], mem_lo[l])
            pe.wait_ge(hankel_in, 16)
            pe.wait_ge(relf_ready, 1)
            pe.wait_ge(rstd_ready, 1)
            for h in range(HEADS):
                if h >= 4:
                    pe.wait_ge(bias_ready, h - 3)
                nc.tensor.matmul(free_ps[h % 4][:, 0:S], flip, hankel[:, h, :], start=True, stop=True).then_inc(flip_done, 1)
            pe.wait_ge(bias_ready, HEADS)
            pe.wait_ge(ident_ready, 1)

            with pe.Fori(0, LAYERS) as l:
                G = G0 + LAYER_GROUPS * l
                E = 4 * MEM_GROUPS + ACT_EVACS * l
                pe.wait_ge(pv_used, 6 * l + 1)
                sum_squares(pe, wideS, 1 + l, 8 + 8 * l)
                pe.wait_ge(wik_in, 16 * (l + 1))
                for k in range(KT):
                    if k % 4 == 0:
                        pe.wait_ge(n32_ready, 2 * l + k // 4 + 1)
                    nc.tensor.matmul(free_ps[1][:, 0:S], wik[:, k, 0:P], h32[:, k, :], start=k == 0, stop=k == KT - 1)
                for t in range(2):
                    for k in range(KT):
                        mm = nc.tensor.matmul(free_ps[2][:, t * HEADS:(t + 1) * HEADS], h32[:, k, t * P:(t + 1) * P],
                                              wik[:, k, P:P + HEADS], start=k == 0, stop=k == KT - 1)
                mm.then_inc(ikw_done, 1)
                pe.wait_ge(dve_evac, SLOTS + DVE_EVACS * l)
                for s in range(SLOTS):
                    block_cols(pe, G, s, act_evac, E + s + 1, hS_hi, hS_lo, (nlo_ready, 2 * l + 1) if s == 0 else None)
                for s in range(SLOTS):
                    block_cols(pe, G + 1, s, act_evac, E + 4 + s + 1, hS_hi, hS_lo)

                def index_products(h):
                    rows, q = slice(HD * (h % 2), HD * (h % 2) + HD), iqT[:, h // 2, :]
                    nc.tensor.matmul(free_ps[h % 4][:, 0:P], q[rows, 0:P], ikT[rows, 0:P], start=True, stop=True)
                    nc.tensor.matmul(free_ps[h % 4][:, P:3 * P], q[rows, P:S], ikT[rows, :], start=True, stop=True).then_inc(idx_done, 1)

                pe.wait_ge(ikw_ready, l + 1)
                pe.wait_ge(act_evac, SLOTS + E + 4)
                for h in range(4):
                    index_products(h)
                for s in range(SLOTS):
                    block_cols(pe, G + 2, s, act_evac, E + 8 + s + 1, hS_hi, hS_lo)
                for h in range(4, HEADS):
                    pe.wait_ge(idx_relu, HEADS * l + h - 3)
                    index_products(h)
                for s in (0, 2):
                    block_rows(pe, G + 3, s, act_evac, E + 12 + s + 1, hS_hi, hS_lo)
                with pe.Fori(0, 5) as g:
                    for s in range(SLOTS):
                        block_cols(pe, G + 4 + g, s, act_evac, E + 16 + 4 * g + s + 1, hS_hi, hS_lo)
                with pe.Fori(0, 4) as hp:
                    pe.wait_ge(mask_ready, l + 1)
                    pe.wait_ge(idx_relu, HEADS * (l + 1))
                    pe.wait_ge(qk_staged, 6 * l + hp + 1)
                    pe.wait_ge(pv_used, 6 * l + hp + 1)
                    for j in range(2):
                        rows = slice(HD * j, HD * j + HD)
                        nc.tensor.matmul(free_ps[j][:, 0:P], st_q[rows, 0:P], st_k[rows, 0:P], start=True, stop=False)
                        nc.tensor.matmul(free_ps[j][:, 0:P], ident_bf[:, :], mask[:, 0:P], start=False, stop=True)
                        nc.tensor.matmul(free_ps[j][:, P:3 * P], st_q[rows, P:S], st_k[rows, :], start=True, stop=False)
                        mm = nc.tensor.matmul(free_ps[j][:, P:3 * P], ident_bf[:, :], mask[:, P:3 * P], start=False, stop=True)
                    mm.then_inc(logit_done, 1)
                    for s in range(SLOTS):
                        block_cols(pe, G + 9 + hp, s, act_evac, E + 36 + 4 * hp + s + 1, hS_hi, hS_lo)
                        if s == 2:
                            pe.wait_ge(prob_ready, 6 * l + hp + 1)
                            for j in range(2):
                                for c in range(3):
                                    mm = nc.tensor.transpose(free_ps[2 + j][:, c * P:(c + 1) * P], soft[:, j, c * P:(c + 1) * P], ident)
                            mm.then_inc(softT_done, 1)
                    pe.wait_ge(softT_ready, 6 * l + hp + 1)
                    pe.wait_ge(v_staged, 6 * l + hp + 1)
                    for j in range(2):
                        o, vc = free_ps[0][HD * j:HD * j + HD, :], slice(HD * j, HD * j + HD)
                        nc.tensor.matmul(o[:, 0:P], st_v[:, 0, vc], softT[:, j, 0:P], start=True, stop=True)
                        nc.tensor.matmul(o[:, P:S], st_v[:, 0, vc], softT[:, j, P:2 * P], start=True, stop=False)
                        mm = nc.tensor.matmul(o[:, P:S], st_v[:, 1, vc], softT[:, j, 2 * P:3 * P], start=False, stop=True)
                    mm.then_inc(pv_done, 1)
                pe.wait_ge(pooled_ready, l + 1)
                pe.wait_ge(poolw_in, 16 * (l + 1))
                for g in range(POOLG):
                    mm = nc.tensor.matmul(free_ps[2 + g // 2][:, (g % 2) * S:(g % 2 + 1) * S], pool_w[:, g, :], pu[:, g, PAD:],
                                          start=True, stop=True)
                mm.then_inc(mixed_done, 1)
                with pe.Fori(0, 2) as mp:
                    pe.wait_ge(qk_staged, 6 * l + 4 + mp + 1)
                    pe.wait_ge(pv_used, 6 * l + 4 + mp + 1)
                    for j in range(2):
                        for t in range(2):
                            mm = nc.tensor.matmul(free_ps[j][:, t * S:(t + 1) * S], st_mq[:, j, t * P:(t + 1) * P],
                                                  mkT[:, bass.ds(4 * l + 2 * mp + j, 1), :].rearrange("p a n -> p (a n)"), start=True, stop=True)
                    mm.then_inc(logit_done, 1)
                    for s in range(SLOTS):
                        block_cols(pe, G + 13 + mp, s, act_evac, E + 52 + 4 * mp + s + 1, hS_hi, hS_lo)
                        if s == 2:
                            pe.wait_ge(prob_ready, 6 * l + 4 + mp + 1)
                            pe.wait_ge(mixed_used, l + 2)
                            for j in range(2):
                                for c in range(4):
                                    mm = nc.tensor.transpose(free_ps[2 + j][:, c * P:(c + 1) * P], soft[:, j, c * P:(c + 1) * P], ident)
                            mm.then_inc(softT_done, 1)
                    pe.wait_ge(softT_ready, 6 * l + 4 + mp + 1)
                    pe.wait_ge(v_staged, 6 * l + 4 + mp + 1)
                    for j in range(2):
                        for t in range(2):
                            o = free_ps[0][:, j * S + t * P:j * S + (t + 1) * P]
                            for m in range(2):
                                mm = nc.tensor.matmul(o, st_mv[:, m, j * P:(j + 1) * P], softT[:, j, (2 * t + m) * P:(2 * t + m + 1) * P],
                                                      start=m == 0, stop=m == 1)
                    mm.then_inc(pv_done, 1)
                with pe.Fori(0, 3) as br:
                    pe.wait_ge(act_evac, SLOTS + E + ACT_EVACS)
                    pe.wait_ge(mixed_used, l + 2)
                    pe.wait_ge(y_ready, 6 * l + 6)
                    for s in range(SLOTS):
                        pe.wait_ge(lo_ready, 4 * (G + 15 + br) + s + 1 + SLOTS)
                        pe.wait_ge(dve_evac, DVE_EVACS * l + 4 * br + s + 1)
                        for c in range(2):
                            for k in range(4):
                                y = (y_hi[:, bass.ds(br, 1), k, :].rearrange("p a n -> p (a n)"),
                                     y_lo[:, bass.ds(br, 1), k, :].rearrange("p a n -> p (a n)"))
                                mm = mm3(stream_ps[s][:, c * S:(c + 1) * S], w_hi[s][:, 4 * c + k, :], w_lo[s][:, 4 * c + k, :],
                                         *y, k == 0, k == 3)
                        mm.then_inc(blk_done, 1)
                with pe.Fori(0, 2) as w:
                    pe.wait_ge(mlo_ready, 2 * l + 2)
                    for s in range(SLOTS):
                        block_cols(pe, G + 18 + w, s, dve_evac, DVE_EVACS * l + 12 + 4 * w + s + 1, hS_hi, hS_lo)
            sum_squares(pe, wideS, 1 + LAYERS, 8 + 8 * LAYERS)
            sum_squares(pe, wide, 2 + LAYERS, 16 + 8 * LAYERS)
            pe.wait_ge(n32_ready, 2 * LAYERS + 4)
            pe.wait_ge(zeros_ready, 1)
            pe.wait_ge(wba_in, 32)
            for t in range(STEPS):
                for d, chunk in ((0, t), (1, STEPS - 1 - t)):
                    for k in range(KT):
                        mm = nc.tensor.matmul(free_ps[1][d * C:(d + 1) * C, t * 2 * DN:(t + 1) * 2 * DN], h32p[:, k, chunk * C:(chunk + 1) * C],
                                              wba[:, k, d * 2 * DN:(d + 1) * 2 * DN], start=k == 0, stop=k == KT - 1)
            mm.then_inc(ba_done, 1)
            pe.wait_ge(dve_evac, SLOTS + D2)

            def qkv(G):
                for s in range(SLOTS):
                    block_cols(pe, G, s, act_evac, E2 + 4 * (G - G2) + s + 1, h_hi, h_lo, (nlo_ready, 2 * LAYERS + 1) if G is G2 and s == 0 else None)

            for w in range(2):
                qkv(G2 + w)
            pe.wait_ge(g_ready, 1)
            pe.wait_ge(c2_in, 16)
            for i, m in enumerate((tri, tri_swap, after, rows_f, rows_b)):
                mm = nc.tensor.matmul(free_ps[2][:, i * STEPS * DN:(i + 1) * STEPS * DN], m,
                                      log_decay[:, :, :].rearrange("p t h -> p (t h)"), start=True, stop=True)
            mm.then_inc(gsum_done, 1)
            pe.wait_ge(gd_ready, 1)
            for t in range(STEPS):
                if t == 3:
                    pe.wait_ge(gsum_ready, 1)
                if t == 4:
                    pe.wait_ge(e_used, 1)
                nc.tensor.matmul(e_bank[t][:, :], same, decay[:, t * DN:(t + 1) * DN, :], start=True, stop=True).then_inc(e_done, 1)
            for w in range(2, 6):
                qkv(G2 + w)

            def unit(j, s):
                pe.wait_ge(lo_ready, 4 * (G_U + j) + s + 1 + SLOTS)
                if s in (1, 2):
                    pe.wait_ge(act_evac, SLOTS + E2 + 24 + 2 * j + s - 1)
                else:
                    pe.wait_ge(dve_evac, SLOTS + D2 + 2 * j + s // 3)
                for k in range(KT):
                    mm = mm3(stream_ps[s % 2][:, 0:T], w_hi[s][:, k, :], w_lo[s][:, k, :], h_hi[:, k, :], h_lo[:, k, :],
                             k == 0, k == KT - 1)
                mm.then_inc(blk_done, 1)

            pe.wait_ge(e_used, STEPS)
            pe.wait_ge(act_evac, SLOTS + E2 + 24)
            for n in range(4):
                pe.wait_ge(l2sq_ready, n + 1)
                if n:
                    pe.wait_ge(l2_used, n)
                for j in range(4):
                    mm = nc.tensor.matmul(free_ps[j][:, 0:T], ones, (wide, k_sq)[n // 2][:, 4 * (n % 2) + j, :], start=True, stop=True)
                mm.then_inc(l2_done, 1)
                for m in range(n, n + 1 if n < 3 else 4 * (UNITS - STEPS)):
                    unit(m // 4, m % 4)
            pe.wait_ge(l2_used, 4)
            pe.sem_inc(su_done, 2)
            with pe.Fori(0, STEPS) as t:
                tile = UNITS - STEPS + t
                f_rows, b_rows = slice(0, C), slice(C, P)
                dirs = ((0, f_rows), (1, b_rows))
                heads = [(j, slice(j * P, (j + 1) * P), slice(j * C, (j + 1) * C)) for j in range(4)]
                flat = lambda x: x.rearrange("p i c -> p (i c)")
                unit(tile, 0)
                for half in range(2):
                    pe.wait_ge(dn_staged, t + 1)
                    pe.wait_ge(s_ready, 2 * t + half + 1)
                    for j, wide_j, _ in heads:
                        for rows, key, kq in ((f_rows, 4, slice(4, 6)), (b_rows, 3, slice(2, 4))):
                            mm = nc.tensor.matmul(bank[half][0][rows, wide_j], kqs[:, 4 * half + j, key, :],
                                                  flat(kqs[:, 4 * half + j, kq, :]), start=True, stop=True)
                    mm.then_inc(kkq_done, 1)
                for half in range(2):
                    pe.wait_ge(dnv_staged, t + 1)
                    pe.wait_ge(o_used, 2 * t + half + 1)
                    for j, wide_j, _ in heads:
                        h = 4 * half + j
                        nc.tensor.transpose(bank[half][1][:, wide_j], flat(vs[:, h, :, :]), ident)
                        mm = nc.tensor.transpose(bank[half][2][:, wide_j], flat(kqs[:, h, 0:2, :]), ident)
                    mm.then_inc(vk_done, 1)
                for half in range(2):
                    pe.wait_ge(kkq_used, 2 * t + half + 1)
                    pe.wait_ge(vk_used, 2 * t + half + 2)
                    for j, wide_j, _ in heads:
                        h = 4 * half + j
                        nc.tensor.matmul(bank[half][0][:, wide_j], flat(kqs[:, h, 4:6, :]), state[:, 0, h, :], start=True, stop=True)
                        mm = nc.tensor.matmul(bank[half][1][:, wide_j], flat(kqs[:, h, 2:4, :]), state[:, 1, h, :], start=True, stop=True)
                    mm.then_inc(ks_done, 1)
                unit(tile, 1)
                for level in range(LEVELS):
                    m = 1 << level
                    later = lambda x, d: x.rearrange("p (b i m) -> p b i m", i=2, m=m)[:, :, 1 - d, :]
                    earlier = lambda x, d: x.rearrange("p (b i m) -> p b i m", i=2, m=m)[:, :, d, :]
                    packed = lambda x: x.rearrange("p (b m) -> p b m", m=m)
                    for half in range(2):
                        pe.wait_ge(lvl_ready, 12 * t + 2 * level + half + 1)
                        if level == 0:
                            pe.wait_ge(vk_used, 2 * t + half + 2)
                        else:
                            pe.wait_ge(yx_ready, 12 * t + 2 * (level - 1) + half + 1)
                        pe.sem_inc(held, 1)
                        for j, _, c in heads:
                            for d, rows in dirs:
                                l = lvl[rows, lvl_slot(level), 4 * half + j, :]
                                if level == 0:
                                    mm = nc.tensor.matmul(bank[half][2][rows, c], l, eye_c[rows, :], start=True, stop=True)
                                else:
                                    mm = nc.tensor.matmul(packed(bank[half][2][rows, j * 32:(j + 1) * 32]), l, later(xy[rows, half, 0, j, :], d),
                                                          start=True, stop=True)
                        mm.then_inc(n1_done, 1)
                    for half in range(2 if level else 0):
                        pe.wait_ge(n1_ready, 10 * t + 2 * (level - 1) + half + 1)
                        pe.sem_inc(held, 1)
                        for j, _, c in heads:
                            for d, rows in dirs:
                                x = xy[rows, half, 1, j, :]
                                at_y, at_x = (bank[half][2][rows, i * 2 * C + j * 32:i * 2 * C + (j + 1) * 32] for i in (1, 2))
                                if level == LEVELS - 1:
                                    mm = nc.tensor.matmul(at_y, x, n1_last[rows, half, j, :], start=True, stop=True)
                                else:
                                    n = n1[level - 1][rows, half, j, :]
                                    nc.tensor.matmul(packed(at_y), x, later(n, d), start=True, stop=True)
                                    mm = nc.tensor.matmul(packed(at_x), n, earlier(x, d), start=True, stop=True)
                        mm.then_inc(yx_done, 1)
                    if level == 2:
                        unit(tile, 2)
                for half in range(2):
                    pe.wait_ge(yx_ready, 12 * t + 2 * (LEVELS - 1) + half + 1)
                    pe.wait_ge(r_ready, 2 * t + half + 2)
                    pe.sem_inc(held, 1)
                    for j, wide_j, _ in heads:
                        for d, rows in dirs:
                            mm = nc.tensor.matmul(bank[half][0][rows, wide_j], xy[rows, half, 0, j, :], vb[rows, 4 * half + j, :], start=True, stop=True)
                    mm.then_inc(vnew_done, 1)
                unit(tile, 3)
                for half in range(2):
                    pe.wait_ge(vnew_ready, 2 * t + half + 1)
                    pe.wait_ge(at_ready, 2 * t + half + 1)
                    for j, _, c in heads:
                        for d, rows in dirs:
                            mm = nc.tensor.matmul(bank[half][1][:, d * 4 * C + c.start:d * 4 * C + c.stop], vo[:, d, 4 * half + j, :],
                                                  at[:, d, 4 * half + j, :], start=True, stop=True)
                    mm.then_inc(o_done, 1)
                for half in range(2):
                    for j, wide_j, _ in heads:
                        for d, rows in dirs:
                            mm = nc.tensor.matmul(bank[half][2 - 2 * d][:, wide_j], kdec[rows, 4 * half + j, :], vo[rows, d, 4 * half + j, :],
                                                  start=True, stop=True)
                    mm.then_inc(su_done, 1)
            pe.wait_ge(s_ready, 2 + 2 * STEPS)
            pe.wait_ge(o_used, 2 + 2 * STEPS)
            pe.wait_ge(dve_evac, SLOTS + D2 + 16)
            pe.wait_ge(act_evac, SLOTS + E2 + 40)
            for w in range(4):
                for s in range(SLOTS):
                    block_cols(pe, G_GATE + w, s, act_evac, E2 + 40 + 4 * w + s + 1, h_hi, h_lo)
                if w < 2:
                    pe.wait_ge(osq_ready, 4 * w + 4)
                    if w:
                        pe.wait_ge(oss_used, w)
                    for j in range(4):
                        mm = nc.tensor.matmul(free_ps[j][:, 0:T], ones, wide[:, 4 * w + j, :], start=True, stop=True)
                    mm.then_inc(oss_done, 1)
            pe.wait_ge(act_evac, SLOTS + E2 + 56)
            for i, (y_ok, hi, lo) in enumerate(((yslo_ready, ys_hi, ys_lo), (ydlo_ready, yd_hi, yd_lo))):
                pe.wait_ge(y_ok, 1)
                with pe.Fori(0, 2) as w:
                    for s in range(SLOTS):
                        block_cols(pe, G_BR + 2 * i + w, s, dve_evac, D2 + 16 + 8 * i + 4 * w + s + 1, hi, lo)
            pe.wait_ge(mlo_ready, 2 * LAYERS + 2)
            with pe.Fori(0, 2) as w:
                for s in range(SLOTS):
                    block_cols(pe, G_WO + w, s, dve_evac, D2 + 32 + 4 * w + s + 1, h_hi, h_lo)
            sum_squares(pe, wide, 3 + LAYERS, 24 + 8 * LAYERS)
            pe.wait_ge(nlo_ready, 2 * LAYERS + 4)
            with pe.Fori(0, FT // 2) as w:
                for s in range(SLOTS):
                    block_cols(pe, G_GU + w, s, dve_evac, D2 + 40 + 4 * w + s + 1, h_hi, h_lo)
            pe.wait_ge(flo_ready, FT)
            with pe.Fori(0, 2) as w:
                for n in range(12):
                    c, s = n // 3, n % SLOTS
                    pe.wait_ge(lo_ready, 4 * G_DOWN + 12 * w + n + 1 + SLOTS)
                    if n % 3 == 0:
                        pe.wait_ge(dve_evac, D2 + 84 + 4 * w + c + 1)
                    for k in range(min(KT, FT - KT * (n % 3))):
                        kf = KT * (n % 3) + k
                        mm = mm3(stream_ps[c][:, 0:T], w_hi[s][:, k, :], w_lo[s][:, k, :], f_hi[:, kf, :], f_lo[:, kf, :],
                                 kf == 0, kf == FT - 1)
                    mm.then_inc(blk_done, 1)
            sum_squares(pe, wide, 4 + LAYERS, 32 + 8 * LAYERS)


def rel_buckets():
    n = np.abs(np.arange(512) - 255)
    pos = np.arange(512) > 255
    large = 8 + (np.log(np.maximum(n, 1).astype(np.float32) / 8) / math.log(128) * 8).astype(np.int32)
    b = np.where(pos, 16, 0) + np.where(n < 8, n, np.minimum(large, 15))
    return (b[None, :] == np.arange(32)[:, None]).astype(np.float32)


def constants_first():
    cst = np.concatenate([np.eye(P), np.ones((P, P))], 1).astype(np.float32)
    rel = np.zeros((P, P + 512), np.float32)
    rel[:, 0:P] = np.eye(P)[::-1]
    rel[0:32, P:] = rel_buckets()
    q, s = np.arange(P)[:, None], np.arange(S)[None, :]
    admit = np.concatenate([np.where(s[:, 0:P] < (q // 64 + 1) * 64, 0.0, NEG),
                            np.where(s < ((q + P) // 64 + 1) * 64, 0.0, NEG)], 1)
    edge = [1.0 / np.minimum(np.arange(16) + 1, w) for w in POOL_WINDOWS]
    admit = np.concatenate([admit, np.broadcast_to(np.concatenate(edge), (P, POOLG * 16))], 1).astype(np.float32)
    return cst, rel, admit


def constants_second():
    r = np.arange(P)
    half, pos = r // C, np.where(r < C, r, P - 1 - r)
    same = half[:, None] == half[None, :]
    tri = same & (pos[:, None] <= pos[None, :])
    mats = [tri, np.roll(tri, C, 1), same & (pos[:, None] > pos[None, :]),
            np.broadcast_to(half[:, None] == 0, (P, P)), np.broadcast_to(half[:, None] == 1, (P, P)), same]
    pr = pos[:, None]
    pc = np.where(half[:, None] == 0, np.arange(C)[None, :], C - 1 - np.arange(C)[None, :])
    cols = [pr <= pc, np.where(pr > pc, -1, 1), pr > pc, pr <= pc, pr == pc]
    cols += [(pr // (2 * m) == pc // (2 * m)) & (pr // m % 2 == 1) & (pc // m % 2 == 0) for m in (1, 2, 4, 8, 16, 32)]
    cols += [(pr <= pc) | (half[:, None] != d) for d in range(2)]
    return np.concatenate(mats + cols, 1).astype(np.float32)


def tiles(w, cols):
    w = w[:, cols]
    return w.reshape(w.shape[0] // P, P, -1).transpose(1, 0, 2).reshape(P, -1)


def blocks(w, start, count):
    return [tiles(w, slice(start + P * j, start + P * (j + 1))) for j in range(count)]


def channels(v):
    return v.reshape(-1, P).T


def pack_stream(i):
    out = []
    for l in range(LAYERS):
        out += blocks(i["w_mem_kv"][l], 0, 8)
    for l in range(LAYERS):
        w = i["w_in"][l]
        u, z, q, k, v, az, iq, ik, iw, mq, mz, g = np.cumsum([0, 512, 512, 512, 512, 512, 512, 512, 64, 8, 512, 512])
        for start in (iq, q, k, v, az, z, mz, u, mq):
            out += blocks(w, start, 4)
        out += blocks(w, g, 24)
        for b in range(3):
            for d in range(4):
                pair = [tiles(i["w_branch"][l, b], slice(P * c, P * (c + 1))) for c in (2 * d, 2 * d + 1)]
                out.append(np.concatenate(pair, 1))
        out += blocks(i["w_out"][l], 0, 8)
    w = i["w_in_2"][0]
    q, k, v, z, b, a, scb, scc, scx, ga, gb = np.cumsum([0, D, D, D, D, 16, 16, D, D, D, D])
    for start in (q, k, v):
        out += blocks(w, start, KT)
    for j in range(KT):
        for start in (scc, scx, scb, z):
            out += blocks(w, start + P * j, 1)
    for start in (ga, gb):
        out += blocks(w, start, KT)
    for n in ("w_branch_sc_2", "w_branch_dn_2", "w_out_2"):
        out += blocks(i[n][0], 0, KT)
    w = i["w_gate_up_2"][0]
    for j in range(FT):
        out += blocks(w, P * j, 1) + blocks(w, P * (FT + j), 1)
    for j in range(KT):
        col = tiles(i["w_down_2"][0], slice(P * j, P * (j + 1)))
        col = np.concatenate([col, np.zeros((P, 3 * BLK - FT * P), np.float32)], 1)
        out += [col[:, BLK * c:BLK * (c + 1)] for c in range(3)]
    out += [np.zeros((P, BLK), np.float32)] * AHEAD
    return np.stack(out)


def kernel(**inputs):
    import concourse.bacc as bacc
    from concourse.bass_utils import run_bass_kernel_spmd

    i = {n: np.asarray(v) for n, v in inputs.items()}
    cst, rel, admit = constants_first()
    w_in = i["w_in"]
    ik = w_in[:, :, 3584:3656]
    wik = np.concatenate([ik[:, :, 0:64], ik[:, :, 0:64], ik[:, :, 64:72]], 2)
    gains = [channels(i["norm_g"].reshape(-1)), channels(i["mem_norm_g"].reshape(-1)), channels(i["pool_scale"].reshape(-1)),
             channels(i["final_g"]), channels(i["norm1_w_2"][0]), channels(i["norm2_w_2"][0]), channels(i["final_norm_w_2"]),
             channels(i["dn_norm_w_2"][0]),
             i["dn_conv_w_2"][0].reshape(5, 24, P).transpose(2, 1, 0).reshape(P, -1),
             i["sc_conv_w_2"][0].reshape(3, 8, P).transpose(2, 1, 0).reshape(P, -1)]
    ba = i["w_in_2"][0][:, 4 * D:4 * D + 4 * DN].reshape(D, 2, 2, DN)
    wba = ba.transpose(0, 2, 1, 3)
    tokens = np.concatenate([i["meta_tokens_2"], i["x"][0]], 0)
    arrays = {
        "stream": pack_stream(i),
        "xT": tokens.T.reshape(KT, P, T).transpose(1, 0, 2),
        "memT": i["mem"][0].T.reshape(KT, P, S).transpose(1, 0, 2),
        "gains": np.concatenate(gains, 1),
        "cst": cst, "rel_cst": rel, "admit": admit,
        "rel_bias": i["rel_bias"],
        "wik": wik.reshape(LAYERS, KT, P, 136).transpose(0, 2, 1, 3),
        "pool_w": i["pool_w"].transpose(0, 2, 1, 3),
        "cst2": constants_second(),
        "wba": wba.reshape(KT, P, 4 * DN).transpose(1, 0, 2),
        "adt": np.repeat(np.concatenate([i["A_log_2"][0], i["dt_bias_2"][0]], 1), C, 0),
    }
    nc = bacc.Bacc("TRN2", target_bir_lowering=False, num_devices=1)
    arrays = {f"{n}_dram": np.ascontiguousarray(v) for n, v in arrays.items()}
    a = {n[:-5]: nc.dram_tensor(n, v.shape, F32, kind="ExternalInput").ap() for n, v in arrays.items()}
    a["rel_scratch"] = nc.dram_tensor("rel_scratch", (HEADS, 512), F32, kind="Internal").ap()
    a["x_spill"] = nc.dram_tensor("x_spill", (P, KT, T), F32, kind="Internal").ap()
    a["groups"] = (arrays["stream_dram"].shape[0] - AHEAD) // SLOTS
    out = nc.dram_tensor("out", (P, KT, S), F32, kind="ExternalOutput").ap()
    build(nc, a, out)
    r = run_bass_kernel_spmd(nc, [arrays], core_ids=[0])
    return np.ascontiguousarray(r.results[0]["out"].transpose(2, 1, 0).reshape(1, S, D))
```
